# Optimizing a Trainium2 kernel written in Bass

```python
import math
import jax, jax.numpy as jnp
from jax import lax
import numpy as np

D_MODEL = 1024
BATCH = 1
SEQ = 512
DEPTH = 2

CHUNK = 64
Q_BLOCK = 128
CONV_K = 4
EPS = 1e-6

GLA_HEADS = 4
GLA_DK = 64
GLA_DV = 128
GLA_QK = GLA_HEADS * GLA_DK
GLA_WIDTH = GLA_HEADS * GLA_DV
GLA_GATE_RANK = 16
GLA_GATE_TEMP = 16.0

DIFF_HEADS = 4
DIFF_DH = 64
DIFF_DV = 2 * DIFF_DH
DIFF_QK = DIFF_HEADS * 2 * DIFF_DH
DIFF_WIDTH = DIFF_HEADS * DIFF_DV

MIX_WIDTH = GLA_WIDTH + DIFF_WIDTH
GLA_CONV_WIDTH = 2 * GLA_QK + GLA_WIDTH
SPLIT_SIZES = (GLA_QK, GLA_QK, GLA_WIDTH, GLA_GATE_RANK, GLA_WIDTH,
               DIFF_QK, DIFF_QK, DIFF_WIDTH, DIFF_WIDTH)
IN_WIDTH = 2 * GLA_QK + 2 * GLA_WIDTH + GLA_GATE_RANK + 2 * DIFF_QK + 2 * DIFF_WIDTH


def rms_norm(x, g):
    xf = x.astype(jnp.float32)
    y = xf * lax.rsqrt(jnp.mean(xf * xf, axis=-1, keepdims=True) + EPS)
    return (y * g.astype(jnp.float32)).astype(x.dtype)

def split_columns(p):
    idx = np.cumsum(np.array(SPLIT_SIZES))[:-1].tolist()
    return jnp.split(p, idx, axis=-1)

def causal_depthwise_conv(u, w):
    S = u.shape[1]
    up = jnp.pad(u, ((0, 0), (CONV_K - 1, 0), (0, 0)))
    out = up[:, 0:S] * w[0]
    for j in range(1, CONV_K):
        out = out + up[:, j:j + S] * w[j]
    return out

def gla_branch(q, k, v, glr, z, w_gk, b_gk, g_out):
    B, S, _ = q.shape
    nc = S // CHUNK
    f32 = jnp.float32
    q = q.astype(f32).reshape(B, nc, CHUNK, GLA_HEADS, GLA_DK) * (GLA_DK ** -0.5)
    k = k.astype(f32).reshape(B, nc, CHUNK, GLA_HEADS, GLA_DK)
    v = v.astype(f32).reshape(B, nc, CHUNK, GLA_HEADS, GLA_DV)
    log_a = jax.nn.log_sigmoid((glr @ w_gk + b_gk).astype(f32)) / GLA_GATE_TEMP
    log_a = log_a.reshape(B, nc, CHUNK, GLA_HEADS, GLA_DK)
    b = jnp.cumsum(log_a, axis=2)
    b_end = b[:, :, -1]
    k_dec = k * jnp.exp(b_end[:, :, None] - b)
    u = jnp.einsum('bnchk,bnchv->nbhkv', k_dec, v)
    a = jnp.exp(b_end).transpose(1, 0, 2, 3)

    def step(state, inp):
        a_c, u_c = inp
        state = a_c[..., None] * state + u_c
        return state, state

    s0 = jnp.zeros((B, GLA_HEADS, GLA_DK, GLA_DV), f32)
    _, states = lax.scan(step, s0, (a, u))
    o = jnp.einsum('bnchk,nbhkv->bnchv', q, states)
    o = rms_norm(o, g_out).reshape(B, S, GLA_WIDTH)
    return o * jax.nn.silu(z.astype(f32))

def diff_branch(q, k, v, z, qn_g, kn_g, lam, lam_init, g_out):
    B, S, _ = q.shape
    f32 = jnp.float32
    q = rms_norm(q.reshape(B, S, DIFF_HEADS, 2, DIFF_DH), qn_g) * (DIFF_DH ** -0.5)
    k = rms_norm(k.reshape(B, S, DIFF_HEADS, 2, DIFF_DH), kn_g)
    v = v.astype(f32).reshape(B, S, DIFF_HEADS, DIFF_DV)
    key_chunk = jnp.arange(S) // CHUNK
    nb = S // Q_BLOCK
    qb = q.reshape(B, nb, Q_BLOCK, DIFF_HEADS, 2, DIFF_DH).transpose(1, 0, 2, 3, 4, 5)
    q_chunk = key_chunk.reshape(nb, Q_BLOCK)

    def block(args):
        qi, qc = args
        s = jnp.einsum('bqhmd,bkhmd->bhmqk', qi, k).astype(f32)
        mask = key_chunk[None, :] <= qc[:, None]
        s = jnp.where(mask, s, -jnp.inf)
        p = jax.nn.softmax(s, axis=-1)
        attn = p[:, :, 0] - lam * p[:, :, 1]
        return jnp.einsum('bhqk,bkhe->bqhe', attn, v)

    o = lax.map(block, (qb, q_chunk))
    o = o.transpose(1, 0, 2, 3, 4).reshape(B, S, DIFF_HEADS, DIFF_DV)
    o = rms_norm(o, g_out) * (1.0 - lam_init)
    return o.reshape(B, S, DIFF_WIDTH) * jax.nn.silu(z.astype(f32))

def first_inputs(seed: int = 0) -> dict:
    key = jax.random.key(seed)
    ks = jax.random.split(key, 18)
    f32 = jnp.float32
    L, D = DEPTH, D_MODEL
    n = lambda k, s, sc: (jax.random.normal(k, s, f32) * sc)
    return {
        "x": n(ks[0], (BATCH, SEQ, D), 1.0),
        "c": n(ks[1], (BATCH, D), 1.0),
        "w_ada": n(ks[2], (L, D, 3 * D), 0.5 * D ** -0.5),
        "b_ada": n(ks[3], (L, 3 * D), 0.02),
        "norm_g": 1.0 + n(ks[4], (L, D), 0.02),
        "w_in": n(ks[5], (L, D, IN_WIDTH), D ** -0.5),
        "conv_w": n(ks[6], (L, CONV_K, GLA_CONV_WIDTH), CONV_K ** -0.5),
        "w_gk": n(ks[7], (L, GLA_GATE_RANK, GLA_QK), GLA_GATE_RANK ** -0.5),
        "b_gk": n(ks[8], (L, GLA_QK), 0.1),
        "gla_norm_g": 1.0 + n(ks[9], (L, GLA_DV), 0.02),
        "qn_g": 1.0 + n(ks[10], (L, DIFF_DH), 0.02),
        "kn_g": 1.0 + n(ks[11], (L, DIFF_DH), 0.02),
        "lam_q1": n(ks[12], (L, DIFF_DH), 0.1),
        "lam_k1": n(ks[13], (L, DIFF_DH), 0.1),
        "lam_q2": n(ks[14], (L, DIFF_DH), 0.1),
        "lam_k2": n(ks[15], (L, DIFF_DH), 0.1),
        "diff_norm_g": 1.0 + n(ks[16], (L, DIFF_DV), 0.02),
        "w_out": n(ks[17], (L, MIX_WIDTH, D), MIX_WIDTH ** -0.5),
    }

def first_block(x, c, w_ada, b_ada, norm_g, w_in, conv_w, w_gk, b_gk, gla_norm_g,
              qn_g, kn_g, lam_q1, lam_k1, lam_q2, lam_k2, diff_norm_g, w_out):
    f32 = jnp.float32
    c_act = jax.nn.silu(c)
    for l in range(DEPTH):
        mod = c_act @ w_ada[l] + b_ada[l]
        shift, scale, gate = jnp.split(mod, 3, axis=-1)
        h = rms_norm(x, norm_g[l]) * (1.0 + scale[:, None]) + shift[:, None]
        proj = h @ w_in[l]
        gq, gk, gv, glr, gz, dq, dk, dv, dz = split_columns(proj)
        gqkv = jax.nn.silu(causal_depthwise_conv(jnp.concatenate([gq, gk, gv], axis=-1), conv_w[l]))
        gq, gk, gv = jnp.split(gqkv, [GLA_QK, 2 * GLA_QK], axis=-1)
        o_gla = gla_branch(gq, gk, gv, glr, gz, w_gk[l], b_gk[l], gla_norm_g[l])
        lam_init = 0.8 - 0.6 * math.exp(-0.3 * l)
        lam = (jnp.exp(jnp.sum(lam_q1[l].astype(f32) * lam_k1[l].astype(f32)))
               - jnp.exp(jnp.sum(lam_q2[l].astype(f32) * lam_k2[l].astype(f32))) + lam_init)
        o_diff = diff_branch(dq, dk, dv, dz, qn_g[l], kn_g[l], lam, lam_init, diff_norm_g[l])
        y = jnp.concatenate([o_gla, o_diff], axis=-1).astype(x.dtype) @ w_out[l]
        x = x + gate[:, None] * y
    return x


DEPTH_2 = 1

CHUNK_2 = 128
A_WIDTH = D_MODEL
A_HEADS = 8
A_HEAD_DIM = A_WIDTH // A_HEADS
B_WIDTH = D_MODEL
B_GROUPS = 16
B_GROUP_DIM = B_WIDTH // B_GROUPS
CONV_WIDTH = 3
D_FF = ((8 * D_MODEL // 3 + 127) // 128) * 128
N_IN = 2 * A_WIDTH + 3 * B_WIDTH + 2 * D_MODEL


def rmsnorm(x, g):
    x32 = x.astype(jnp.float32)
    y = x32 * lax.rsqrt(jnp.mean(x32 * x32, axis=-1, keepdims=True) + EPS)
    return y.astype(x.dtype) * g

def swiglu(h, w_in, w_out):
    gate, up = jnp.split(h @ w_in, 2, axis=-1)
    return (jax.nn.silu(gate) * up) @ w_out

def spatial_gating(u, v, norm_g, w_s, b_s):
    bsz, s, _ = v.shape
    v = rmsnorm(v, norm_g)
    v = v.reshape(bsz, s // CHUNK_2, CHUNK_2, A_HEADS, A_HEAD_DIM)
    v = jnp.einsum('hqp,bcphd->bcqhd', w_s, v) + b_s.T[None, None, :, :, None]
    return u * v.reshape(bsz, s, A_WIDTH)

def short_conv(t, w):
    s = t.shape[1]
    pad = CONV_WIDTH // 2
    tp = jnp.pad(t, ((0, 0), (pad, CONV_WIDTH - 1 - pad), (0, 0)))
    out = w[0] * tp[:, 0:s]
    for k in range(1, CONV_WIDTH):
        out = out + w[k] * tp[:, k:k + s]
    return out

def hybrid_mixer(h, w_in, sgu_norm, sgu_w, sgu_b, conv_w, w_proj_a, w_proj_b, w_out):
    z = h @ w_in
    za, zb, zg = jnp.split(z, [2 * A_WIDTH, 2 * A_WIDTH + 3 * B_WIDTH], axis=-1)
    u, v = jnp.split(jax.nn.gelu(za), 2, axis=-1)
    y_a = spatial_gating(u, v, sgu_norm, sgu_w, sgu_b) @ w_proj_a
    gate_b, gate_c, xb = jnp.split(zb, 3, axis=-1)
    y_b = (gate_b * short_conv(gate_c * xb, conv_w)) @ w_proj_b
    g_a, g_b = jnp.split(zg, 2, axis=-1)
    merged = jax.nn.sigmoid(g_a) * y_a + jax.nn.sigmoid(g_b) * y_b
    return merged @ w_out

def second_inputs(seed: int = 0) -> dict:
    key = jax.random.key(seed)
    ks = jax.random.split(key, 20)
    f32 = jnp.float32

    def nrm(k, shape, scale):
        return jax.random.normal(k, shape, f32) * scale

    def gain(k, shape):
        return 1.0 + 0.05 * jax.random.normal(k, shape, f32)

    return {
        "x": nrm(ks[0], (BATCH, SEQ, D_MODEL), 1.0),
        "ffn1_norm": gain(ks[1], (DEPTH_2, D_MODEL)),
        "ffn1_w_in": nrm(ks[2], (DEPTH_2, D_MODEL, 2 * D_FF), D_MODEL ** -0.5),
        "ffn1_w_out": nrm(ks[3], (DEPTH_2, D_FF, D_MODEL), D_FF ** -0.5),
        "mix_norm": gain(ks[4], (DEPTH_2, D_MODEL)),
        "w_in": nrm(ks[5], (DEPTH_2, D_MODEL, N_IN), D_MODEL ** -0.5),
        "sgu_norm": gain(ks[6], (DEPTH_2, A_WIDTH)),
        "sgu_w": nrm(ks[7], (DEPTH_2, A_HEADS, CHUNK_2, CHUNK_2), CHUNK_2 ** -0.5),
        "sgu_b": gain(ks[8], (DEPTH_2, A_HEADS, CHUNK_2)),
        "conv_w": nrm(ks[9], (DEPTH_2, CONV_WIDTH, B_WIDTH), CONV_WIDTH ** -0.5),
        "w_proj_a": nrm(ks[10], (DEPTH_2, A_WIDTH, D_MODEL), A_WIDTH ** -0.5),
        "w_proj_b": nrm(ks[11], (DEPTH_2, B_WIDTH, D_MODEL), B_WIDTH ** -0.5),
        "w_out": nrm(ks[12], (DEPTH_2, D_MODEL, D_MODEL), D_MODEL ** -0.5),
        "ffn2_norm": gain(ks[13], (DEPTH_2, D_MODEL)),
        "ffn2_w_in": nrm(ks[14], (DEPTH_2, D_MODEL, 2 * D_FF), D_MODEL ** -0.5),
        "ffn2_w_out": nrm(ks[15], (DEPTH_2, D_FF, D_MODEL), D_FF ** -0.5),
        "final_norm": gain(ks[16], (D_MODEL,)),
    }

def second_block(x, ffn1_norm, ffn1_w_in, ffn1_w_out, mix_norm, w_in, sgu_norm, sgu_w,
              sgu_b, conv_w, w_proj_a, w_proj_b, w_out, ffn2_norm, ffn2_w_in,
              ffn2_w_out, final_norm):
    for l in range(DEPTH_2):
        x = x + 0.5 * swiglu(rmsnorm(x, ffn1_norm[l]), ffn1_w_in[l], ffn1_w_out[l])
        x = x + hybrid_mixer(rmsnorm(x, mix_norm[l]), w_in[l], sgu_norm[l], sgu_w[l],
                             sgu_b[l], conv_w[l], w_proj_a[l], w_proj_b[l], w_out[l])
        x = x + 0.5 * swiglu(rmsnorm(x, ffn2_norm[l]), ffn2_w_in[l], ffn2_w_out[l])
    return rmsnorm(x, final_norm)


def setup_inputs(seed=0):
    out = dict(first_inputs(seed))
    for name, value in second_inputs(seed + 1).items():
        if name != "x":
            out[name + "_2"] = value
    return out


def reference(
    x, c, w_ada, b_ada, norm_g, w_in, conv_w, w_gk, b_gk, gla_norm_g, qn_g, kn_g, lam_q1,
    lam_k1, lam_q2, lam_k2, diff_norm_g, w_out, ffn1_norm_2, ffn1_w_in_2, ffn1_w_out_2,
    mix_norm_2, w_in_2, sgu_norm_2, sgu_w_2, sgu_b_2, conv_w_2, w_proj_a_2, w_proj_b_2, w_out_2,
    ffn2_norm_2, ffn2_w_in_2, ffn2_w_out_2, final_norm_2,
):
    x = first_block(
        x, c, w_ada, b_ada, norm_g, w_in, conv_w, w_gk, b_gk, gla_norm_g, qn_g, kn_g, lam_q1,
        lam_k1, lam_q2, lam_k2, diff_norm_g, w_out,
    )
    return second_block(
        x, ffn1_norm_2, ffn1_w_in_2, ffn1_w_out_2, mix_norm_2, w_in_2, sgu_norm_2, sgu_w_2,
        sgu_b_2, conv_w_2, w_proj_a_2, w_proj_b_2, w_out_2, ffn2_norm_2, ffn2_w_in_2,
        ffn2_w_out_2, final_norm_2,
    )


_drawn_inputs = setup_inputs


def setup_inputs(seed=0):
    import zlib

    import numpy as np

    out = dict(_drawn_inputs(seed))
    spreads = {}
    factors = {'norm_g': 7.128,
     'w_gk': 3.165,
     'b_gk': 8.0,
     'gla_norm_g': 8.0,
     'qn_g': 8.0,
     'kn_g': 8.0,
     'lam_q1': 5.909,
     'lam_k1': 4.574,
     'lam_q2': 4.798,
     'lam_k2': 6.183,
     'diff_norm_g': 8.0,
     'sgu_norm_2': 200.0,
     'sgu_b_2': 200.0,
     'ffn2_norm_2': 83.912,
     'ffn1_norm_2': 8.0,
     'ffn1_w_in_2': 2.867,
     'ffn1_w_out_2': 2.875,
     'mix_norm_2': 5.925}
    for name, (base, spread) in spreads.items():
        noise = np.random.default_rng([zlib.crc32(name.encode()), seed]).standard_normal(out[name].shape)
        drawn = base * np.exp(spread * noise) if base else spread * noise
        out[name] = __import__('jax').numpy.asarray(drawn.astype(out[name].dtype))
    for name, factor in factors.items():
        out[name] = (out[name] * factor).astype(out[name].dtype)
    return out
```

```python
import math
from contextlib import ExitStack

import numpy as np

import concourse.bass as bass
import concourse.mybir as mybir

F32 = mybir.dt.float32
F32R = mybir.dt.float32r
ALU = mybir.AluOpType
ACT = mybir.ActivationFunctionType
AX_X = mybir.AxisListType.X

P = 128
D = 1024
S = 512
KT = D // P
TB = S // P
EPS = 1e-6
LAYERS = 2
CHUNK = 64
NCH = S // CHUNK
HEADS = 4
DK = 64
RANK = 16
CONV_K = 4
GLA_QK = 256
WIDTH = 512
D_FF = 2816
FT = D_FF // P
FH = FT // 2
CW = 16 * P
FW = FH * P
NEG = -1.0e30

L_Q, L_K, L_V, L_CONV, L_Z, L_OUT = 2, 2, 2, 4, 4, 4
L_UNITS = L_Q + L_K + L_V + L_CONV + L_Z + L_OUT
M_V, M_U, M_CX, M_GB, M_MERGE, M_OUT = 4, 4, 8, 4, 16, 4
M_UNITS = M_V + M_U + M_CX + M_GB + M_MERGE + M_OUT
FFN_UNITS = FT + KT
FFN_CHUNKS = FT + 2 * KT
UNIT0 = {"layer0": 0, "layer1": L_UNITS, "ffn1": 2 * L_UNITS}
UNIT0["mixer"] = UNIT0["ffn1"] + FFN_UNITS
UNIT0["ffn2"] = UNIT0["mixer"] + M_UNITS
CHUNK0 = {"layer0": 0, "layer1": L_UNITS, "ffn1": 2 * L_UNITS}
CHUNK0["mixer"] = CHUNK0["ffn1"] + FFN_CHUNKS
CHUNK0["ffn2"] = CHUNK0["mixer"] + M_UNITS
STEPS = HEADS * TB


def lam_init(l):
    return 0.8 - 0.6 * math.exp(-0.3 * l)


def build(nc, ins, out):
    ctx = ExitStack()
    with ctx:
        def sem(name):
            return ctx.enter_context(nc.semaphore(name))

        base = nc.sbuf_base
        top = nc.sbuf_usable_end
        base = (base + 63) // 64 * 64
        cursor = [base]

        def at(name, shape, dt, offset):
            n = 4 * int(np.prod(shape[1:]))
            assert offset + n <= top, (name, offset + n, top)
            return nc.alloc_sbuf_tensor_at(name, shape, dt, offset=offset, align_bytes=4)

        def sb(name, shape, dt=F32):
            n = (4 * int(np.prod(shape[1:])) + 31) // 32 * 32
            t = at(name, shape, dt, cursor[0])
            cursor[0] += n
            return t

        ps = ctx.enter_context(nc.psum_tensor("ps", [P, 8, 512], F32))

        x = sb("x", [P, KT, S])
        xh = sb("xh", [P, KT, S], F32R)
        xl = sb("xl", [P, KT, S], F32R)
        raw = [sb(f"raw{u}", [P, CW]) for u in range(2)]
        wh = [sb(f"wh{u}", [P, CW], F32R) for u in range(2)]
        wl = [sb(f"wl{u}", [P, CW], F32R) for u in range(2)]
        ones = sb("ones", [P, P])
        ident = sb("ident", [P, P])
        later = sb("later", [P, P])
        inchunk = sb("inchunk", [P, 2])
        inhalf = sb("inhalf", [P, 2])
        eps = sb("eps", [P, 3])
        sumsq = sb("sumsq", [P, S])
        sq = sb("sq", [P, 2, S])
        tmp = sb("tmp", [P, 2, S])
        diag = sq[:, 1].rearrange("p (b c) -> p b c", b=TB)
        norm_sd = sb("norm_sd", [P, TB])
        norm_r = sb("norm_r", [P, TB])
        mod = sb("mod", [P, LAYERS, 24])
        b_ada = sb("b_ada", [P, LAYERS, 24])
        norm_g = sb("norm_g", [P, LAYERS, KT])
        gains = sb("gains", [P, 4, KT])
        c_col = sb("c_col", [P, KT])
        c_act = sb("c_act", [P, KT])
        conv_w = sb("conv_w", [P, LAYERS, KT, CONV_K])
        conv2_w = sb("conv2_w", [P, KT, 3])
        sgu_g = sb("sgu_g", [P, KT])
        qk_g = sb("qk_g", [P, LAYERS, 2])
        qkg = sb("qkg", [P, LAYERS])
        lam_in = sb("lam_in", [P, LAYERS, 4, DK])
        lam_p = sb("lam_p", [P, LAYERS, 2, DK])
        lam_s = sb("lam_s", [P, LAYERS, 2])
        lam_e = sb("lam_e", [P, LAYERS, 2])
        neglam = sb("neglam", [P, LAYERS])
        o_g = sb("o_g", [P, LAYERS, 2, P])
        wgk = sb("wgk", [RANK + 1, LAYERS, GLA_QK])
        glr = sb("glr", [32, S])
        wr_raw = sb("wr_raw", [P, LAYERS, KT, RANK])
        arena = cursor[0]

        def place(name, shape, dt=F32):
            n = (4 * int(np.prod(shape[1:])) + 31) // 32 * 32
            t = at(name, shape, dt, cursor[0])
            cursor[0] += n
            return t

        acc = place("ada_acc", [P, 3 * D])
        ada_w = [place(f"ada_w{i}", [P, 3 * D // 2]) for i in range(4)]

        cursor[0] = arena
        u_in = place("u_in", [P, KT, S + CONV_K - 1])
        at_conv = cursor[0]
        conv = place("conv", [P, KT, S])
        q = place("q", [P, HEADS, S])
        at_k = cursor[0]
        k_tok = place("k_tok", [P, TB, WIDTH])
        kf = place("kf", [P, HEADS, S])
        v = place("v", [P, TB, WIDTH])
        zg = place("zg", [P, TB, 2 * WIDTH])
        at_p = cursor[0]
        prob = place("prob", [P, 2, 2, S])
        attn_t = place("attn_t", [P, 2, S])
        o_diff = place("o_diff", [P, TB, WIDTH])
        ss_qk = place("ss_qk", [P, 2, TB, 8])
        r_qk = place("r_qk", [P, 2, TB, 8])
        nrq = place("nrq", [P, TB, 8])
        smax = place("smax", [P, 2, 2])
        nbias = place("nbias", [P, 2, 2])
        zs = place("zs", [P, 2, 2])
        rz = place("rz", [P, 2, 2])
        ss_o = place("ss_o", [P, TB, 8])
        sd_o = place("sd_o", [P, TB, 8])
        r_o = place("r_o", [P, TB, 8])
        aend = place("aend", [P, 2, NCH])
        k_sq = at("k_sq", [P, TB, WIDTH], F32, at_p)
        states = at("states", [P, NCH, 2, 256], F32, arena)
        log_a = at("log_a", [P, TB, 256], F32, at_k)
        decay = at("decay", [P, TB, 256], F32, at_k + 4096)
        gv = at("gv", [P, TB, WIDTH], F32, at_p)
        soft = at("soft", [P, TB, 256], F32, at_p + 8192)
        wr_h = at("wr_h", [P, KT, P], F32R, at_p + 4096)
        o_gla = at("o_gla", [P, TB, WIDTH], F32, at_conv + 4 * S * 4)
        o = (o_gla, o_diff)
        wr_l = at("wr_l", [P, KT, P], F32R, at_p)

        cursor[0] = arena
        fh = place("fh", [P, FT, S], F32R)
        fl = place("fl", [P, FT, S], F32R)
        gate = place("gate", [P, 2, S])

        cursor[0] = arena
        at_v2 = cursor[0]
        v2 = place("v2", [P, TB, D])
        u2 = place("u2", [P, KT, S])
        bh = at("bh", [P, KT, S], F32R, at_v2)
        bl = at("bl", [P, KT, S], F32R, at_v2 + KT * S * 4)
        ah = place("ah", [P, KT, S], F32R)
        al = place("al", [P, KT, S], F32R)
        at_m = cursor[0]
        cv = place("cv", [P, KT, S])
        mh = at("mh", [P, KT, S], F32R, at_m)
        at_ml = cursor[0]
        ml = place("ml", [P, KT, S], F32R)
        ws_t = at("ws_t", [P, KT, P], F32, at_ml)
        bs = at("bs", [P, KT, P], F32, at_ml + 4096)
        v2_sq = at("v2_sq", [P, D], F32, at_ml + 8192)
        ss_v = at("ss_v", [P, 3, TB], F32, at_ml + 12288)
        gc = place("gc", [P, 2, S])
        tpad = place("tpad", [P, 2, S + 2])

        y = at("y", [P, KT, S], F32, arena)

        raw_landed = [sem(f"raw_landed{u}") for u in range(2)]
        w_high = sem("w_high")
        w_ready = sem("w_ready")
        half_used = sem("half_used")
        tile_done = sem("tile_done")
        banks_free = [sem(f"banks_free{u}") for u in range(2)]
        small_in = sem("small_in")
        x_in = sem("x_in")
        ada_landed = [sem(f"ada_landed{i}") for i in range(4)]
        ada_used = sem("ada_used")
        consts = sem("consts")
        dve_step = sem("dve_step")
        act_step = sem("act_step")
        pool_step = sem("pool_step")
        pool_saw = sem("pool_saw")
        c_ready = sem("c_ready")
        ada_sum = sem("ada_sum")
        ada_cols = sem("ada_cols")
        ada_read = sem("ada_read")
        lam_ready = sem("lam_ready")
        lam_exp = sem("lam_exp")
        x_ready = sem("x_ready")
        sq_ready = sem("sq_ready")
        sq_used = sem("sq_used")
        sumsq_ready = sem("sumsq_ready")
        norm_ss = sem("norm_ss")
        norm_root = sem("norm_root")
        diag_ready = sem("diag_ready")
        norm_bc = sem("norm_bc")
        tmp_ready = sem("tmp_ready")
        high_ready = sem("high_ready")
        low_ready = sem("low_ready")
        lr_w = sem("lr_w")
        glr_done = sem("glr_done")
        glr_copied = sem("glr_copied")
        qk_copied = sem("qk_copied")
        conv_in = sem("conv_in")
        conv_done = sem("conv_done")
        conv_act = sem("conv_act")
        z_in = sem("z_in")
        q_sq = sem("q_sq")
        q_ss = sem("q_ss")
        qk_var = sem("qk_var")
        qk_root = sem("qk_root")
        k_normed = sem("k_normed")
        k_turned = sem("k_turned")
        kf_ready = sem("kf_ready")
        scores = sem("scores")
        bias_ready = sem("bias_ready")
        exp_done = sem("exp_done")
        attn_ready = sem("attn_ready")
        attn_turned = sem("attn_turned")
        at_copied = sem("at_copied")
        pv_done = sem("pv_done")
        o_copied = sem("o_copied")
        gate_mm = sem("gate_mm")
        gate_min = sem("gate_min")
        gate_soft = sem("gate_soft")
        loga_ready = sem("loga_ready")
        decay_mm = sem("decay_mm")
        decay_exp = sem("decay_exp")
        gk_turned = sem("gk_turned")
        gk_ready = sem("gk_ready")
        gv_turned = sem("gv_turned")
        gv_ready = sem("gv_ready")
        outer_done = sem("outer_done")
        state_ready = sem("state_ready")
        gla_o = sem("gla_o")
        gla_copied = sem("gla_copied")
        o_var = sem("o_var")
        o_root = sem("o_root")
        o_normed = sem("o_normed")
        o_turned = sem("o_turned")
        mix_high = sem("mix_high")
        mix_low = sem("mix_low")
        ff_gate = sem("ff_gate")
        m_v = sem("m_v")
        m_u = sem("m_u")
        m_root_in = sem("m_root_in")
        m_root = sem("m_root")
        m_vn = sem("m_vn")
        m_gc = sem("m_gc")
        m_prod = sem("m_prod")
        sgu_in = sem("sgu_in")
        sgu_mm = sem("sgu_mm")
        sgu_free = sem("sgu_free")
        m_sig = sem("m_sig")
        m_sig_used = sem("m_sig_used")
        y_ready = sem("y_ready")
        y_out = sem("y_out")

        SPLIT0 = {}
        n = 0
        for name, count in (("norm0", 8), ("norm1", 8), ("norm2", 8), ("ffn1", FT), ("norm3", 8),
                            ("sgu", 8), ("gb", 8), ("merge", 8), ("norm4", 8), ("ffn2", FT)):
            SPLIT0[name] = n
            n += count

        block = ctx.enter_context(nc.Block())

        segments = []
        for l in range(LAYERS):
            segments += [(ins[f"layer{l}_stream"], L_UNITS, CW, UNIT0[f"layer{l}"], 0)]
        segments += [(ins["ffn1_in_stream"], FT, CW, UNIT0["ffn1"], 0),
                     (ins["ffn1_out_stream"], 2 * KT, FW, UNIT0["ffn1"] + FT, 0),
                     (ins["mixer_stream"], M_UNITS, CW, UNIT0["mixer"], KT),
                     (ins["ffn2_in_stream"], FT, CW, UNIT0["ffn2"], KT),
                     (ins["ffn2_out_stream"], 2 * KT, FW, UNIT0["ffn2"] + FT, KT)]

        small = [
            (c_col, ins["c_col"]), (b_ada, ins["b_ada"]), (norm_g, ins["norm_g"]), (gains, ins["gains"]),
            (conv_w, ins["conv_w"]), (conv2_w, ins["conv2_w"]), (sgu_g, ins["sgu_g"]), (qk_g, ins["qk_g"]),
            (wr_raw, ins["w_lr"]),
        ]
        N_SMALL = 16 * (len(small) + 3 + LAYERS)
        ADA_N = LAYERS * KT * 2

        @block.sync
        def _(sp):
            sp.dma_start(x[:], ins["x_t"]).then_inc(x_in, 16)

            def load_pair(dram, size, i, chunk):
                for u in range(2):
                    if not (isinstance(i, int) and chunk == 0):
                        sp.wait_ge(w_ready, i * 2 + (chunk + u - 1))
                    sp.dma_start(raw[u][:, 0:size], dram[i * 2 + u]).then_inc(raw_landed[u], 16)

            chunk = 0
            for dram, count, size, _, _ in segments:
                first = 0
                if chunk == 0:
                    load_pair(dram, size, 0, 0)
                    first = 1
                with sp.Fori(first, count // 2) as i:
                    load_pair(dram, size, i, chunk)
                chunk += count
            for k in range(KT):
                sp.wait_ge(y_ready, k + 1)
                sp.dma_start(out[:, k], y[:, k]).then_inc(y_out, 16)
            sp.wait_ge(y_out, 16 * KT)

        @block.gpsimd
        def _(pool):
            nc.gpsimd.memset(ones[:], 1.0).then_inc(pool_step, 1)
            nc.gpsimd.memset(ident[:], 0.0).then_inc(pool_step, 1)
            nc.gpsimd.memset(later[:], 1.0 / 16).then_inc(pool_step, 1)
            nc.gpsimd.memset(glr[:], 1.0).then_inc(pool_step, 1)
            pool.wait_ge(pool_step, 4)
            nc.gpsimd.affine_select(out=ident[:], in_=ident[:], compare_op=ALU.not_equal, fill=1.0, base=0,
                                    pattern=[[-1, P]], channel_multiplier=1).then_inc(pool_step, 1)
            nc.gpsimd.affine_select(out=later[:], in_=later[:], compare_op=ALU.is_gt, fill=0.0, base=0,
                                    pattern=[[-1, P]], channel_multiplier=1).then_inc(pool_step, 1)
            def split(size, i, chunk, unit, u):
                pool.wait_ge(raw_landed[u], i * 16 + (8 * chunk + 16))
                if size == CW:
                    if not (isinstance(i, int) and chunk == 0):
                        pool.wait_ge(tile_done, i * 4 + (2 * unit + 2 * u - 2))
                elif u == 0:
                    pool.wait_ge(half_used, i + (1 if unit < UNIT0["mixer"] else KT + 1))
                else:
                    pool.wait_ge(tile_done, i * 2 + 2 * unit)
                pool.sem_inc(pool_saw, 1)
                nc.gpsimd.tensor_copy(wh[u][:, 0:size], raw[u][:, 0:size]).then_inc(w_high, 1)
                pool.wait_ge(w_high, i * 2 + (chunk + u + 1))
                nc.gpsimd.tensor_tensor(wl[u][:, 0:size], raw[u][:, 0:size], wh[u][:, 0:size].bitcast(F32),
                                        ALU.subtract).then_inc(w_ready, 1)

            chunk = 0
            for dram, count, size, unit, halves in segments:
                first = 0
                if chunk == 0:
                    split(size, 0, 0, 0, 0)
                    split(size, 0, 0, 0, 1)
                    first = 1
                else:
                    pool.wait_ge(tile_done, 2 * unit - 2)
                    if halves:
                        pool.wait_ge(half_used, halves + 1)
                with pool.Fori(first, count // 2) as i:
                    for u in range(2):
                        split(size, i, chunk, unit, u)
                chunk += count

        N_CONST = 10

        @block.scalar
        def _(act):
            for dst, src in small:
                act.dma_start(dst[:], src).then_inc(small_in, 16)
            act.dma_start(lam_in[:], ins["lam"].to_broadcast([P, LAYERS * 4 * DK])
                          .rearrange("p (l a d) -> p l a d", l=LAYERS, a=4)).then_inc(small_in, 16)
            act.dma_start(o_g[:], ins["o_g"].to_broadcast([P, LAYERS * 2 * P])
                          .rearrange("p (l a d) -> p l a d", l=LAYERS, a=2)).then_inc(small_in, 16)
            act.dma_start(wgk[0:RANK], ins["w_gk"]).then_inc(small_in, 16)
            for l in range(LAYERS):
                act.dma_start(wgk[RANK:RANK + 1, l], ins["b_gk"][l:l + 1]).then_inc(small_in, 16)
            chain = [0]

            def link(ins_):
                chain[0] += 1
                ins_.then_inc(act_step, 1)
                act.wait_ge(act_step, chain[0])

            def copied(unit):
                for u in range(2):
                    act.wait_ge(banks_free[u], unit + 4)

            def ada_load(n):
                l, k, half = n // (2 * KT), n // 2 % KT, n % 2
                if n >= 4:
                    act.wait_ge(ada_used, n - 3)
                act.dma_start(ada_w[n % 4][:], ins["w_ada"][l, k, :, half * 1536:half * 1536 + 1536]
                              ).then_inc(ada_landed[n % 4], 16)

            for n in range(4):
                ada_load(n)
            act.wait_ge(small_in, N_SMALL)
            nc.scalar.activation(c_act[:], c_col[:], ACT.Silu).then_inc(c_ready, 1)
            for n in range(4, ADA_N):
                ada_load(n)
            act.wait_ge(lam_ready, 1)
            nc.scalar.activation(lam_e[:], lam_s[:], ACT.Exp).then_inc(lam_exp, 1)

            def squares(n, ms=range(KT)):
                for m in ms:
                    at_ = n * KT + m
                    if n == 0:
                        act.wait_ge(x_in, 16)
                    else:
                        act.wait_ge(x_ready, at_ - KT + 1)
                    if at_ >= 2:
                        act.wait_ge(sq_used, at_ - 1)
                    nc.scalar.activation(sq[:, m % 2], x[:, m], ACT.Square).then_inc(sq_ready, 1)

            def norm(n, splits=True):
                act.wait_ge(norm_ss, n + 1)
                nc.scalar.activation(norm_sd[:], ps[:, 6, 0:TB], ACT.Sqrt, bias=eps[:, 0:1],
                                     scale=1.0 / D).then_inc(norm_root, 1)
                if splits:
                    for k in range(KT):
                        high(f"norm{n}", k, xh[:, k])

            def high(name, k, dst):
                at_ = SPLIT0[name] + k
                act.wait_ge(tmp_ready, at_ + 1)
                nc.scalar.activation(dst, tmp[:, k % 2], ACT.Copy).then_inc(high_ready, 1)

            act.wait_ge(consts, N_CONST)
            for l in range(LAYERS):
                name = f"layer{l}"
                unit = UNIT0[name]
                if l == 0:
                    squares(0)
                norm(l)

                for u in range(2):
                    for t in range(2):
                        act.wait_ge(tile_done, 2 * unit + 2 * u + t + 1)
                        nc.scalar.activation(q[:, 2 * u + t], ps[:, 2 * u + t], ACT.Copy
                                             ).then_inc(banks_free[u], 1)
                unit += L_Q
                for dst in (k_tok, v):
                    for u in range(2):
                        for t in range(2):
                            act.wait_ge(tile_done, 2 * unit + 2 * u + t + 1)
                            nc.scalar.activation(dst[:, 2 * t:2 * t + 2, 256 * u:256 * u + 256],
                                                 ps[:, 2 * u + t].rearrange("p (b c) -> p b c", b=2),
                                                 ACT.Copy).then_inc(banks_free[u], 1)
                    copied(unit)
                    act.sem_inc(qk_copied, 1)
                    unit += 2
                act.wait_ge(glr_done, l + 1)
                nc.scalar.activation(glr[0:RANK], ps[0:RANK, 4], ACT.Copy).then_inc(glr_copied, 1)
                act.wait_ge(qk_var, l + 1)
                nc.scalar.activation(r_qk[:], ss_qk[:], ACT.Sqrt, bias=eps[:, 0:1], scale=1.0 / DK
                                     ).then_inc(qk_root, 1)
                with act.Fori(0, L_CONV // 2) as i:
                    for u in range(2):
                        for t in range(2):
                            act.wait_ge(tile_done, i * 4 + (2 * unit + 2 * u + t + 1))
                            nc.scalar.activation(
                                u_in[:, bass.ds(i * 4 + (2 * u + t), 1), CONV_K - 1:], ps[:, 2 * u + t:2 * u + t + 1],
                                ACT.Copy).then_inc(banks_free[u], 1)
                            act.wait_ge(banks_free[u], i * 2 + (2 * (unit // 2) + t + 3))
                            act.sem_inc(conv_in, 1)
                unit += L_CONV
                for i in range(L_Z // 2):
                    for u in range(2):
                        for t in range(2):
                            act.wait_ge(tile_done, 2 * unit + 4 * i + 2 * u + t + 1)
                            nc.scalar.activation(
                                zg[:, 2 * t:2 * t + 2, 512 * i + 256 * u:512 * i + 256 * u + 256],
                                ps[:, 2 * u + t].rearrange("p (b c) -> p b c", b=2),
                                ACT.Silu).then_inc(banks_free[u], 1)
                copied(unit + L_Z - 2)
                act.sem_inc(z_in, 1)
                unit += L_Z
                for m in range(KT):
                    act.wait_ge(conv_done, l * KT + m + 1)
                    nc.scalar.activation(conv[:, m], conv[:, m], ACT.Silu).then_inc(conv_act, 1)

                for h in range(HEADS):
                    act.wait_ge(k_turned, l * HEADS + h + 1)
                    nc.scalar.activation(kf[:, h], ps[:, 4 + h], ACT.Copy).then_inc(kf_ready, 1)
                def exps(s):
                    qb, h = s // HEADS, s % HEADS
                    n = P * (qb + 1)
                    if s >= 2:
                        act.wait_ge(attn_turned, l * STEPS + s - 1)
                    act.wait_ge(bias_ready, l * STEPS + s + 1)
                    for m in range(2):
                        nc.scalar.activation(prob[:, s % 2, m, 0:n], ps[:, 4 + m, 0:n], ACT.Exp,
                                             bias=nbias[:, s % 2, m:m + 1],
                                             scale=r_qk[:, 1, qb, 2 * h + m:2 * h + m + 1],
                                             accum_out=zs[:, s % 2, m:m + 1]).then_inc(exp_done, 1)

                def copy_turned(s):
                    n = P * (s // HEADS + 1)
                    act.wait_ge(attn_turned, l * STEPS + s + 1)
                    if s >= 2:
                        act.wait_ge(pv_done, l * STEPS + s - 1)
                    nc.scalar.activation(attn_t[:, s % 2, 0:n], ps[:, 6, 0:n], ACT.Copy
                                         ).then_inc(at_copied, 1)

                def copy_o(s):
                    qb, h = s // HEADS, s % HEADS
                    act.wait_ge(pv_done, l * STEPS + s + 1)
                    nc.scalar.activation(o_diff[:, qb, h * P:h * P + P], ps[:, 7, 0:P],
                                         ACT.Copy).then_inc(o_copied, 1)

                for s in range(STEPS + 2):
                    if s < STEPS:
                        exps(s)
                    if 1 <= s <= STEPS:
                        copy_turned(s - 1)
                    if s >= 2:
                        copy_o(s - 2)

                act.wait_ge(gate_min, l + 1)
                link(nc.scalar.activation(soft[:], ps[:, 4:6].rearrange("p a (b c) -> p (a b) c", b=2),
                                          ACT.Abs))
                link(nc.scalar.activation(soft[:], soft[:], ACT.Exp, scale=-1.0))
                nc.scalar.activation(soft[:], soft[:], ACT.Ln, bias=eps[:, 2:3]).then_inc(gate_soft, 1)
                act.wait_ge(decay_mm, 2 * l + 1)
                nc.scalar.activation(decay[:], ps[:, 6:8].rearrange("p a (b c) -> p (a b) c", b=2),
                                     ACT.Exp).then_inc(decay_exp, 1)
                act.wait_ge(decay_mm, 2 * l + 2)
                nc.scalar.activation(aend[:], ps[:, 4, 0:16].rearrange("p (a c) -> p a c", a=2),
                                     ACT.Exp).then_inc(decay_exp, 1)
                for tb in range(TB):
                    act.wait_ge(gv_turned, l * TB + tb + 1)
                    nc.scalar.activation(gv[:, tb], ps[:, 4 + tb % 2], ACT.Copy).then_inc(gv_ready, 1)
                for tb in range(TB):
                    act.wait_ge(gla_o, l * TB + tb + 1)
                    nc.scalar.activation(o_gla[:, tb].rearrange("p (a b c) -> p a b c", a=2, b=2),
                                         ps[:, 6:8, 0:256].rearrange("p b (a c) -> p a b c", a=2),
                                         ACT.Copy).then_inc(gla_copied, 1)
                act.wait_ge(o_var, l + 1)
                nc.scalar.activation(sd_o[:, :, 0:4], ss_o[:, :, 0:4], ACT.Sqrt, bias=eps[:, 1:2],
                                     scale=1.0 / P).then_inc(o_root, 1)
                nc.scalar.activation(sd_o[:, :, 4:8], ss_o[:, :, 4:8], ACT.Sqrt, bias=eps[:, 0:1],
                                     scale=1.0 / P).then_inc(o_root, 1)
                for j in range(2 * TB):
                    g, tb = j // TB, j % TB
                    act.wait_ge(o_turned, l * 8 + j + 1)
                    nc.scalar.activation(xh[:, 4 * g:4 * g + 4, tb * P:tb * P + P],
                                         ps[:, 4 + j % 4].rearrange("p (h c) -> p h c", h=4),
                                         ACT.Copy).then_inc(mix_high, 1)
                squares(l + 1)

            def ffn(name, n):
                norm(n)
                unit = UNIT0[name]
                split = SPLIT0[name]
                with act.Fori(0, FT // 2) as i:
                    for u in range(2):
                        act.wait_ge(tile_done, i * 4 + (2 * unit + 2 * u + 1))
                        act.wait_ge(tmp_ready, i * 2 + (split + u - 1))
                        nc.scalar.activation(gate[:, u], ps[:, 2 * u], ACT.Silu).then_inc(ff_gate, 1)
                        act.wait_ge(tmp_ready, i * 2 + (split + u + 1))
                        nc.scalar.activation(fh[:, bass.ds(i * 2 + u, 1)], tmp[:, u:u + 1], ACT.Copy
                                             ).then_inc(high_ready, 1)
                squares(n + 1)

            ffn("ffn1", 2)

            norm(3)
            unit = UNIT0["mixer"]
            for j in range(M_V):
                for t in range(2):
                    act.wait_ge(tile_done, 2 * unit + 2 * j + t + 1)
                    nc.scalar.activation(v2[:, 2 * t:2 * t + 2, 256 * j:256 * j + 256],
                                         ps[:, 2 * (j % 2) + t].rearrange("p (b c) -> p b c", b=2),
                                         ACT.Gelu_apprx_tanh).then_inc(banks_free[j % 2], 1)
            copied(unit + 2)
            act.sem_inc(m_v, 1)
            act.dma_start(ws_t[:], ins["sgu_w_t"]).then_inc(sgu_in, 16)
            act.dma_start(bs[:].rearrange("p h q -> p (h q)"), ins["sgu_b"].to_broadcast([P, KT * P])
                          ).then_inc(sgu_in, 16)
            unit += M_V
            with act.Fori(0, M_U // 2) as i:
                for u in range(2):
                    for t in range(2):
                        act.wait_ge(tile_done, i * 4 + (2 * unit + 2 * u + t + 1))
                        nc.scalar.activation(u2[:, bass.ds(i * 4 + (2 * u + t), 1)],
                                             ps[:, 2 * u + t:2 * u + t + 1],
                                             ACT.Gelu_apprx_tanh).then_inc(banks_free[u], 1)
            copied(unit + 2)
            act.sem_inc(m_u, 1)
            unit += M_U
            act.wait_ge(m_root_in, 1)
            nc.scalar.activation(ss_v[:, 1], ss_v[:, 0], ACT.Sqrt, bias=eps[:, 0:1], scale=1.0 / D
                                 ).then_inc(m_root, 1)
            with act.Fori(0, M_CX // 2) as i:
                for u in range(2):
                    act.wait_ge(tile_done, i * 4 + (2 * unit + 2 * u + 1))
                    act.wait_ge(m_prod, i * 2 + (u + 1))
                    nc.scalar.activation(gc[:, u], ps[:, 2 * u], ACT.Copy).then_inc(m_gc, 1)
            unit += M_CX
            for h in range(KT):
                high("sgu", h, ah[:, h])
            for m in range(KT):
                high("gb", m, bh[:, m])
            unit += M_GB
            for j in range(KT):
                for t in range(2):
                    act.wait_ge(tile_done, 2 * unit + 4 * j + t + 1)
                    if j:
                        act.wait_ge(m_sig_used, 2 * j)
                    nc.scalar.activation(gc[:, t], ps[:, t], ACT.Sigmoid).then_inc(m_sig, 1)
                act.wait_ge(m_sig, 2 * j + 2)
                act.sem_inc(banks_free[0], 2)
                high("merge", j, mh[:, j])
            squares(4)
            ffn("ffn2", 4)
            norm(5, splits=False)

        @block.tensor
        def _(pe):
            def products(bank_ap, wt, xk, first, last):
                (w0, w1), (x0, x1) = wt, xk
                nc.tensor.matmul(bank_ap, w0, x0, start=first, stop=False)
                nc.tensor.matmul(bank_ap, w0, x1, start=False, stop=False)
                return nc.tensor.matmul(bank_ap, w1, x0, start=False, stop=last)

            def claim(i, unit, u):
                pe.wait_ge(banks_free[u], i * 2 + (unit + 2))

            def chunk_ready(i, chunk, u):
                pe.wait_ge(w_ready, i * 2 + (chunk + u + 1))

            def feature_unit(i, unit, chunk, u, moving):
                claim(i, unit, u)
                chunk_ready(i, chunk, u)
                for t in range(2):
                    mh_, ml_ = moving[t]
                    for k in range(KT):
                        cols = slice((t * KT + k) * P, (t * KT + k + 1) * P)
                        last = products(ps[:, 2 * u + t], (wh[u][:, cols], wl[u][:, cols]),
                                        (mh_[:, k], ml_[:, k]), k == 0, k == KT - 1)
                    last.then_inc(tile_done, 1)

            def token_unit(i, unit, chunk, u):
                claim(i, unit, u)
                chunk_ready(i, chunk, u)
                for tb in range(TB):
                    cols = slice(tb * P, tb * P + P)
                    dst = ps[:, 2 * u + tb // 2, (tb % 2) * 256:(tb % 2) * 256 + 256]
                    for k in range(KT):
                        w = slice(k * 256, k * 256 + 256)
                        nc.tensor.matmul(dst, xh[:, k, cols], wh[u][:, w], start=(k == 0), stop=False)
                        nc.tensor.matmul(dst, xl[:, k, cols], wh[u][:, w], start=False, stop=False)
                        last = nc.tensor.matmul(dst, xh[:, k, cols], wl[u][:, w], start=False,
                                                stop=(k == KT - 1))
                    if tb % 2:
                        last.then_inc(tile_done, 1)

            def units(count, unit, chunk, body):
                with pe.Fori(0, count // 2) as i:
                    for u in range(2):
                        body(i, unit, chunk, u)

            both_x = [(xh, xl), (xh, xl)]

            def norm(n):
                pe.wait_ge(sumsq_ready, n + 1)
                for tb in range(TB):
                    last = nc.tensor.matmul(ps[:, 6, tb:tb + 1], sumsq[:, tb * P:tb * P + P], ones[:, 0:1],
                                            start=True, stop=True)
                last.then_inc(norm_ss, 1)
                pe.wait_ge(diag_ready, n + 1)
                nc.tensor.matmul(ps[:, 7], ones[:], sq[:, 1], start=True,
                                 stop=True).then_inc(norm_bc, 1)

            pe.wait_ge(consts, N_CONST)
            pe.sem_inc(half_used, 1)
            for l in range(LAYERS):
                pe.wait_ge(ada_sum, l + 1)
                for m in range(24):
                    last = nc.tensor.matmul(ps[:, 4, m:m + 1], acc[:, m * P:m * P + P], ones[:, 0:1],
                                            start=True, stop=True)
                last.then_inc(ada_cols, 1)
            for l in range(LAYERS):
                name = f"layer{l}"
                unit, chunk = UNIT0[name], CHUNK0[name]
                norm(l)
                pe.wait_ge(low_ready, SPLIT0[f"norm{l}"] + KT)
                units(L_Q, unit, chunk, lambda i, a, b, u: feature_unit(i, a, b, u, both_x))
                unit += L_Q
                chunk += L_Q
                units(L_K + L_V, unit, chunk, token_unit)
                unit += L_K + L_V
                chunk += L_K + L_V
                pe.wait_ge(lr_w, l + 1)
                for k in range(KT):
                    last = products(ps[:, 4], (wr_h[:, k], wr_l[:, k]), (xh[:, k], xl[:, k]), k == 0,
                                    k == KT - 1)
                last.then_inc(glr_done, 1)
                for h in range(HEADS):
                    pe.wait_ge(q_sq, l * HEADS + h + 1)
                    for tb in range(TB):
                        last = nc.tensor.matmul(ps[:, 5, tb * 8 + 2 * h:tb * 8 + 2 * h + 2],
                                                sq[:, h % 2, tb * P:tb * P + P], inhalf[:],
                                                start=True, stop=True)
                    last.then_inc(q_ss, 1)
                units(L_CONV, unit, chunk, lambda i, a, b, u: feature_unit(i, a, b, u, both_x))
                unit += L_CONV
                chunk += L_CONV
                units(L_Z, unit, chunk, token_unit)
                unit += L_Z
                chunk += L_Z

                pe.wait_ge(k_normed, l + 1)
                for h in range(HEADS):
                    for tb in range(TB):
                        last = nc.tensor.transpose(ps[:, 4 + h, tb * P:tb * P + P],
                                                   k_tok[:, tb, h * P:h * P + P], ident[:])
                    last.then_inc(k_turned, 1)
                pe.wait_ge(kf_ready, (l + 1) * HEADS)

                def score(s):
                    qb, h = s // HEADS, s % HEADS
                    if s:
                        pe.wait_ge(exp_done, 2 * (l * STEPS + s))
                    for m in range(2):
                        rows = slice(64 * m, 64 * m + 64)
                        nc.tensor.matmul(ps[:, 4 + m, 0:P * (qb + 1)], q[rows, h, qb * P:qb * P + P],
                                         kf[rows, h, 0:P * (qb + 1)], start=True, stop=True
                                         ).then_inc(scores, 1)

                def turn(s):
                    pe.wait_ge(attn_ready, l * STEPS + s + 1)
                    if s:
                        pe.wait_ge(at_copied, l * STEPS + s)
                    for kb in range(s // HEADS + 1):
                        last = nc.tensor.transpose(ps[:, 6, kb * P:kb * P + P],
                                                   prob[:, s % 2, 0, kb * P:kb * P + P], ident[:])
                    last.then_inc(attn_turned, 1)

                def pv(s):
                    qb, h = s // HEADS, s % HEADS
                    pe.wait_ge(at_copied, l * STEPS + s + 1)
                    if s:
                        pe.wait_ge(o_copied, l * STEPS + s)
                    for kb in range(qb + 1):
                        last = nc.tensor.matmul(ps[:, 7, 0:P], attn_t[:, s % 2, kb * P:kb * P + P],
                                                v[:, kb, h * P:h * P + P], start=(kb == 0), stop=(kb == qb))
                    last.then_inc(pv_done, 1)

                for s in range(STEPS + 2):
                    if s < STEPS:
                        score(s)
                    if 1 <= s <= STEPS:
                        turn(s - 1)
                    if s >= 2:
                        pv(s - 2)

                pe.wait_ge(exp_done, 2 * (l + 1) * STEPS)
                for tb in range(TB):
                    last = nc.tensor.matmul(ps[:, 4 + tb // 2, (tb % 2) * 256:(tb % 2) * 256 + 256],
                                            glr[0:RANK + 1, tb * P:tb * P + P], wgk[:, l], start=True, stop=True)
                last.then_inc(gate_mm, 1)
                pe.wait_ge(loga_ready, l + 1)
                pe.wait_ge(o_copied, (l + 1) * STEPS)
                for tb in range(TB):
                    last = nc.tensor.matmul(ps[:, 6 + tb // 2, (tb % 2) * 256:(tb % 2) * 256 + 256],
                                            later[:], log_a[:, tb], start=True, stop=True)
                last.then_inc(decay_mm, 1)
                for tb in range(TB):
                    for p in range(2):
                        last = nc.tensor.matmul(ps[:, 4, p * NCH + 2 * tb:p * NCH + 2 * tb + 2],
                                                log_a[:, tb, p * P:p * P + P], inchunk[:], start=True,
                                                stop=True)
                last.then_inc(decay_mm, 1)
                pe.wait_ge(conv_act, (l + 1) * KT)
                pe.wait_ge(decay_exp, 2 * l + 2)
                for tb in range(TB):
                    for p in range(2):
                        c0 = (tb % 2) * 256 + p * P
                        last = nc.tensor.transpose(ps[:, 6 + tb // 2, c0:c0 + P],
                                                   conv[:, 2 + p, tb * P:tb * P + P], ident[:])
                last.then_inc(gk_turned, 1)
                for tb in range(TB):
                    if tb >= 2:
                        pe.wait_ge(gv_ready, l * TB + tb - 1)
                    for h in range(HEADS):
                        last = nc.tensor.transpose(ps[:, 4 + tb % 2, h * P:h * P + P],
                                                   conv[:, 4 + h, tb * P:tb * P + P], ident[:])
                    last.then_inc(gv_turned, 1)
                pe.wait_ge(gk_ready, l + 1)
                pe.wait_ge(gv_ready, (l + 1) * TB)

                def outer(c):
                    if c >= 2:
                        pe.wait_ge(state_ready, l * NCH + c - 1)
                    rows = slice(64 * (c % 2), 64 * (c % 2) + 64)
                    for p in range(2):
                        last = nc.tensor.matmul(ps[:, 4 + c % 2, p * 256:p * 256 + 256],
                                                decay[rows, c // 2, p * P:p * P + P],
                                                gv[rows, c // 2, p * 256:p * 256 + 256],
                                                start=True, stop=True)
                    last.then_inc(outer_done, 1)

                def read_out(tb):
                    pe.wait_ge(state_ready, l * NCH + 2 * tb + 2)
                    if tb:
                        pe.wait_ge(gla_copied, l * TB + tb)
                    for half in range(2):
                        c = 2 * tb + half
                        for h in range(HEADS):
                            rows = slice(64 * (h % 2), 64 * (h % 2) + 64)
                            last = nc.tensor.matmul(
                                ps[64 * half:64 * half + 64, 6 + h % 2, (h // 2) * P:(h // 2) * P + P],
                                conv[rows, h // 2, c * CHUNK:(c + 1) * CHUNK],
                                states[rows, c, h // 2, (h % 2) * P:(h % 2) * P + P],
                                start=True, stop=True)
                    last.then_inc(gla_o, 1)

                for c in range(NCH):
                    outer(c)
                    if c >= 3 and c % 2:
                        read_out(c // 2 - 1)
                read_out(TB - 1)

                pe.wait_ge(gla_copied, (l + 1) * TB)
                for j in range(2 * TB):
                    g, tb = j // TB, j % TB
                    pe.wait_ge(o_normed, l * 8 + j + 1)
                    if j >= 4:
                        pe.wait_ge(mix_low, l * 8 + j - 3)
                    for h in range(HEADS):
                        last = nc.tensor.transpose(ps[:, 4 + j % 4, h * P:h * P + P],
                                                   o[g][:, tb, h * P:h * P + P], ident[:])
                    last.then_inc(o_turned, 1)
                pe.wait_ge(mix_low, (l + 1) * 8)
                units(L_OUT, unit, chunk, lambda i, a, b, u: feature_unit(i, a, b, u, both_x))

            def ffn(name, n):
                norm(n)
                pe.wait_ge(low_ready, SPLIT0[f"norm{n}"] + KT)
                unit, chunk = UNIT0[name], CHUNK0[name]
                units(FT, unit, chunk, lambda i, a, b, u: feature_unit(i, a, b, u, both_x))
                unit += FT
                chunk += FT
                pe.wait_ge(low_ready, SPLIT0[name] + FT)
                with pe.Fori(0, KT // 2) as i:
                    for m in range(2):
                        claim(i, unit, m)
                        for half in range(2):
                            pe.wait_ge(w_ready, i * 4 + (chunk + 2 * m + half + 1))
                            for kk in range(FH):
                                k = half * FH + kk
                                cols = slice(kk * P, kk * P + P)
                                last = products(ps[:, 2 * m], (wh[half][:, cols], wl[half][:, cols]),
                                                (fh[:, k], fl[:, k]), k == 0, k == FT - 1)
                            if half == 0:
                                last.then_inc(half_used, 1)
                        last.then_inc(tile_done, 2)

            ffn("ffn1", 2)

            norm(3)
            pe.wait_ge(low_ready, SPLIT0["norm3"] + KT)
            unit, chunk = UNIT0["mixer"], CHUNK0["mixer"]
            units(M_V, unit, chunk, token_unit)
            unit += M_V
            chunk += M_V
            units(M_U + M_CX, unit, chunk, lambda i, a, b, u: feature_unit(i, a, b, u, both_x))
            unit += M_U + M_CX
            chunk += M_U + M_CX
            pe.wait_ge(m_vn, 1)
            pe.wait_ge(sgu_in, 32)
            for h in range(KT):
                if h >= 2:
                    pe.wait_ge(sgu_free, h - 1)
                for c in range(TB):
                    last = nc.tensor.matmul(ps[:, 4 + h % 2, c * P:c * P + P], v2[:, c, h * P:h * P + P],
                                            ws_t[:, h], start=True, stop=True)
                last.then_inc(sgu_mm, 1)
            units(M_GB, unit, chunk, lambda i, a, b, u: feature_unit(i, a, b, u, both_x))
            unit += M_GB
            chunk += M_GB
            pe.wait_ge(low_ready, SPLIT0["gb"] + KT)
            units(M_MERGE, unit, chunk,
                  lambda i, a, b, u: feature_unit(i, a, b, u, both_x if u == 0 else [(ah, al), (bh, bl)]))
            unit += M_MERGE
            chunk += M_MERGE
            pe.wait_ge(low_ready, SPLIT0["merge"] + KT)
            units(M_OUT, unit, chunk, lambda i, a, b, u: feature_unit(i, a, b, u, [(mh, ml), (mh, ml)]))
            ffn("ffn2", 4)
            norm(5)

        @block.vector
        def _(dve):
            chain = [0]

            def link(ins_):
                chain[0] = chain[0] + 1
                ins_.then_inc(dve_step, 1)
                dve.wait_ge(dve_step, chain[0])

            def low(name, k, dst, hi):
                at_ = SPLIT0[name] + k
                dve.wait_ge(high_ready, at_ + 1)
                nc.vector.tensor_tensor(dst, tmp[:, k % 2], hi.bitcast(F32), ALU.subtract).then_inc(low_ready, 1)

            def tmp_free(name, k):
                at_ = SPLIT0[name] + k
                if at_ >= 2:
                    dve.wait_ge(low_ready, at_ - 1)

            def add_square(n, m):
                at_ = n * KT + m
                dve.wait_ge(sq_ready, at_ + 1)
                if m == 0:
                    ins_ = nc.vector.tensor_copy(sumsq[:], sq[:, 0])
                else:
                    dve.wait_ge(sq_used, at_)
                    ins_ = nc.vector.tensor_tensor(sumsq[:], sumsq[:], sq[:, m % 2], ALU.add)
                ins_.then_inc(sq_used, 1)
                if m == KT - 1:
                    dve.wait_ge(sq_used, at_ + 1)
                    dve.sem_inc(sumsq_ready, 1)

            def norm(n, gain, shift=None):
                dve.wait_ge(norm_root, n + 1)
                link(nc.vector.reciprocal(norm_r[:], norm_sd[:]))
                nc.vector.tensor_tensor(diag, ident[:].unsqueeze(1).to_broadcast([P, TB, P]),
                                        norm_r[:].unsqueeze(2).to_broadcast([P, TB, P]), ALU.mult
                                        ).then_inc(diag_ready, 1)
                dve.wait_ge(norm_bc, n + 1)
                for k in range(KT):
                    name = f"norm{n}"
                    if n == 5:
                        nc.vector.scalar_tensor_tensor(out=y[:, k], in0=x[:, k], scalar=gain[:, k:k + 1],
                                                       in1=ps[:, 7], op0=ALU.mult, op1=ALU.mult
                                                       ).then_inc(y_ready, 1)
                        continue
                    tmp_free(name, k)
                    if shift is None:
                        nc.vector.scalar_tensor_tensor(out=tmp[:, k % 2], in0=x[:, k],
                                                       scalar=gain[:, k:k + 1], in1=ps[:, 7],
                                                       op0=ALU.mult, op1=ALU.mult).then_inc(tmp_ready, 1)
                    else:
                        link(nc.vector.tensor_tensor(tmp[:, k % 2], x[:, k], ps[:, 7], ALU.mult))
                        nc.vector.tensor_scalar(tmp[:, k % 2], tmp[:, k % 2], gain[:, k:k + 1],
                                                shift[:, k:k + 1], ALU.mult, ALU.add).then_inc(tmp_ready, 1)
                    if k:
                        low(name, k - 1, xl[:, k - 1], xh[:, k - 1])
                if n < 5:
                    low(f"norm{n}", KT - 1, xl[:, KT - 1], xh[:, KT - 1])

            def residual(n, unit, scale_of, whole_unit):
                for m in range(KT):
                    j, t = (m, 0) if whole_unit else (m // 2, m % 2)
                    u = j % 2
                    dve.wait_ge(tile_done, 2 * (unit + j) + (2 if whole_unit else t + 1))
                    nc.vector.scalar_tensor_tensor(out=x[:, m], in0=ps[:, 2 * u + t], scalar=scale_of(m),
                                                   in1=x[:, m], op0=ALU.mult, op1=ALU.add
                                                   ).then_inc(x_ready, 1)
                    dve.wait_ge(x_ready, (n - 1) * KT + m + 1)
                    dve.sem_inc(banks_free[u], 2 if whole_unit else 1)
                    if m:
                        add_square(n, m - 1)
                add_square(n, KT - 1)

            for u in range(2):
                dve.sem_inc(banks_free[u], 2)
            nc.vector.memset(inchunk[:], 0.0).then_inc(consts, 1)
            nc.vector.memset(inhalf[:], 0.0).then_inc(consts, 1)
            dve.wait_ge(consts, 2)
            for h in range(2):
                rows = slice(h * 64, h * 64 + 64)
                nc.vector.memset(inchunk[rows, h:h + 1], 1.0 / 16).then_inc(consts, 1)
                nc.vector.memset(inhalf[rows, h:h + 1], 1.0).then_inc(consts, 1)
            for i, value in enumerate((EPS, 64 * EPS, 1.0)):
                nc.vector.memset(eps[:, i:i + 1], value).then_inc(consts, 1)
            dve.wait_ge(pool_step, 6)
            nc.vector.memset(later[64:128, 0:64], 0.0).then_inc(consts, 1)
            dve.wait_ge(small_in, N_SMALL)
            nc.vector.tensor_tensor(qkg[:], qk_g[:, :, 0], qk_g[:, :, 1], ALU.mult).then_inc(dve_step, 1)
            nc.vector.tensor_tensor(lam_p[:], lam_in[:, :, 0:4:2], lam_in[:, :, 1:4:2], ALU.mult
                                    ).then_inc(dve_step, 1)
            dve.wait_ge(dve_step, 2)
            chain[0] = 2
            link(nc.vector.tensor_scalar(qkg[:], qkg[:], DK ** -0.5, None, ALU.mult))
            nc.vector.tensor_reduce(lam_s[:], lam_p[:], AX_X, ALU.add).then_inc(lam_ready, 1)
            for l in range(LAYERS):
                link(nc.vector.tensor_scalar(o_g[:, l, 1], o_g[:, l, 1], 1.0 - lam_init(l), None, ALU.mult))
            dve.wait_ge(c_ready, 1)
            for l in range(LAYERS):
                if l:
                    dve.wait_ge(ada_cols, l)
                for k in range(KT):
                    for half in range(2):
                        n = (l * KT + k) * 2 + half
                        cols = slice(half * 1536, half * 1536 + 1536)
                        dve.wait_ge(ada_landed[n % 4], 16 * (n // 4 + 1))
                        if k == 0:
                            ins_ = nc.vector.tensor_scalar(acc[:, cols], ada_w[n % 4][:], c_act[:, 0:1], None,
                                                           ALU.mult)
                        else:
                            dve.wait_ge(ada_used, n - 1)
                            ins_ = nc.vector.scalar_tensor_tensor(
                                out=acc[:, cols], in0=ada_w[n % 4][:], scalar=c_act[:, k:k + 1],
                                in1=acc[:, cols], op0=ALU.mult, op1=ALU.add)
                        ins_.then_inc(ada_used, 1)
                dve.wait_ge(ada_used, (l + 1) * 2 * KT)
                dve.sem_inc(ada_sum, 1)
                dve.wait_ge(ada_cols, l + 1)
                link(nc.vector.tensor_tensor(mod[:, l], ps[:, 4, 0:24], b_ada[:, l], ALU.add))
                link(nc.vector.scalar_tensor_tensor(out=mod[:, l, 8:16], in0=mod[:, l, 8:16], scalar=1.0,
                                                    in1=norm_g[:, l], op0=ALU.add, op1=ALU.mult))
            dve.wait_ge(lam_exp, 1)
            for l in range(LAYERS):
                link(nc.vector.scalar_tensor_tensor(out=neglam[:, l:l + 1], in0=lam_e[:, l, 1:2],
                                                    scalar=-lam_init(l), in1=lam_e[:, l, 0:1],
                                                    op0=ALU.add, op1=ALU.subtract))
            dve.wait_ge(consts, N_CONST)

            for m in range(KT):
                add_square(0, m)
            for l in range(LAYERS):
                name = f"layer{l}"
                unit = UNIT0[name]
                link(nc.vector.memset(wr_h[:].bitcast(F32), 0.0))
                link(nc.vector.memset(wr_l[:].bitcast(F32), 0.0))
                norm(l, mod[:, l, 8:16], mod[:, l, 0:8])
                link(nc.vector.tensor_copy(wr_h[:, :, 0:RANK], wr_raw[:, l]))
                nc.vector.tensor_tensor(wr_l[:, :, 0:RANK], wr_raw[:, l], wr_h[:, :, 0:RANK].bitcast(F32),
                                        ALU.subtract).then_inc(lr_w, 1)
                nc.vector.memset(u_in[:, :, 0:CONV_K - 1], 0.0).then_inc(dve_step, 1)
                chain[0] += 1
                for h in range(HEADS):
                    dve.wait_ge(tile_done, 2 * unit + h + 1)
                    dve.wait_ge(banks_free[h // 2], unit + 3 + h % 2)
                    if h >= 2:
                        dve.wait_ge(q_ss, l * HEADS + h - 1)
                    nc.vector.tensor_tensor(sq[:, h % 2], q[:, h], q[:, h], ALU.mult).then_inc(q_sq, 1)
                dve.wait_ge(q_sq, (l + 1) * HEADS)
                link(nc.vector.tensor_scalar(q[:], q[:], qkg[:, l:l + 1], None, ALU.mult))
                dve.wait_ge(qk_copied, 2 * l + 1)
                dve.wait_ge(glr_done, l + 1)
                link(nc.vector.tensor_tensor(k_sq[:], k_tok[:], k_tok[:], ALU.mult))
                link(nc.vector.tensor_reduce(ss_qk[:, 0].rearrange("p b g -> p (b g)"),
                                             k_sq[:].rearrange("p b (g d) -> p (b g) d", d=DK), AX_X, ALU.add))
                dve.wait_ge(q_ss, (l + 1) * HEADS)
                nc.vector.tensor_copy(ss_qk[:, 1].rearrange("p b g -> p (b g)"), ps[:, 5, 0:32]
                                      ).then_inc(qk_var, 1)
                dve.wait_ge(qk_root, l + 1)
                link(nc.vector.reciprocal(r_qk[:], r_qk[:]))
                link(nc.vector.tensor_scalar(nrq[:], r_qk[:, 1], -1.0, None, ALU.mult))
                nc.vector.tensor_tensor(
                    k_tok[:].rearrange("p b (g d) -> p (b g) d", d=DK),
                    k_tok[:].rearrange("p b (g d) -> p (b g) d", d=DK),
                    r_qk[:, 0].rearrange("p b g -> p (b g)").unsqueeze(2).to_broadcast([P, TB * 8, DK]),
                    ALU.mult).then_inc(k_normed, 1)
                for m in range(KT):
                    dve.wait_ge(conv_in, l * KT + m + 1)
                    link(nc.vector.tensor_scalar(conv[:, m], u_in[:, m, 0:S], conv_w[:, l, m, 0:1], None,
                                                 ALU.mult))
                    for j in range(1, CONV_K):
                        ins_ = nc.vector.scalar_tensor_tensor(
                            out=conv[:, m], in0=u_in[:, m, j:j + S], scalar=conv_w[:, l, m, j:j + 1],
                            in1=conv[:, m], op0=ALU.mult, op1=ALU.add)
                        if j < CONV_K - 1:
                            link(ins_)
                    ins_.then_inc(conv_done, 1)
                dve.wait_ge(z_in, l + 1)
                for tb in range(TB):
                    nc.vector.tensor_tensor(
                        zg[:, tb].rearrange("p (g h d) -> p g h d", g=2, h=HEADS),
                        zg[:, tb].rearrange("p (g h d) -> p g h d", g=2, h=HEADS),
                        o_g[:, l].unsqueeze(2).to_broadcast([P, 2, HEADS, P]), ALU.mult
                    ).then_inc(dve_step, 1)
                chain[0] += TB

                def biases(s):
                    qb, h = s // HEADS, s % HEADS
                    n = P * (qb + 1)
                    dve.wait_ge(scores, 2 * (l * STEPS + s) + 2)
                    for m in range(2):
                        ins_ = nc.vector.memset(ps[0:64, 4 + m, n - 64:n], NEG)
                        ins_.then_inc(dve_step, 1)
                        chain[0] += 1
                    dve.wait_ge(dve_step, chain[0])
                    link(nc.vector.tensor_reduce(smax[:, s % 2], ps[:, 4:6, 0:n], AX_X, ALU.max))
                    nc.vector.tensor_tensor(nbias[:, s % 2], smax[:, s % 2], nrq[:, qb, 2 * h:2 * h + 2], ALU.mult
                                            ).then_inc(bias_ready, 1)

                def combine(s):
                    n = P * (s // HEADS + 1)
                    dve.wait_ge(exp_done, 2 * (l * STEPS + s) + 2)
                    link(nc.vector.reciprocal(rz[:, s % 2], zs[:, s % 2]))
                    link(nc.vector.tensor_scalar(prob[:, s % 2, 1, 0:n], prob[:, s % 2, 1, 0:n], rz[:, s % 2, 1:2],
                                                 neglam[:, l:l + 1], ALU.mult, ALU.mult))
                    nc.vector.scalar_tensor_tensor(out=prob[:, s % 2, 0, 0:n], in0=prob[:, s % 2, 0, 0:n],
                                                   scalar=rz[:, s % 2, 0:1], in1=prob[:, s % 2, 1, 0:n],
                                                   op0=ALU.mult, op1=ALU.add).then_inc(attn_ready, 1)

                for s in range(STEPS + 1):
                    if s < STEPS:
                        biases(s)
                    if s:
                        combine(s - 1)

                dve.wait_ge(gate_mm, l + 1)
                nc.vector.tensor_scalar(log_a[:], ps[:, 4:6].rearrange("p a (b c) -> p (a b) c", b=2), 0.0,
                                        None, ALU.min).then_inc(gate_min, 1)
                dve.wait_ge(gate_soft, l + 1)
                nc.vector.tensor_tensor(log_a[:], log_a[:], soft[:], ALU.subtract).then_inc(loga_ready, 1)
                dve.wait_ge(gk_turned, l + 1)
                nc.vector.tensor_tensor(decay[:], ps[:, 6:8].rearrange("p a (b c) -> p (a b) c", b=2),
                                        decay[:], ALU.mult).then_inc(gk_ready, 1)
                for c in range(NCH):
                    dve.wait_ge(outer_done, l * NCH + c + 1)
                    for p in range(2):
                        if c == 0:
                            ins_ = nc.vector.tensor_copy(states[:, 0, p], ps[:, 4, p * 256:p * 256 + 256])
                        else:
                            if p == 0:
                                dve.wait_ge(state_ready, l * NCH + c)
                            ins_ = nc.vector.scalar_tensor_tensor(
                                out=states[:, c, p], in0=states[:, c - 1, p], scalar=aend[:, p, c:c + 1],
                                in1=ps[:, 4 + c % 2, p * 256:p * 256 + 256], op0=ALU.mult, op1=ALU.add)
                        if p == 0:
                            link(ins_)
                    ins_.then_inc(state_ready, 1)
                dve.wait_ge(o_copied, (l + 1) * STEPS)
                dve.wait_ge(gla_copied, (l + 1) * TB)
                dve.wait_ge(gla_o, (l + 1) * TB)
                for g in range(2):
                    for tb in range(TB):
                        o_sq = conv[:, tb % 2]
                        heads = slice(4 * g, 4 * g + 4)
                        link(nc.vector.tensor_tensor(o_sq, o[g][:, tb], o[g][:, tb], ALU.mult))
                        link(nc.vector.tensor_reduce(ss_o[:, tb, heads],
                                                     o_sq.rearrange("p (h d) -> p h d", d=P), AX_X, ALU.add))
                        link(nc.vector.tensor_tensor(o[g][:, tb], o[g][:, tb],
                                                     zg[:, tb, g * WIDTH:(g + 1) * WIDTH], ALU.mult))
                dve.sem_inc(o_var, 1)
                dve.wait_ge(o_root, 2 * l + 2)
                link(nc.vector.reciprocal(r_o[:], sd_o[:]))

                def mix_lows(j):
                    g, tb = j // TB, j % TB
                    dve.wait_ge(mix_high, l * 8 + j + 1)
                    hi = xh[:, 4 * g:4 * g + 4, tb * P:tb * P + P]
                    nc.vector.tensor_tensor(xl[:, 4 * g:4 * g + 4, tb * P:tb * P + P],
                                            ps[:, 4 + j % 4].rearrange("p (h c) -> p h c", h=4),
                                            hi.bitcast(F32), ALU.subtract).then_inc(mix_low, 1)

                for j in range(2 * TB):
                    g, tb = j // TB, j % TB
                    part = o[g][:, tb].rearrange("p (h d) -> p h d", d=P)
                    nc.vector.tensor_tensor(part, part,
                                            r_o[:, tb, 4 * g:4 * g + 4].unsqueeze(2).to_broadcast([P, 4, P]),
                                            ALU.mult).then_inc(o_normed, 1)
                    if j >= 2:
                        mix_lows(j - 2)
                mix_lows(6)
                mix_lows(7)
                residual(l + 1, unit + L_UNITS - L_OUT, lambda m: mod[:, l, 16 + m:17 + m], False)

            def ffn(name, n, gain):
                norm(n, gain)
                unit, split = UNIT0[name], SPLIT0[name]
                gate0 = 0 if name == "ffn1" else FT
                with dve.Fori(0, FT // 2) as i:
                    for u in range(2):
                        dve.wait_ge(ff_gate, i * 2 + (gate0 + u + 1))
                        dve.wait_ge(tile_done, i * 4 + (2 * unit + 2 * u + 2))
                        dve.wait_ge(low_ready, i * 2 + (split + u - 1))
                        nc.vector.tensor_tensor(tmp[:, u], ps[:, 2 * u + 1], gate[:, u], ALU.mult
                                                ).then_inc(tmp_ready, 1)
                        dve.wait_ge(tmp_ready, i * 2 + (split + u + 1))
                        dve.sem_inc(banks_free[u], 2)
                        dve.wait_ge(high_ready, i * 2 + (split + u + 1))
                        nc.vector.tensor_tensor(fl[:, bass.ds(i * 2 + u, 1)], tmp[:, u:u + 1],
                                                fh[:, bass.ds(i * 2 + u, 1)].bitcast(F32), ALU.subtract
                                                ).then_inc(low_ready, 1)
                residual(n + 1, unit + FT, lambda m: 0.5, True)

            ffn("ffn1", 2, gains[:, 0])

            norm(3, gains[:, 1])
            unit = UNIT0["mixer"]
            nc.vector.memset(tpad[:], 0.0).then_inc(dve_step, 1)
            chain[0] += 1
            dve.wait_ge(dve_step, chain[0])
            dve.sem_inc(m_prod, 2)
            dve.wait_ge(m_v, 1)
            for tb in range(TB):
                link(nc.vector.tensor_tensor(v2_sq[:], v2[:, tb], v2[:, tb], ALU.mult))
                link(nc.vector.tensor_reduce(ss_v[:, 0, tb:tb + 1], v2_sq[:], AX_X, ALU.add))
            dve.sem_inc(m_root_in, 1)
            dve.wait_ge(m_root, 1)
            link(nc.vector.reciprocal(ss_v[:, 2], ss_v[:, 1]))
            for tb in range(TB):
                link(nc.vector.tensor_scalar(v2[:, tb], v2[:, tb], ss_v[:, 2, tb:tb + 1], None, ALU.mult))
            dve.sem_inc(m_vn, 1)
            unit += M_V + M_U
            for j in range(M_CX):
                u = j % 2
                dve.wait_ge(m_gc, j + 1)
                dve.wait_ge(tile_done, 2 * (unit + j) + 2)
                link(nc.vector.tensor_tensor(tpad[:, u, 1:S + 1], ps[:, 2 * u + 1], gc[:, u], ALU.mult))
                dve.sem_inc(banks_free[u], 2)
                dve.sem_inc(m_prod, 1)
                link(nc.vector.tensor_scalar(cv[:, j], tpad[:, u, 0:S], conv2_w[:, j, 0:1], None, ALU.mult))
                for tap in (1, 2):
                    link(nc.vector.scalar_tensor_tensor(out=cv[:, j], in0=tpad[:, u, tap:tap + S],
                                                        scalar=conv2_w[:, j, tap:tap + 1], in1=cv[:, j],
                                                        op0=ALU.mult, op1=ALU.add))
            unit += M_CX
            dve.wait_ge(m_u, 1)
            dve.wait_ge(sgu_in, 32)
            for h in range(KT):
                dve.wait_ge(sgu_mm, h + 1)
                tmp_free("sgu", h)
                link(nc.vector.scalar_tensor_tensor(
                    out=tmp[:, h % 2].rearrange("p (c q) -> p c q", c=TB),
                    in0=ps[:, 4 + h % 2].rearrange("p (c q) -> p c q", c=TB), scalar=sgu_g[:, h:h + 1],
                    in1=bs[:, h].unsqueeze(1).to_broadcast([P, TB, P]), op0=ALU.mult, op1=ALU.add))
                dve.sem_inc(sgu_free, 1)
                nc.vector.tensor_tensor(tmp[:, h % 2], tmp[:, h % 2], u2[:, h], ALU.mult).then_inc(tmp_ready, 1)
                if h:
                    low("sgu", h - 1, al[:, h - 1], ah[:, h - 1])
            low("sgu", KT - 1, al[:, KT - 1], ah[:, KT - 1])
            for m in range(KT):
                u, t = m // 2 % 2, m % 2
                dve.wait_ge(tile_done, 2 * (unit + m // 2) + t + 1)
                tmp_free("gb", m)
                nc.vector.tensor_tensor(tmp[:, m % 2], ps[:, 2 * u + t], cv[:, m], ALU.mult
                                        ).then_inc(tmp_ready, 1)
                dve.wait_ge(tmp_ready, SPLIT0["gb"] + m + 1)
                dve.sem_inc(banks_free[u], 1)
                low("gb", m, bl[:, m], bh[:, m])
            unit += M_GB
            for j in range(KT):
                dve.wait_ge(m_sig, 2 * j + 2)
                dve.wait_ge(tile_done, 2 * unit + 4 * j + 4)
                tmp_free("merge", j)
                for t in range(2):
                    link(nc.vector.tensor_tensor(gc[:, t], ps[:, 2 + t], gc[:, t], ALU.mult))
                dve.sem_inc(banks_free[1], 2)
                nc.vector.tensor_tensor(tmp[:, j % 2], gc[:, 0], gc[:, 1], ALU.add).then_inc(tmp_ready, 1)
                dve.wait_ge(tmp_ready, SPLIT0["merge"] + j + 1)
                dve.sem_inc(m_sig_used, 2)
                low("merge", j, ml[:, j], mh[:, j])
            unit += M_MERGE
            residual(4, unit, lambda m: 1.0, False)
            ffn("ffn2", 4, gains[:, 2])
            norm(5, gains[:, 3])


def _tiles(w):
    return w.reshape(-1, P, w.shape[-1]).transpose(1, 0, 2)


def _feature_chunks(a, b):
    n = a.shape[1] // P
    both = np.stack([_tiles(a).reshape(P, KT, n, P), _tiles(b).reshape(P, KT, n, P)])
    return both.transpose(3, 1, 0, 2, 4).reshape(n, P, CW)


def _pair_chunks(w):
    n = w.shape[1] // P
    t = _tiles(w).reshape(P, KT, n // 2, 2, P)
    return t.transpose(2, 0, 3, 1, 4).reshape(n // 2, P, CW)


def _token_chunks(w):
    n = w.shape[1] // 256
    return _tiles(w).reshape(P, KT, n, 256).transpose(2, 0, 1, 3).reshape(n, P, CW)


def _half_chunks(w):
    t = w.reshape(2, FH, P, KT, P)
    return t.transpose(3, 0, 2, 1, 4).reshape(2 * KT, P, FW)


def _columns(a):
    a = a.reshape(*a.shape[:-1], -1, P)
    return np.moveaxis(a, -1, 0)


def kernel(x, c, w_ada, b_ada, norm_g, w_in, conv_w, w_gk, b_gk, gla_norm_g, qn_g, kn_g, lam_q1, lam_k1,
           lam_q2, lam_k2, diff_norm_g, w_out, ffn1_norm_2, ffn1_w_in_2, ffn1_w_out_2, mix_norm_2, w_in_2,
           sgu_norm_2, sgu_w_2, sgu_b_2, conv_w_2, w_proj_a_2, w_proj_b_2, w_out_2, ffn2_norm_2,
           ffn2_w_in_2, ffn2_w_out_2, final_norm_2):
    import concourse.bacc as bacc
    from concourse.bass_utils import run_bass_kernel_spmd

    arrays = {
        "x_t": _tiles(x[0].T),
        "c_col": _columns(c[0]),
        "b_ada": _columns(b_ada),
        "norm_g": _columns(norm_g),
        "gains": _columns(np.stack([ffn1_norm_2[0], mix_norm_2[0], ffn2_norm_2[0], final_norm_2])),
        "conv_w": _columns(conv_w).transpose(0, 1, 3, 2),
        "conv2_w": _columns(conv_w_2[0]).transpose(0, 2, 1),
        "sgu_g": _columns(sgu_norm_2[0]),
        "qk_g": np.stack([np.concatenate([qn_g, qn_g], 1).T, np.concatenate([kn_g, kn_g], 1).T], 2),
        "lam": np.stack([lam_q1, lam_k1, lam_q2, lam_k2], 1).reshape(1, -1),
        "o_g": np.stack([gla_norm_g, diff_norm_g], 1).reshape(1, -1),
        "w_gk": w_gk.transpose(1, 0, 2),
        "b_gk": b_gk,
        "w_ada": w_ada.reshape(LAYERS, KT, P, 3 * D),
        "sgu_w_t": sgu_w_2[0].transpose(2, 0, 1),
        "sgu_b": sgu_b_2[0].reshape(1, -1),
    }
    at, cols = 0, {}
    for name, n in (("gq", 256), ("gk", 256), ("gv", 512), ("lr", RANK), ("gz", 512), ("dq", 512),
                    ("dk", 512), ("dv", 512), ("dz", 512)):
        cols[name] = slice(at, at + n)
        at += n
    arrays["w_lr"] = np.stack([_tiles(w_in[l][:, cols["lr"]]) for l in range(LAYERS)], 1)
    for l in range(LAYERS):
        w = w_in[l]
        arrays[f"layer{l}_stream"] = np.concatenate([
            _pair_chunks(w[:, cols["dq"]]), _token_chunks(w[:, cols["dk"]]), _token_chunks(w[:, cols["dv"]]),
            _pair_chunks(w[:, 0:1024]), _token_chunks(w[:, cols["gz"]]), _token_chunks(w[:, cols["dz"]]),
            _pair_chunks(w_out[l])])
    for name, win, wout in (("ffn1", ffn1_w_in_2[0], ffn1_w_out_2[0]), ("ffn2", ffn2_w_in_2[0], ffn2_w_out_2[0])):
        arrays[name + "_in_stream"] = _feature_chunks(win[:, :D_FF], win[:, D_FF:])
        arrays[name + "_out_stream"] = _half_chunks(wout)
    u, v, gate_b, gate_c, xb, g_a, g_b = np.split(w_in_2[0], 7, axis=1)
    gates, projections = _feature_chunks(g_a, g_b), _feature_chunks(w_proj_a_2[0], w_proj_b_2[0])
    arrays["mixer_stream"] = np.concatenate([
        _token_chunks(v), _pair_chunks(u), _feature_chunks(gate_c, xb), _pair_chunks(gate_b),
        np.stack([gates, projections], 1).reshape(2 * KT, P, CW), _pair_chunks(w_out_2[0])])

    nc = bacc.Bacc("TRN2", target_bir_lowering=False, num_devices=1, dynamic_dma_scratch_size=1024)
    arrays = {name: np.ascontiguousarray(a) for name, a in arrays.items()}
    ins = {name: nc.dram_tensor(name, a.shape, F32, kind="ExternalInput").ap() for name, a in arrays.items()}
    out = nc.dram_tensor("y_t", (P, KT, S), F32, kind="ExternalOutput").ap()
    build(nc, ins, out)
    r = run_bass_kernel_spmd(nc, [arrays], core_ids=[0])
    return r.results[0]["y_t"].transpose(2, 1, 0).reshape(1, S, D)
```

```python
import math
from contextlib import ExitStack

import numpy as np

import concourse.bass as bass
import concourse.mybir as mybir

F32 = mybir.dt.float32
F32R = mybir.dt.float32r
ALU = mybir.AluOpType
ACT = mybir.ActivationFunctionType
AX_X = mybir.AxisListType.X

P = 128
D = 1024
S = 512
KT = D // P
TB = S // P
EPS = 1e-6
LAYERS = 2
CHUNK = 64
NCH = S // CHUNK
HEADS = 4
DK = 64
RANK = 16
CONV_K = 4
GLA_QK = 256
WIDTH = 512
D_FF = 2816
FT = D_FF // P
FH = FT // 2
CW = 16 * P
FW = FH * P
NEG = -1.0e30

L_CONV, L_Q, L_K, L_V, L_Z, L_OUT = 4, 2, 2, 2, 4, 4
L_UNITS = L_Q + L_K + L_V + L_CONV + L_Z + L_OUT
M_V, M_U, M_CX, M_GB, M_MERGE, M_OUT = 4, 4, 8, 4, 16, 4
M_UNITS = M_V + M_U + M_CX + M_GB + M_MERGE + M_OUT
FFN_UNITS = FT + KT
FFN_CHUNKS = FT + 2 * KT
UNIT0 = {"layer0": 0, "layer1": L_UNITS, "ffn1": 2 * L_UNITS}
UNIT0["mixer"] = UNIT0["ffn1"] + FFN_UNITS
UNIT0["ffn2"] = UNIT0["mixer"] + M_UNITS
CHUNK0 = {"layer0": 0, "layer1": L_UNITS, "ffn1": 2 * L_UNITS}
CHUNK0["mixer"] = CHUNK0["ffn1"] + FFN_CHUNKS
CHUNK0["ffn2"] = CHUNK0["mixer"] + M_UNITS
STEPS = HEADS * TB


def layer_order():
    parts = [("part", stage, j, p) for stage, n in
             (("conv", L_CONV), ("q", L_Q), ("k", L_K), ("v", L_V), ("z", L_Z))
             for j in range(n) for p in range(4)]
    after = {}

    def put(n, *stage):
        after.setdefault(n, []).append(stage)

    put(3, "lr")
    put(6, "gate")
    put(10, "decay")
    for m in range(KT):
        put(2 * m + 2, "conv", m)
    put(19, "conv_act")
    put(21, "turn_k")
    for tb in range(TB):
        put(22 + tb, "turn_v", tb)
    for c in range(NCH):
        put(26 + c, "outer", c)
    for tb in range(TB):
        put(29 + 2 * tb, "read_out", tb)
        put(30 + 2 * tb, "gla_ss", tb)
    put(33, "q_squares")
    put(36, "q_sums")
    put(36, "k_sums")
    put(37, "qk_norm")
    put(39, "turn_keys")
    for s in range(STEPS + 2):
        put(min(40 + s, 55), "attn", s)
        if s >= 5 and s % 4 == 1:
            put(min(41 + s, 55), "diff_ss", (s - 5) // 4)
        if s == 9:
            put(49, "gains", 0)
    put(55, "gains", 1)
    order = []
    for n, part in enumerate(parts):
        order += [part, *after.get(n, [])]
    return order


ORDER = layer_order()
PART0 = {"conv": 0, "q": L_CONV, "k": L_CONV + L_Q, "v": L_CONV + L_Q + L_K,
         "z": L_CONV + L_Q + L_K + L_V}


def emptied(unit, t):
    return 2 * (unit // 2) + 3 + t


def lam_init(l):
    return 0.8 - 0.6 * math.exp(-0.3 * l)


def build(nc, ins, out):
    ctx = ExitStack()
    with ctx:
        def sem(name):
            return ctx.enter_context(nc.semaphore(name))

        base = nc.sbuf_base
        top = nc.sbuf_usable_end
        base = (base + 63) // 64 * 64
        cursor = [base]

        def at(name, shape, dt, offset):
            n = 4 * int(np.prod(shape[1:]))
            assert offset + n <= top, (name, offset + n, top)
            return nc.alloc_sbuf_tensor_at(name, shape, dt, offset=offset, align_bytes=4)

        def sb(name, shape, dt=F32):
            n = (4 * int(np.prod(shape[1:])) + 31) // 32 * 32
            t = at(name, shape, dt, cursor[0])
            cursor[0] += n
            return t

        ps = ctx.enter_context(nc.psum_tensor("ps", [P, 8, 512], F32))

        x = sb("x", [P, KT, S])
        xh = sb("xh", [P, KT, S], F32R)
        xl = sb("xl", [P, KT, S], F32R)
        raw = [sb(f"raw{u}", [P, CW]) for u in range(2)]
        wh = [sb(f"wh{u}", [P, CW], F32R) for u in range(2)]
        wl = [sb(f"wl{u}", [P, CW], F32R) for u in range(2)]
        ones = sb("ones", [P, P])
        ident = sb("ident", [P, P])
        later = sb("later", [P, P])
        inchunk = sb("inchunk", [P, 2])
        inhalf = sb("inhalf", [P, 2])
        eps = sb("eps", [P, 3])
        sumsq = sb("sumsq", [P, S])
        sq = sb("sq", [P, 2, S])
        tmp = sb("tmp", [P, 2, S])
        diag = sq[:, 1].rearrange("p (b c) -> p b c", b=TB)
        norm_sd = sb("norm_sd", [P, TB])
        norm_r = sb("norm_r", [P, TB])
        mod = sb("mod", [P, LAYERS, 24])
        b_ada = sb("b_ada", [P, LAYERS, 24])
        norm_g = sb("norm_g", [P, LAYERS, KT])
        gains = sb("gains", [P, 4, KT])
        c_col = sb("c_col", [P, KT])
        c_act = sb("c_act", [P, KT])
        conv_w = sb("conv_w", [P, LAYERS, KT, CONV_K])
        conv2_w = sb("conv2_w", [P, KT, 3])
        sgu_g = sb("sgu_g", [P, KT])
        qk_g = sb("qk_g", [P, LAYERS, 2])
        qkg = sb("qkg", [P, LAYERS])
        lam_in = sb("lam_in", [P, LAYERS, 4, DK])
        lam_p = sb("lam_p", [P, LAYERS, 2, DK])
        lam_s = sb("lam_s", [P, LAYERS, 2])
        lam_e = sb("lam_e", [P, LAYERS, 2])
        neglam = sb("neglam", [P, LAYERS])
        o_g = sb("o_g", [P, LAYERS, 2, P])
        wgk = sb("wgk", [RANK + 1, LAYERS, GLA_QK])
        glr = sb("glr", [32, S])
        wr_raw = sb("wr_raw", [P, LAYERS, KT, RANK])
        arena = cursor[0]

        def place(name, shape, dt=F32):
            n = (4 * int(np.prod(shape[1:])) + 31) // 32 * 32
            t = at(name, shape, dt, cursor[0])
            cursor[0] += n
            return t

        acc = place("ada_acc", [P, 3 * D])
        ada_w = [place(f"ada_w{i}", [P, 3 * D // 2]) for i in range(4)]

        cursor[0] = arena
        u_in = place("u_in", [P, KT, S + CONV_K - 1])
        at_conv = cursor[0]
        conv = place("conv", [P, KT, S])
        q = place("q", [P, HEADS, S])
        k_tok = place("k_tok", [P, TB, WIDTH])
        at_kf = cursor[0]
        kf = place("kf", [P, HEADS, S])
        v = place("v", [P, TB, WIDTH])
        at_zg = cursor[0]
        zg = place("zg", [P, TB, 2 * WIDTH])
        at_p = cursor[0]
        prob = place("prob", [P, 2, 2, S])
        attn_t = place("attn_t", [P, 2, S])
        at_od = cursor[0]
        o_diff = place("o_diff", [P, TB, WIDTH])
        ss_qk = place("ss_qk", [P, 2, TB, 8])
        r_qk = place("r_qk", [P, 2, TB, 8])
        nrq = place("nrq", [P, TB, 8])
        smax = place("smax", [P, 2, 2])
        nbias = place("nbias", [P, 2, 2])
        zs = place("zs", [P, 2, 2])
        rz = place("rz", [P, 2, 2])
        ss_o = place("ss_o", [P, TB, 8])
        sd_o = place("sd_o", [P, TB, 8])
        r_o = place("r_o", [P, TB, 8])
        aend = place("aend", [P, 2, NCH])
        k_sq = at("k_sq", [P, TB, WIDTH], F32, at_od)
        states = at("states", [P, NCH, 2, 256], F32, arena)
        log_a = at("log_a", [P, TB, 256], F32, at_kf)
        decay = at("decay", [P, TB, 256], F32, at_kf + 4096)
        gv = at("gv", [P, TB, WIDTH], F32, at_p)
        soft = at("soft", [P, TB, 256], F32, at_p + 8192)
        wr_h = at("wr_h", [P, KT, P], F32R, at_zg + 4096)
        o_gla = at("o_gla", [P, TB, WIDTH], F32, at_conv + 4 * S * 4)
        o = (o_gla, o_diff)
        wr_l = at("wr_l", [P, KT, P], F32R, at_zg)

        cursor[0] = arena
        fh = place("fh", [P, FT, S], F32R)
        fl = place("fl", [P, FT, S], F32R)
        gate = place("gate", [P, 2, S])

        cursor[0] = arena
        at_v2 = cursor[0]
        v2 = place("v2", [P, TB, D])
        u2 = place("u2", [P, KT, S])
        bh = at("bh", [P, KT, S], F32R, at_v2)
        bl = at("bl", [P, KT, S], F32R, at_v2 + KT * S * 4)
        ah = place("ah", [P, KT, S], F32R)
        al = place("al", [P, KT, S], F32R)
        at_m = cursor[0]
        cv = place("cv", [P, KT, S])
        mh = at("mh", [P, KT, S], F32R, at_m)
        at_ml = cursor[0]
        ml = place("ml", [P, KT, S], F32R)
        ws_t = at("ws_t", [P, KT, P], F32, at_ml)
        bs = at("bs", [P, KT, P], F32, at_ml + 4096)
        v2_sq = at("v2_sq", [P, D], F32, at_ml + 8192)
        ss_v = at("ss_v", [P, 3, TB], F32, at_ml + 12288)
        gc = place("gc", [P, 2, S])
        tpad = place("tpad", [P, 2, S + 2])

        y = at("y", [P, KT, S], F32, arena)

        raw_landed = [sem(f"raw_landed{u}") for u in range(2)]
        w_high = sem("w_high")
        w_ready = sem("w_ready")
        half_used = sem("half_used")
        tile_done = sem("tile_done")
        banks_free = [sem(f"banks_free{u}") for u in range(2)]
        small_in = sem("small_in")
        x_in = sem("x_in")
        ada_landed = [sem(f"ada_landed{i}") for i in range(4)]
        ada_used = sem("ada_used")
        consts = sem("consts")
        dve_step = sem("dve_step")
        act_step = sem("act_step")
        pool_step = sem("pool_step")
        c_ready = sem("c_ready")
        ada_sum = sem("ada_sum")
        ada_cols = sem("ada_cols")
        ada_read = sem("ada_read")
        lam_ready = sem("lam_ready")
        lam_exp = sem("lam_exp")
        x_ready = sem("x_ready")
        sq_ready = sem("sq_ready")
        sq_used = sem("sq_used")
        sumsq_ready = sem("sumsq_ready")
        norm_ss = sem("norm_ss")
        norm_root = sem("norm_root")
        diag_ready = sem("diag_ready")
        norm_bc = sem("norm_bc")
        tmp_ready = sem("tmp_ready")
        high_ready = sem("high_ready")
        low_ready = sem("low_ready")
        lr_w = sem("lr_w")
        glr_done = sem("glr_done")
        glr_copied = sem("glr_copied")
        conv_done = sem("conv_done")
        conv_act = sem("conv_act")
        q_sq = sem("q_sq")
        q_ss = sem("q_ss")
        qk_var = sem("qk_var")
        qk_root = sem("qk_root")
        k_normed = sem("k_normed")
        k_turned = sem("k_turned")
        kf_ready = sem("kf_ready")
        scores = sem("scores")
        bias_ready = sem("bias_ready")
        exp_done = sem("exp_done")
        attn_ready = sem("attn_ready")
        attn_turned = sem("attn_turned")
        at_copied = sem("at_copied")
        pv_done = sem("pv_done")
        o_copied = sem("o_copied")
        gate_mm = sem("gate_mm")
        gate_min = sem("gate_min")
        gate_soft = sem("gate_soft")
        loga_ready = sem("loga_ready")
        decay_mm = sem("decay_mm")
        decay_exp = sem("decay_exp")
        gk_turned = sem("gk_turned")
        gk_ready = sem("gk_ready")
        gv_turned = sem("gv_turned")
        gv_ready = sem("gv_ready")
        outer_done = sem("outer_done")
        state_ready = sem("state_ready")
        gla_o = sem("gla_o")
        gla_copied = sem("gla_copied")
        o_var = sem("o_var")
        o_root = sem("o_root")
        o_normed = sem("o_normed")
        o_turned = sem("o_turned")
        mix_high = sem("mix_high")
        mix_low = sem("mix_low")
        z_act = sem("z_act")
        ff_gate = sem("ff_gate")
        m_root_in = sem("m_root_in")
        m_root = sem("m_root")
        m_vn = sem("m_vn")
        m_gc = sem("m_gc")
        m_prod = sem("m_prod")
        sgu_in = sem("sgu_in")
        sgu_mm = sem("sgu_mm")
        sgu_free = sem("sgu_free")
        m_sig = sem("m_sig")
        m_sig_used = sem("m_sig_used")
        y_ready = sem("y_ready")
        y_out = sem("y_out")

        SPLIT0 = {}
        n = 0
        for name, count in (("norm0", 8), ("norm1", 8), ("norm2", 8), ("ffn1", FT), ("norm3", 8),
                            ("sgu", 8), ("gb", 8), ("merge", 8), ("norm4", 8), ("ffn2", FT)):
            SPLIT0[name] = n
            n += count

        block = ctx.enter_context(nc.Block())

        segments = []
        for l in range(LAYERS):
            segments += [(ins[f"layer{l}_stream"], L_UNITS, CW)]
        segments += [(ins["ffn1_in_stream"], FT, CW), (ins["ffn1_out_stream"], 2 * KT, FW),
                     (ins["mixer_stream"], M_UNITS, CW),
                     (ins["ffn2_in_stream"], FT, CW), (ins["ffn2_out_stream"], 2 * KT, FW)]
        CHUNKS = sum(count for _, count, _ in segments)

        small = [
            (c_col, ins["c_col"]), (b_ada, ins["b_ada"]), (norm_g, ins["norm_g"]), (gains, ins["gains"]),
            (conv_w, ins["conv_w"]), (conv2_w, ins["conv2_w"]), (sgu_g, ins["sgu_g"]), (qk_g, ins["qk_g"]),
            (wr_raw, ins["w_lr"]),
        ]
        N_SMALL = 16 * (len(small) + 3 + LAYERS)
        ADA_N = LAYERS * KT * 2

        @block.sync
        def _(sp):
            sp.dma_start(x[:], ins["x_t"]).then_inc(x_in, 16)

            def load_pair(dram, size, i, chunk):
                for u in range(2):
                    if not (isinstance(i, int) and chunk == 0):
                        sp.wait_ge(w_ready, i * 2 + (chunk + u - 1))
                    sp.dma_start(raw[u][:, 0:size], dram[i * 2 + u]).then_inc(raw_landed[u], 16)

            chunk = 0
            for dram, count, size in segments:
                first = 0
                if chunk == 0:
                    load_pair(dram, size, 0, 0)
                    first = 1
                with sp.Fori(first, count // 2) as i:
                    load_pair(dram, size, i, chunk)
                chunk += count
            for k in range(KT):
                sp.wait_ge(y_ready, k + 1)
                sp.dma_start(out[:, k], y[:, k]).then_inc(y_out, 16)
            sp.wait_ge(y_out, 16 * KT)

        @block.gpsimd
        def _(pool):
            nc.gpsimd.memset(ones[:], 1.0).then_inc(pool_step, 1)
            nc.gpsimd.memset(ident[:], 0.0).then_inc(pool_step, 1)
            nc.gpsimd.memset(later[:], 1.0 / 16).then_inc(pool_step, 1)
            nc.gpsimd.memset(glr[:], 1.0).then_inc(pool_step, 1)
            pool.wait_ge(pool_step, 4)
            nc.gpsimd.affine_select(out=ident[:], in_=ident[:], compare_op=ALU.not_equal, fill=1.0, base=0,
                                    pattern=[[-1, P]], channel_multiplier=1).then_inc(pool_step, 1)
            nc.gpsimd.affine_select(out=later[:], in_=later[:], compare_op=ALU.is_gt, fill=0.0, base=0,
                                    pattern=[[-1, P]], channel_multiplier=1).then_inc(pool_step, 1)
            def split(size, i, chunk, u):
                pool.wait_ge(w_high, i * 2 + (chunk + u + 1))
                nc.gpsimd.tensor_tensor(wl[u][:, 0:size], raw[u][:, 0:size], wh[u][:, 0:size].bitcast(F32),
                                        ALU.subtract).then_inc(w_ready, 1)

            chunk = 0
            for _, count, size in segments:
                with pool.Fori(0, count // 2) as i:
                    for u in range(2):
                        split(size, i, chunk, u)
                chunk += count

        N_CONST = 10

        @block.scalar
        def _(act):
            for dst, src in small:
                act.dma_start(dst[:], src).then_inc(small_in, 16)
            act.dma_start(lam_in[:], ins["lam"].to_broadcast([P, LAYERS * 4 * DK])
                          .rearrange("p (l a d) -> p l a d", l=LAYERS, a=4)).then_inc(small_in, 16)
            act.dma_start(o_g[:], ins["o_g"].to_broadcast([P, LAYERS * 2 * P])
                          .rearrange("p (l a d) -> p l a d", l=LAYERS, a=2)).then_inc(small_in, 16)
            act.dma_start(wgk[0:RANK], ins["w_gk"]).then_inc(small_in, 16)
            for l in range(LAYERS):
                act.dma_start(wgk[RANK:RANK + 1, l], ins["b_gk"][l:l + 1]).then_inc(small_in, 16)
            chain = [0]

            def link(ins_):
                chain[0] += 1
                ins_.then_inc(act_step, 1)
                act.wait_ge(act_step, chain[0])

            def take_high(chunk, i=0):
                if isinstance(i, int) and chunk >= CHUNKS:
                    return
                u = chunk % 2
                act.wait_ge(raw_landed[u], i * 16 + (16 * (chunk // 2) + 16))
                nc.scalar.activation(wh[u][:], raw[u][:], ACT.Copy).then_inc(w_high, 1)

            def ada_load(n):
                l, k, half = n // (2 * KT), n // 2 % KT, n % 2
                if n >= 4:
                    act.wait_ge(ada_used, n - 3)
                act.dma_start(ada_w[n % 4][:], ins["w_ada"][l, k, :, half * 1536:half * 1536 + 1536]
                              ).then_inc(ada_landed[n % 4], 16)

            for n in range(4):
                ada_load(n)
            act.wait_ge(small_in, N_SMALL)
            nc.scalar.activation(c_act[:], c_col[:], ACT.Silu).then_inc(c_ready, 1)
            for n in range(4, ADA_N):
                ada_load(n)
            act.wait_ge(lam_ready, 1)
            nc.scalar.activation(lam_e[:], lam_s[:], ACT.Exp).then_inc(lam_exp, 1)

            def squares(n, ms=range(KT)):
                for m in ms:
                    at_ = n * KT + m
                    if n == 0:
                        act.wait_ge(x_in, 16)
                    else:
                        act.wait_ge(x_ready, at_ - KT + 1)
                    if at_ >= 2:
                        act.wait_ge(sq_used, at_ - 1)
                    nc.scalar.activation(sq[:, m % 2], x[:, m], ACT.Square).then_inc(sq_ready, 1)

            def norm(n, splits=True):
                act.wait_ge(norm_ss, n + 1)
                nc.scalar.activation(norm_sd[:], ps[:, 6, 0:TB], ACT.Sqrt, bias=eps[:, 0:1],
                                     scale=1.0 / D).then_inc(norm_root, 1)
                if splits:
                    for k in range(KT):
                        high(f"norm{n}", k, xh[:, k])

            def high(name, k, dst):
                at_ = SPLIT0[name] + k
                act.wait_ge(tmp_ready, at_ + 1)
                nc.scalar.activation(dst, tmp[:, k % 2], ACT.Copy).then_inc(high_ready, 1)

            act.wait_ge(consts, N_CONST)
            squares(0)
            take_high(0)
            take_high(1)
            for l in range(LAYERS):
                unit0 = UNIT0[f"layer{l}"]
                norm(l)

                def empty(stage, j, t):
                    unit = unit0 + PART0[stage] + j
                    u = unit % 2
                    act.wait_ge(tile_done, 2 * unit + t + 1)
                    if t:
                        take_high(unit + 2)
                    bank = ps[:, 2 * u + t]
                    if stage == "conv":
                        dst = u_in[:, 2 * j + t, CONV_K - 1:]
                    elif stage == "q":
                        dst = q[:, 2 * j + t]
                    else:
                        dst = {"k": k_tok, "v": v, "z": zg}[stage][:, 2 * t:2 * t + 2, 256 * j:256 * j + 256]
                        bank = bank.rearrange("p (b c) -> p b c", b=2)
                    nc.scalar.activation(dst, bank, ACT.Copy).then_inc(banks_free[u], 1)

                def exps(s):
                    qb, h = s // HEADS, s % HEADS
                    n = P * (qb + 1)
                    if s >= 2:
                        act.wait_ge(attn_turned, l * STEPS + s - 1)
                    act.wait_ge(bias_ready, l * STEPS + s + 1)
                    for m in range(2):
                        nc.scalar.activation(prob[:, s % 2, m, 0:n], ps[:, 4 + m, 0:n], ACT.Exp,
                                             bias=nbias[:, s % 2, m:m + 1],
                                             scale=r_qk[:, 1, qb, 2 * h + m:2 * h + m + 1],
                                             accum_out=zs[:, s % 2, m:m + 1]).then_inc(exp_done, 1)

                def copy_turned(s):
                    n = P * (s // HEADS + 1)
                    act.wait_ge(attn_turned, l * STEPS + s + 1)
                    if s >= 2:
                        act.wait_ge(pv_done, l * STEPS + s - 1)
                    nc.scalar.activation(attn_t[:, s % 2, 0:n], ps[:, 6, 0:n], ACT.Copy
                                         ).then_inc(at_copied, 1)

                def copy_o(s):
                    qb, h = s // HEADS, s % HEADS
                    act.wait_ge(pv_done, l * STEPS + s + 1)
                    nc.scalar.activation(o_diff[:, qb, h * P:h * P + P], ps[:, 7, 0:P],
                                         ACT.Copy).then_inc(o_copied, 1)

                for stage, *at_ in ORDER:
                    if stage == "part":
                        if at_[2] % 2:
                            empty(at_[0], at_[1], at_[2] // 2)
                    elif stage == "lr":
                        act.wait_ge(glr_done, l + 1)
                        nc.scalar.activation(glr[0:RANK], ps[0:RANK, 4], ACT.Copy).then_inc(glr_copied, 1)
                    elif stage == "conv_act":
                        for m in range(KT):
                            act.wait_ge(conv_done, l * KT + m + 1)
                            nc.scalar.activation(conv[:, m], conv[:, m], ACT.Silu).then_inc(conv_act, 1)
                    elif stage == "gate":
                        act.wait_ge(gate_min, l + 1)
                        link(nc.scalar.activation(soft[:], ps[:, 4:6].rearrange("p a (b c) -> p (a b) c", b=2),
                                                  ACT.Abs))
                        link(nc.scalar.activation(soft[:], soft[:], ACT.Exp, scale=-1.0))
                        nc.scalar.activation(soft[:], soft[:], ACT.Ln, bias=eps[:, 2:3]).then_inc(gate_soft, 1)
                    elif stage == "decay":
                        act.wait_ge(decay_mm, 2 * l + 1)
                        nc.scalar.activation(decay[:], ps[:, 6:8].rearrange("p a (b c) -> p (a b) c", b=2),
                                             ACT.Exp).then_inc(decay_exp, 1)
                        act.wait_ge(decay_mm, 2 * l + 2)
                        nc.scalar.activation(aend[:], ps[:, 4, 0:16].rearrange("p (a c) -> p a c", a=2),
                                             ACT.Exp).then_inc(decay_exp, 1)
                    elif stage == "turn_v":
                        tb = at_[0]
                        act.wait_ge(gv_turned, l * TB + tb + 1)
                        nc.scalar.activation(gv[:, tb], ps[:, 4 + tb % 2], ACT.Copy).then_inc(gv_ready, 1)
                    elif stage == "read_out":
                        tb = at_[0]
                        act.wait_ge(gla_o, l * TB + tb + 1)
                        nc.scalar.activation(o_gla[:, tb].rearrange("p (a b c) -> p a b c", a=2, b=2),
                                             ps[:, 6:8, 0:256].rearrange("p b (a c) -> p a b c", a=2),
                                             ACT.Copy).then_inc(gla_copied, 1)
                    elif stage == "qk_norm":
                        act.wait_ge(qk_var, l + 1)
                        nc.scalar.activation(r_qk[:], ss_qk[:], ACT.Sqrt, bias=eps[:, 0:1], scale=1.0 / DK
                                             ).then_inc(qk_root, 1)
                    elif stage == "turn_keys":
                        for h in range(HEADS):
                            act.wait_ge(k_turned, l * HEADS + h + 1)
                            nc.scalar.activation(kf[:, h], ps[:, 4 + h], ACT.Copy).then_inc(kf_ready, 1)
                    elif stage == "attn":
                        s = at_[0]
                        if s < STEPS:
                            exps(s)
                        if 1 <= s <= STEPS:
                            copy_turned(s - 1)
                        if s >= 2:
                            copy_o(s - 2)
                    elif stage == "gains":
                        g = at_[0]
                        if g == 0:
                            unit = unit0 + PART0["z"] + 1
                            for u in range(2):
                                act.wait_ge(banks_free[u], emptied(unit, 1))
                        else:
                            unit = unit0 + PART0["z"] + 3
                            for u in range(2):
                                act.wait_ge(banks_free[u], emptied(unit, 1))
                        part = zg[:, :, g * WIDTH:(g + 1) * WIDTH]
                        nc.scalar.activation(part, part, ACT.Silu).then_inc(z_act, 1)

                act.wait_ge(o_var, l + 1)
                nc.scalar.activation(sd_o[:, :, 0:4], ss_o[:, :, 0:4], ACT.Sqrt, bias=eps[:, 1:2],
                                     scale=1.0 / P).then_inc(o_root, 1)
                nc.scalar.activation(sd_o[:, :, 4:8], ss_o[:, :, 4:8], ACT.Sqrt, bias=eps[:, 0:1],
                                     scale=1.0 / P).then_inc(o_root, 1)
                for j in range(2 * TB):
                    g, tb = j // TB, j % TB
                    act.wait_ge(o_turned, l * 8 + j + 1)
                    nc.scalar.activation(xh[:, 4 * g:4 * g + 4, tb * P:tb * P + P],
                                         ps[:, 4 + j % 4].rearrange("p (h c) -> p h c", h=4),
                                         ACT.Copy).then_inc(mix_high, 1)
                out_unit = unit0 + L_UNITS - L_OUT
                for j in range(L_OUT):
                    act.wait_ge(tile_done, 2 * (out_unit + j + 1))
                    take_high(out_unit + j + 2)
                    squares(l + 1, (2 * j, 2 * j + 1))

            def ffn(name, n):
                norm(n)
                unit, chunk = UNIT0[name], CHUNK0[name]
                split = SPLIT0[name]
                with act.Fori(0, FT // 2) as i:
                    for u in range(2):
                        act.wait_ge(tile_done, i * 4 + (2 * unit + 2 * u + 1))
                        act.wait_ge(tmp_ready, i * 2 + (split + u - 1))
                        nc.scalar.activation(gate[:, u], ps[:, 2 * u], ACT.Silu).then_inc(ff_gate, 1)
                        act.wait_ge(tile_done, i * 4 + (2 * unit + 2 * u + 2))
                        take_high(chunk + 2 + u, i)
                        act.wait_ge(tmp_ready, i * 2 + (split + u + 1))
                        nc.scalar.activation(fh[:, bass.ds(i * 2 + u, 1)], tmp[:, u:u + 1], ACT.Copy
                                             ).then_inc(high_ready, 1)
                unit += FT
                chunk += FT
                for m in range(KT):
                    act.wait_ge(half_used, (0 if name == "ffn1" else KT) + m + 1)
                    take_high(chunk + 2 * m + 2)
                    act.wait_ge(tile_done, 2 * (unit + m + 1))
                    take_high(chunk + 2 * m + 3)
                    squares(n + 1, (m,))

            ffn("ffn1", 2)

            norm(3)
            unit, chunk = UNIT0["mixer"], CHUNK0["mixer"]
            for j in range(M_V):
                for t in range(2):
                    act.wait_ge(tile_done, 2 * unit + 2 * j + t + 1)
                    if t:
                        take_high(chunk + j + 2)
                    nc.scalar.activation(v2[:, 2 * t:2 * t + 2, 256 * j:256 * j + 256],
                                         ps[:, 2 * (j % 2) + t].rearrange("p (b c) -> p b c", b=2),
                                         ACT.Gelu_apprx_tanh).then_inc(banks_free[j % 2], 1)
            act.dma_start(ws_t[:], ins["sgu_w_t"]).then_inc(sgu_in, 16)
            act.dma_start(bs[:].rearrange("p h q -> p (h q)"), ins["sgu_b"].to_broadcast([P, KT * P])
                          ).then_inc(sgu_in, 16)
            unit += M_V
            chunk += M_V
            with act.Fori(0, M_U // 2) as i:
                for u in range(2):
                    for t in range(2):
                        act.wait_ge(tile_done, i * 4 + (2 * unit + 2 * u + t + 1))
                        if t:
                            take_high(chunk + u + 2, i)
                        nc.scalar.activation(u2[:, bass.ds(i * 4 + (2 * u + t), 1)],
                                             ps[:, 2 * u + t:2 * u + t + 1],
                                             ACT.Gelu_apprx_tanh).then_inc(banks_free[u], 1)
            unit += M_U
            chunk += M_U
            act.wait_ge(m_root_in, 1)
            nc.scalar.activation(ss_v[:, 1], ss_v[:, 0], ACT.Sqrt, bias=eps[:, 0:1], scale=1.0 / D
                                 ).then_inc(m_root, 1)
            with act.Fori(0, M_CX // 2) as i:
                for u in range(2):
                    act.wait_ge(tile_done, i * 4 + (2 * unit + 2 * u + 1))
                    act.wait_ge(m_prod, i * 2 + (u + 1))
                    nc.scalar.activation(gc[:, u], ps[:, 2 * u], ACT.Copy).then_inc(m_gc, 1)
                    act.wait_ge(tile_done, i * 4 + (2 * unit + 2 * u + 2))
                    take_high(chunk + u + 2, i)
            unit += M_CX
            chunk += M_CX
            for h in range(KT):
                high("sgu", h, ah[:, h])
            for j in range(M_GB):
                high("gb", 2 * j, bh[:, 2 * j])
                act.wait_ge(tile_done, 2 * (unit + j + 1))
                take_high(chunk + j + 2)
                high("gb", 2 * j + 1, bh[:, 2 * j + 1])
            unit += M_GB
            chunk += M_GB
            for j in range(KT):
                for t in range(2):
                    act.wait_ge(tile_done, 2 * unit + 4 * j + t + 1)
                    if t:
                        take_high(chunk + 2 * j + 2)
                    if j:
                        act.wait_ge(m_sig_used, 2 * j)
                    nc.scalar.activation(gc[:, t], ps[:, t], ACT.Sigmoid).then_inc(m_sig, 1)
                act.wait_ge(m_sig, 2 * j + 2)
                act.sem_inc(banks_free[0], 2)
                act.wait_ge(tile_done, 2 * unit + 4 * j + 4)
                take_high(chunk + 2 * j + 3)
                high("merge", j, mh[:, j])
            unit += M_MERGE
            chunk += M_MERGE
            for j in range(M_OUT):
                act.wait_ge(tile_done, 2 * (unit + j + 1))
                take_high(chunk + j + 2)
                squares(4, (2 * j, 2 * j + 1))
            ffn("ffn2", 4)
            norm(5, splits=False)

        @block.tensor
        def _(pe):
            def products(bank_ap, wt, xk, first, last):
                (w0, w1), (x0, x1) = wt, xk
                nc.tensor.matmul(bank_ap, w0, x0, start=first, stop=False)
                nc.tensor.matmul(bank_ap, w0, x1, start=False, stop=False)
                return nc.tensor.matmul(bank_ap, w1, x0, start=False, stop=last)

            def claim(i, unit, u):
                pe.wait_ge(banks_free[u], i * 2 + (unit + 2))

            def chunk_ready(i, chunk, u):
                pe.wait_ge(w_ready, i * 2 + (chunk + u + 1))

            def feature_unit(i, unit, chunk, u, moving, low0=None):
                claim(i, unit, u)
                chunk_ready(i, chunk, u)
                for t in range(2):
                    mh_, ml_ = moving[t]
                    for k in range(KT):
                        if t == 0 and low0 is not None:
                            pe.wait_ge(low_ready, low0 + k + 1)
                        cols = slice((t * KT + k) * P, (t * KT + k + 1) * P)
                        last = products(ps[:, 2 * u + t], (wh[u][:, cols], wl[u][:, cols]),
                                        (mh_[:, k], ml_[:, k]), k == 0, k == KT - 1)
                    last.then_inc(tile_done, 1)

            def token_block(u, tb):
                cols = slice(tb * P, tb * P + P)
                dst = ps[:, 2 * u + tb // 2, (tb % 2) * 256:(tb % 2) * 256 + 256]
                for k in range(KT):
                    w = slice(k * 256, k * 256 + 256)
                    nc.tensor.matmul(dst, xh[:, k, cols], wh[u][:, w], start=(k == 0), stop=False)
                    nc.tensor.matmul(dst, xl[:, k, cols], wh[u][:, w], start=False, stop=False)
                    last = nc.tensor.matmul(dst, xh[:, k, cols], wl[u][:, w], start=False,
                                            stop=(k == KT - 1))
                return last

            def token_unit(i, unit, chunk, u):
                claim(i, unit, u)
                chunk_ready(i, chunk, u)
                for tb in range(TB):
                    last = token_block(u, tb)
                    if tb % 2:
                        last.then_inc(tile_done, 1)

            def units(count, unit, chunk, body):
                with pe.Fori(0, count // 2) as i:
                    for u in range(2):
                        body(i, unit, chunk, u)

            both_x = [(xh, xl), (xh, xl)]

            def norm(n):
                pe.wait_ge(sumsq_ready, n + 1)
                for tb in range(TB):
                    last = nc.tensor.matmul(ps[:, 6, tb:tb + 1], sumsq[:, tb * P:tb * P + P], ones[:, 0:1],
                                            start=True, stop=True)
                last.then_inc(norm_ss, 1)
                pe.wait_ge(diag_ready, n + 1)
                nc.tensor.matmul(ps[:, 7], ones[:], sq[:, 1], start=True,
                                 stop=True).then_inc(norm_bc, 1)

            pe.wait_ge(consts, N_CONST)
            for l in range(LAYERS):
                pe.wait_ge(ada_sum, l + 1)
                for m in range(24):
                    last = nc.tensor.matmul(ps[:, 4, m:m + 1], acc[:, m * P:m * P + P], ones[:, 0:1],
                                            start=True, stop=True)
                last.then_inc(ada_cols, 1)
            for l in range(LAYERS):
                unit0 = UNIT0[f"layer{l}"]
                norm(l)

                def part(stage, j, p):
                    unit = unit0 + PART0[stage] + j
                    u, t, half = unit % 2, p // 2, p % 2
                    if p == 0:
                        pe.wait_ge(banks_free[u], emptied(unit, 1) - 2)
                        pe.wait_ge(w_ready, unit + 1)
                    if stage in ("conv", "q"):
                        for k in range(half * KT // 2, (half + 1) * KT // 2):
                            if (stage, j, t) == ("conv", 0, 0):
                                pe.wait_ge(low_ready, SPLIT0[f"norm{l}"] + k + 1)
                            cols = slice((t * KT + k) * P, (t * KT + k + 1) * P)
                            last = products(ps[:, 2 * u + t], (wh[u][:, cols], wl[u][:, cols]),
                                            (xh[:, k], xl[:, k]), k == 0, k == KT - 1)
                    else:
                        last = token_block(u, p)
                    if half:
                        last.then_inc(tile_done, 1)

                def score(s):
                    qb, h = s // HEADS, s % HEADS
                    if s:
                        pe.wait_ge(exp_done, 2 * (l * STEPS + s))
                    for m in range(2):
                        rows = slice(64 * m, 64 * m + 64)
                        nc.tensor.matmul(ps[:, 4 + m, 0:P * (qb + 1)], q[rows, h, qb * P:qb * P + P],
                                         kf[rows, h, 0:P * (qb + 1)], start=True, stop=True
                                         ).then_inc(scores, 1)

                def turn(s):
                    pe.wait_ge(attn_ready, l * STEPS + s + 1)
                    if s:
                        pe.wait_ge(at_copied, l * STEPS + s)
                    for kb in range(s // HEADS + 1):
                        last = nc.tensor.transpose(ps[:, 6, kb * P:kb * P + P],
                                                   prob[:, s % 2, 0, kb * P:kb * P + P], ident[:])
                    last.then_inc(attn_turned, 1)

                def pv(s):
                    qb, h = s // HEADS, s % HEADS
                    pe.wait_ge(at_copied, l * STEPS + s + 1)
                    if s:
                        pe.wait_ge(o_copied, l * STEPS + s)
                    for kb in range(qb + 1):
                        last = nc.tensor.matmul(ps[:, 7, 0:P], attn_t[:, s % 2, kb * P:kb * P + P],
                                                v[:, kb, h * P:h * P + P], start=(kb == 0), stop=(kb == qb))
                    last.then_inc(pv_done, 1)

                def outer(c):
                    if c >= 2:
                        pe.wait_ge(state_ready, l * NCH + c - 1)
                    rows = slice(64 * (c % 2), 64 * (c % 2) + 64)
                    for p in range(2):
                        last = nc.tensor.matmul(ps[:, 4 + c % 2, p * 256:p * 256 + 256],
                                                decay[rows, c // 2, p * P:p * P + P],
                                                gv[rows, c // 2, p * 256:p * 256 + 256],
                                                start=True, stop=True)
                    last.then_inc(outer_done, 1)

                def read_out(tb):
                    pe.wait_ge(state_ready, l * NCH + 2 * tb + 2)
                    if tb:
                        pe.wait_ge(gla_copied, l * TB + tb)
                    for half in range(2):
                        c = 2 * tb + half
                        for h in range(HEADS):
                            rows = slice(64 * (h % 2), 64 * (h % 2) + 64)
                            last = nc.tensor.matmul(
                                ps[64 * half:64 * half + 64, 6 + h % 2, (h // 2) * P:(h // 2) * P + P],
                                conv[rows, h // 2, c * CHUNK:(c + 1) * CHUNK],
                                states[rows, c, h // 2, (h % 2) * P:(h % 2) * P + P],
                                start=True, stop=True)
                    last.then_inc(gla_o, 1)

                for stage, *at_ in ORDER:
                    if stage == "part":
                        part(*at_)
                    elif stage == "lr":
                        pe.wait_ge(lr_w, l + 1)
                        for k in range(KT):
                            last = products(ps[:, 4], (wr_h[:, k], wr_l[:, k]), (xh[:, k], xl[:, k]),
                                            k == 0, k == KT - 1)
                        last.then_inc(glr_done, 1)
                    elif stage == "gate":
                        pe.wait_ge(glr_copied, l + 1)
                        for tb in range(TB):
                            last = nc.tensor.matmul(ps[:, 4 + tb // 2, (tb % 2) * 256:(tb % 2) * 256 + 256],
                                                    glr[0:RANK + 1, tb * P:tb * P + P], wgk[:, l],
                                                    start=True, stop=True)
                        last.then_inc(gate_mm, 1)
                    elif stage == "decay":
                        pe.wait_ge(loga_ready, l + 1)
                        for tb in range(TB):
                            last = nc.tensor.matmul(ps[:, 6 + tb // 2, (tb % 2) * 256:(tb % 2) * 256 + 256],
                                                    later[:], log_a[:, tb], start=True, stop=True)
                        last.then_inc(decay_mm, 1)
                        for tb in range(TB):
                            for p in range(2):
                                last = nc.tensor.matmul(ps[:, 4, p * NCH + 2 * tb:p * NCH + 2 * tb + 2],
                                                        log_a[:, tb, p * P:p * P + P], inchunk[:],
                                                        start=True, stop=True)
                        last.then_inc(decay_mm, 1)
                    elif stage == "turn_k":
                        pe.wait_ge(conv_act, (l + 1) * KT)
                        pe.wait_ge(decay_exp, 2 * l + 2)
                        for tb in range(TB):
                            for p in range(2):
                                c0 = (tb % 2) * 256 + p * P
                                last = nc.tensor.transpose(ps[:, 6 + tb // 2, c0:c0 + P],
                                                           conv[:, 2 + p, tb * P:tb * P + P], ident[:])
                        last.then_inc(gk_turned, 1)
                    elif stage == "turn_v":
                        tb = at_[0]
                        if tb >= 2:
                            pe.wait_ge(gv_ready, l * TB + tb - 1)
                        for h in range(HEADS):
                            last = nc.tensor.transpose(ps[:, 4 + tb % 2, h * P:h * P + P],
                                                       conv[:, 4 + h, tb * P:tb * P + P], ident[:])
                        last.then_inc(gv_turned, 1)
                    elif stage == "outer":
                        if at_[0] == 0:
                            pe.wait_ge(gk_ready, l + 1)
                            pe.wait_ge(gv_ready, (l + 1) * TB)
                        outer(at_[0])
                    elif stage == "read_out":
                        read_out(at_[0])
                    elif stage == "q_sums":
                        pe.wait_ge(q_sq, (l + 1) * HEADS)
                        pe.wait_ge(state_ready, (l + 1) * NCH)
                        for h in range(HEADS):
                            for tb in range(TB):
                                last = nc.tensor.matmul(ps[:, 5, tb * 8 + 2 * h:tb * 8 + 2 * h + 2],
                                                        (sq, tmp)[h // 2][:, h % 2, tb * P:tb * P + P],
                                                        inhalf[:], start=True, stop=True)
                        last.then_inc(q_ss, 1)
                    elif stage == "turn_keys":
                        pe.wait_ge(k_normed, l + 1)
                        pe.wait_ge(gla_copied, (l + 1) * TB)
                        for h in range(HEADS):
                            for tb in range(TB):
                                last = nc.tensor.transpose(ps[:, 4 + h, tb * P:tb * P + P],
                                                           k_tok[:, tb, h * P:h * P + P], ident[:])
                            last.then_inc(k_turned, 1)
                    elif stage == "attn":
                        s = at_[0]
                        if s == 0:
                            pe.wait_ge(kf_ready, (l + 1) * HEADS)
                        if s == 2:
                            for u in range(2):
                                pe.wait_ge(banks_free[u], emptied(unit0 + PART0["v"] + u, 1))
                        if s < STEPS:
                            score(s)
                        if 1 <= s <= STEPS:
                            turn(s - 1)
                        if s >= 2:
                            pv(s - 2)

                for j in range(2 * TB):
                    g, tb = j // TB, j % TB
                    pe.wait_ge(o_normed, l * 8 + j + 1)
                    if j >= 4:
                        pe.wait_ge(mix_low, l * 8 + j - 3)
                    for h in range(HEADS):
                        last = nc.tensor.transpose(ps[:, 4 + j % 4, h * P:h * P + P],
                                                   o[g][:, tb, h * P:h * P + P], ident[:])
                    last.then_inc(o_turned, 1)
                pe.wait_ge(mix_low, (l + 1) * 8)
                unit = unit0 + L_UNITS - L_OUT
                units(L_OUT, unit, unit, lambda i, a, b, u: feature_unit(i, a, b, u, both_x))

            def ffn(name, n):
                norm(n)
                unit, chunk = UNIT0[name], CHUNK0[name]
                feature_unit(0, unit, chunk, 0, both_x, low0=SPLIT0[f"norm{n}"])
                feature_unit(0, unit, chunk, 1, both_x)
                with pe.Fori(1, FT // 2) as i:
                    for u in range(2):
                        feature_unit(i, unit, chunk, u, both_x)
                unit += FT
                chunk += FT
                pe.wait_ge(low_ready, SPLIT0[name] + FT)
                with pe.Fori(0, KT // 2) as i:
                    for m in range(2):
                        claim(i, unit, m)
                        for half in range(2):
                            pe.wait_ge(w_ready, i * 4 + (chunk + 2 * m + half + 1))
                            for kk in range(FH):
                                k = half * FH + kk
                                cols = slice(kk * P, kk * P + P)
                                last = products(ps[:, 2 * m], (wh[half][:, cols], wl[half][:, cols]),
                                                (fh[:, k], fl[:, k]), k == 0, k == FT - 1)
                            if half == 0:
                                last.then_inc(half_used, 1)
                        last.then_inc(tile_done, 2)

            ffn("ffn1", 2)

            norm(3)
            pe.wait_ge(low_ready, SPLIT0["norm3"] + KT)
            unit, chunk = UNIT0["mixer"], CHUNK0["mixer"]
            units(M_V, unit, chunk, token_unit)
            unit += M_V
            chunk += M_V
            units(M_U + M_CX, unit, chunk, lambda i, a, b, u: feature_unit(i, a, b, u, both_x))
            unit += M_U + M_CX
            chunk += M_U + M_CX
            pe.wait_ge(m_vn, 1)
            pe.wait_ge(sgu_in, 32)
            for h in range(KT):
                if h >= 2:
                    pe.wait_ge(sgu_free, h - 1)
                for c in range(TB):
                    last = nc.tensor.matmul(ps[:, 4 + h % 2, c * P:c * P + P], v2[:, c, h * P:h * P + P],
                                            ws_t[:, h], start=True, stop=True)
                last.then_inc(sgu_mm, 1)
            units(M_GB, unit, chunk, lambda i, a, b, u: feature_unit(i, a, b, u, both_x))
            unit += M_GB
            chunk += M_GB
            pe.wait_ge(low_ready, SPLIT0["gb"] + KT)
            units(M_MERGE, unit, chunk,
                  lambda i, a, b, u: feature_unit(i, a, b, u, both_x if u == 0 else [(ah, al), (bh, bl)]))
            unit += M_MERGE
            chunk += M_MERGE
            pe.wait_ge(low_ready, SPLIT0["merge"] + KT)
            units(M_OUT, unit, chunk, lambda i, a, b, u: feature_unit(i, a, b, u, [(mh, ml), (mh, ml)]))
            ffn("ffn2", 4)
            norm(5)

        @block.vector
        def _(dve):
            chain = [0]

            def link(ins_):
                chain[0] = chain[0] + 1
                ins_.then_inc(dve_step, 1)
                dve.wait_ge(dve_step, chain[0])

            def low(name, k, dst, hi):
                at_ = SPLIT0[name] + k
                dve.wait_ge(high_ready, at_ + 1)
                nc.vector.tensor_tensor(dst, tmp[:, k % 2], hi.bitcast(F32), ALU.subtract).then_inc(low_ready, 1)

            def tmp_free(name, k):
                at_ = SPLIT0[name] + k
                if at_ >= 2:
                    dve.wait_ge(low_ready, at_ - 1)

            def add_square(n, m):
                at_ = n * KT + m
                dve.wait_ge(sq_ready, at_ + 1)
                if m == 0:
                    ins_ = nc.vector.tensor_copy(sumsq[:], sq[:, 0])
                else:
                    dve.wait_ge(sq_used, at_)
                    ins_ = nc.vector.tensor_tensor(sumsq[:], sumsq[:], sq[:, m % 2], ALU.add)
                ins_.then_inc(sq_used, 1)
                if m == KT - 1:
                    dve.wait_ge(sq_used, at_ + 1)
                    dve.sem_inc(sumsq_ready, 1)

            def norm(n, gain, shift=None):
                dve.wait_ge(norm_root, n + 1)
                link(nc.vector.reciprocal(norm_r[:], norm_sd[:]))
                nc.vector.tensor_tensor(diag, ident[:].unsqueeze(1).to_broadcast([P, TB, P]),
                                        norm_r[:].unsqueeze(2).to_broadcast([P, TB, P]), ALU.mult
                                        ).then_inc(diag_ready, 1)
                dve.wait_ge(norm_bc, n + 1)
                for k in range(KT):
                    name = f"norm{n}"
                    if n == 5:
                        nc.vector.scalar_tensor_tensor(out=y[:, k], in0=x[:, k], scalar=gain[:, k:k + 1],
                                                       in1=ps[:, 7], op0=ALU.mult, op1=ALU.mult
                                                       ).then_inc(y_ready, 1)
                        continue
                    tmp_free(name, k)
                    if shift is None:
                        nc.vector.scalar_tensor_tensor(out=tmp[:, k % 2], in0=x[:, k],
                                                       scalar=gain[:, k:k + 1], in1=ps[:, 7],
                                                       op0=ALU.mult, op1=ALU.mult).then_inc(tmp_ready, 1)
                    else:
                        link(nc.vector.tensor_tensor(tmp[:, k % 2], x[:, k], ps[:, 7], ALU.mult))
                        nc.vector.tensor_scalar(tmp[:, k % 2], tmp[:, k % 2], gain[:, k:k + 1],
                                                shift[:, k:k + 1], ALU.mult, ALU.add).then_inc(tmp_ready, 1)
                    if k:
                        low(name, k - 1, xl[:, k - 1], xh[:, k - 1])
                if n < 5:
                    low(f"norm{n}", KT - 1, xl[:, KT - 1], xh[:, KT - 1])

            def residual(n, unit, scale_of, whole_unit):
                for m in range(KT):
                    j, t = (m, 0) if whole_unit else (m // 2, m % 2)
                    u = j % 2
                    dve.wait_ge(tile_done, 2 * (unit + j) + (2 if whole_unit else t + 1))
                    nc.vector.scalar_tensor_tensor(out=x[:, m], in0=ps[:, 2 * u + t], scalar=scale_of(m),
                                                   in1=x[:, m], op0=ALU.mult, op1=ALU.add
                                                   ).then_inc(x_ready, 1)
                    dve.wait_ge(x_ready, (n - 1) * KT + m + 1)
                    dve.sem_inc(banks_free[u], 2 if whole_unit else 1)
                    if m:
                        add_square(n, m - 1)
                add_square(n, KT - 1)

            for u in range(2):
                dve.sem_inc(banks_free[u], 2)
            nc.vector.memset(inchunk[:], 0.0).then_inc(consts, 1)
            nc.vector.memset(inhalf[:], 0.0).then_inc(consts, 1)
            dve.wait_ge(consts, 2)
            for h in range(2):
                rows = slice(h * 64, h * 64 + 64)
                nc.vector.memset(inchunk[rows, h:h + 1], 1.0 / 16).then_inc(consts, 1)
                nc.vector.memset(inhalf[rows, h:h + 1], 1.0).then_inc(consts, 1)
            for i, value in enumerate((EPS, 64 * EPS, 1.0)):
                nc.vector.memset(eps[:, i:i + 1], value).then_inc(consts, 1)
            dve.wait_ge(pool_step, 6)
            nc.vector.memset(later[64:128, 0:64], 0.0).then_inc(consts, 1)
            dve.wait_ge(small_in, N_SMALL)
            nc.vector.tensor_tensor(qkg[:], qk_g[:, :, 0], qk_g[:, :, 1], ALU.mult).then_inc(dve_step, 1)
            nc.vector.tensor_tensor(lam_p[:], lam_in[:, :, 0:4:2], lam_in[:, :, 1:4:2], ALU.mult
                                    ).then_inc(dve_step, 1)
            dve.wait_ge(dve_step, 2)
            chain[0] = 2
            link(nc.vector.tensor_scalar(qkg[:], qkg[:], DK ** -0.5, None, ALU.mult))
            nc.vector.tensor_reduce(lam_s[:], lam_p[:], AX_X, ALU.add).then_inc(lam_ready, 1)
            for l in range(LAYERS):
                link(nc.vector.tensor_scalar(o_g[:, l, 1], o_g[:, l, 1], 1.0 - lam_init(l), None, ALU.mult))
            dve.wait_ge(c_ready, 1)
            for l in range(LAYERS):
                if l:
                    dve.wait_ge(ada_cols, l)
                for k in range(KT):
                    for half in range(2):
                        n = (l * KT + k) * 2 + half
                        cols = slice(half * 1536, half * 1536 + 1536)
                        dve.wait_ge(ada_landed[n % 4], 16 * (n // 4 + 1))
                        if k == 0:
                            ins_ = nc.vector.tensor_scalar(acc[:, cols], ada_w[n % 4][:], c_act[:, 0:1], None,
                                                           ALU.mult)
                        else:
                            dve.wait_ge(ada_used, n - 1)
                            ins_ = nc.vector.scalar_tensor_tensor(
                                out=acc[:, cols], in0=ada_w[n % 4][:], scalar=c_act[:, k:k + 1],
                                in1=acc[:, cols], op0=ALU.mult, op1=ALU.add)
                        ins_.then_inc(ada_used, 1)
                dve.wait_ge(ada_used, (l + 1) * 2 * KT)
                dve.sem_inc(ada_sum, 1)
                dve.wait_ge(ada_cols, l + 1)
                link(nc.vector.tensor_tensor(mod[:, l], ps[:, 4, 0:24], b_ada[:, l], ALU.add))
                link(nc.vector.scalar_tensor_tensor(out=mod[:, l, 8:16], in0=mod[:, l, 8:16], scalar=1.0,
                                                    in1=norm_g[:, l], op0=ALU.add, op1=ALU.mult))
            dve.wait_ge(lam_exp, 1)
            for l in range(LAYERS):
                link(nc.vector.scalar_tensor_tensor(out=neglam[:, l:l + 1], in0=lam_e[:, l, 1:2],
                                                    scalar=-lam_init(l), in1=lam_e[:, l, 0:1],
                                                    op0=ALU.add, op1=ALU.subtract))
            dve.wait_ge(consts, N_CONST)

            for m in range(KT):
                add_square(0, m)
            for l in range(LAYERS):
                unit0 = UNIT0[f"layer{l}"]
                norm(l, mod[:, l, 8:16], mod[:, l, 0:8])
                link(nc.vector.memset(wr_h[:].bitcast(F32), 0.0))
                link(nc.vector.memset(wr_l[:].bitcast(F32), 0.0))
                link(nc.vector.tensor_copy(wr_h[:, :, 0:RANK], wr_raw[:, l]))
                nc.vector.tensor_tensor(wr_l[:, :, 0:RANK], wr_raw[:, l], wr_h[:, :, 0:RANK].bitcast(F32),
                                        ALU.subtract).then_inc(lr_w, 1)
                link(nc.vector.memset(u_in[:, :, 0:CONV_K - 1], 0.0))

                def copied(stage, j, t=1):
                    unit = unit0 + PART0[stage] + j
                    dve.wait_ge(banks_free[unit % 2], emptied(unit, t))

                def head_sums(g, tb):
                    o_sq = conv[:, 2 + tb % 2]
                    link(nc.vector.tensor_tensor(o_sq, o[g][:, tb], o[g][:, tb], ALU.mult))
                    link(nc.vector.tensor_reduce(ss_o[:, tb, 4 * g:4 * g + 4],
                                                 o_sq.rearrange("p (h d) -> p h d", d=P), AX_X, ALU.add))

                def gated(g, tb):
                    link(nc.vector.tensor_tensor(o[g][:, tb], o[g][:, tb],
                                                 zg[:, tb, g * WIDTH:(g + 1) * WIDTH], ALU.mult))

                def biases(s):
                    qb, h = s // HEADS, s % HEADS
                    n = P * (qb + 1)
                    dve.wait_ge(scores, 2 * (l * STEPS + s) + 2)
                    for m in range(2):
                        ins_ = nc.vector.memset(ps[0:64, 4 + m, n - 64:n], NEG)
                        ins_.then_inc(dve_step, 1)
                        chain[0] += 1
                    dve.wait_ge(dve_step, chain[0])
                    link(nc.vector.tensor_reduce(smax[:, s % 2], ps[:, 4:6, 0:n], AX_X, ALU.max))
                    nc.vector.tensor_tensor(nbias[:, s % 2], smax[:, s % 2], nrq[:, qb, 2 * h:2 * h + 2], ALU.mult
                                            ).then_inc(bias_ready, 1)

                def combine(s):
                    n = P * (s // HEADS + 1)
                    dve.wait_ge(exp_done, 2 * (l * STEPS + s) + 2)
                    link(nc.vector.reciprocal(rz[:, s % 2], zs[:, s % 2]))
                    link(nc.vector.tensor_scalar(prob[:, s % 2, 1, 0:n], prob[:, s % 2, 1, 0:n], rz[:, s % 2, 1:2],
                                                 neglam[:, l:l + 1], ALU.mult, ALU.mult))
                    nc.vector.scalar_tensor_tensor(out=prob[:, s % 2, 0, 0:n], in0=prob[:, s % 2, 0, 0:n],
                                                   scalar=rz[:, s % 2, 0:1], in1=prob[:, s % 2, 1, 0:n],
                                                   op0=ALU.mult, op1=ALU.add).then_inc(attn_ready, 1)

                for stage, *at_ in ORDER:
                    if stage == "conv":
                        m = at_[0]
                        copied("conv", m // 2, m % 2)
                        link(nc.vector.tensor_scalar(conv[:, m], u_in[:, m, 0:S], conv_w[:, l, m, 0:1], None,
                                                     ALU.mult))
                        for j in range(1, CONV_K):
                            ins_ = nc.vector.scalar_tensor_tensor(
                                out=conv[:, m], in0=u_in[:, m, j:j + S], scalar=conv_w[:, l, m, j:j + 1],
                                in1=conv[:, m], op0=ALU.mult, op1=ALU.add)
                            if j < CONV_K - 1:
                                link(ins_)
                        ins_.then_inc(conv_done, 1)
                    elif stage == "gate":
                        dve.wait_ge(gate_mm, l + 1)
                        nc.vector.tensor_scalar(log_a[:], ps[:, 4:6].rearrange("p a (b c) -> p (a b) c", b=2),
                                                0.0, None, ALU.min).then_inc(gate_min, 1)
                        dve.wait_ge(gate_soft, l + 1)
                        nc.vector.tensor_tensor(log_a[:], log_a[:], soft[:], ALU.subtract
                                                ).then_inc(loga_ready, 1)
                    elif stage == "turn_k":
                        dve.wait_ge(gk_turned, l + 1)
                        nc.vector.tensor_tensor(decay[:], ps[:, 6:8].rearrange("p a (b c) -> p (a b) c", b=2),
                                                decay[:], ALU.mult).then_inc(gk_ready, 1)
                    elif stage == "outer":
                        c = at_[0]
                        dve.wait_ge(outer_done, l * NCH + c + 1)
                        if c:
                            dve.wait_ge(state_ready, l * NCH + c)
                        for p in range(2):
                            if c == 0:
                                ins_ = nc.vector.tensor_copy(states[:, 0, p], ps[:, 4, p * 256:p * 256 + 256])
                            else:
                                ins_ = nc.vector.scalar_tensor_tensor(
                                    out=states[:, c, p], in0=states[:, c - 1, p], scalar=aend[:, p, c:c + 1],
                                    in1=ps[:, 4 + c % 2, p * 256:p * 256 + 256], op0=ALU.mult, op1=ALU.add)
                            if p == 0:
                                link(ins_)
                        ins_.then_inc(state_ready, 1)
                    elif stage == "gla_ss":
                        dve.wait_ge(gla_copied, l * TB + at_[0] + 1)
                        head_sums(0, at_[0])
                    elif stage == "q_squares":
                        for h in range(HEADS):
                            copied("q", h // 2, h % 2)
                            nc.vector.tensor_tensor((sq, tmp)[h // 2][:, h % 2], q[:, h], q[:, h], ALU.mult
                                                    ).then_inc(q_sq, 1)
                        dve.wait_ge(q_sq, (l + 1) * HEADS)
                        link(nc.vector.tensor_scalar(q[:], q[:], qkg[:, l:l + 1], None, ALU.mult))
                    elif stage == "k_sums":
                        copied("k", 0)
                        copied("k", 1)
                        link(nc.vector.tensor_tensor(k_sq[:], k_tok[:], k_tok[:], ALU.mult))
                        link(nc.vector.tensor_reduce(ss_qk[:, 0].rearrange("p b g -> p (b g)"),
                                                     k_sq[:].rearrange("p b (g d) -> p (b g) d", d=DK),
                                                     AX_X, ALU.add))
                    elif stage == "qk_norm":
                        dve.wait_ge(q_ss, l + 1)
                        nc.vector.tensor_copy(ss_qk[:, 1].rearrange("p b g -> p (b g)"), ps[:, 5, 0:32]
                                              ).then_inc(qk_var, 1)
                        dve.wait_ge(qk_root, l + 1)
                        link(nc.vector.reciprocal(r_qk[:], r_qk[:]))
                        link(nc.vector.tensor_scalar(nrq[:], r_qk[:, 1], -1.0, None, ALU.mult))
                        keys = k_tok[:].rearrange("p b (g d) -> p (b g) d", d=DK)
                        rk = r_qk[:, 0].rearrange("p b g -> p (b g)").unsqueeze(2)
                        nc.vector.tensor_tensor(keys, keys, rk.to_broadcast([P, TB * 8, DK]), ALU.mult
                                                ).then_inc(k_normed, 1)
                    elif stage == "attn":
                        s = at_[0]
                        if s < STEPS:
                            biases(s)
                        if 1 <= s <= STEPS:
                            combine(s - 1)
                    elif stage == "diff_ss":
                        qb = at_[0]
                        dve.wait_ge(o_copied, l * STEPS + HEADS * (qb + 1))
                        head_sums(1, qb)
                    elif stage == "gains":
                        g = at_[0]
                        dve.wait_ge(z_act, 2 * l + g + 1)
                        part = zg[:, :, g * WIDTH:(g + 1) * WIDTH].rearrange("p b (h d) -> p b h d", d=P)
                        link(nc.vector.tensor_tensor(
                            part, part, o_g[:, l, g].unsqueeze(1).unsqueeze(1).to_broadcast([P, TB, HEADS, P]),
                            ALU.mult))
                        for tb in range(TB):
                            gated(g, tb)
                dve.sem_inc(o_var, 1)
                dve.wait_ge(o_root, 2 * l + 2)
                link(nc.vector.reciprocal(r_o[:], sd_o[:]))

                def mix_lows(j):
                    g, tb = j // TB, j % TB
                    dve.wait_ge(mix_high, l * 8 + j + 1)
                    hi = xh[:, 4 * g:4 * g + 4, tb * P:tb * P + P]
                    nc.vector.tensor_tensor(xl[:, 4 * g:4 * g + 4, tb * P:tb * P + P],
                                            ps[:, 4 + j % 4].rearrange("p (h c) -> p h c", h=4),
                                            hi.bitcast(F32), ALU.subtract).then_inc(mix_low, 1)

                for j in range(2 * TB):
                    g, tb = j // TB, j % TB
                    part = o[g][:, tb].rearrange("p (h d) -> p h d", d=P)
                    nc.vector.tensor_tensor(part, part,
                                            r_o[:, tb, 4 * g:4 * g + 4].unsqueeze(2).to_broadcast([P, 4, P]),
                                            ALU.mult).then_inc(o_normed, 1)
                    if j >= 2:
                        mix_lows(j - 2)
                mix_lows(6)
                mix_lows(7)
                residual(l + 1, unit0 + L_UNITS - L_OUT, lambda m: mod[:, l, 16 + m:17 + m], False)

            def ffn(name, n, gain):
                norm(n, gain)
                unit, split = UNIT0[name], SPLIT0[name]
                gate0 = 0 if name == "ffn1" else FT
                with dve.Fori(0, FT // 2) as i:
                    for u in range(2):
                        dve.wait_ge(ff_gate, i * 2 + (gate0 + u + 1))
                        dve.wait_ge(tile_done, i * 4 + (2 * unit + 2 * u + 2))
                        dve.wait_ge(low_ready, i * 2 + (split + u - 1))
                        nc.vector.tensor_tensor(tmp[:, u], ps[:, 2 * u + 1], gate[:, u], ALU.mult
                                                ).then_inc(tmp_ready, 1)
                        dve.wait_ge(tmp_ready, i * 2 + (split + u + 1))
                        dve.sem_inc(banks_free[u], 2)
                        dve.wait_ge(high_ready, i * 2 + (split + u + 1))
                        nc.vector.tensor_tensor(fl[:, bass.ds(i * 2 + u, 1)], tmp[:, u:u + 1],
                                                fh[:, bass.ds(i * 2 + u, 1)].bitcast(F32), ALU.subtract
                                                ).then_inc(low_ready, 1)
                residual(n + 1, unit + FT, lambda m: 0.5, True)

            ffn("ffn1", 2, gains[:, 0])

            norm(3, gains[:, 1])
            unit = UNIT0["mixer"]
            nc.vector.memset(tpad[:], 0.0).then_inc(dve_step, 1)
            chain[0] += 1
            dve.wait_ge(dve_step, chain[0])
            dve.sem_inc(m_prod, 2)
            for u in range(2):
                dve.wait_ge(banks_free[u], emptied(unit + 3, 1))
            for tb in range(TB):
                link(nc.vector.tensor_tensor(v2_sq[:], v2[:, tb], v2[:, tb], ALU.mult))
                link(nc.vector.tensor_reduce(ss_v[:, 0, tb:tb + 1], v2_sq[:], AX_X, ALU.add))
            dve.sem_inc(m_root_in, 1)
            dve.wait_ge(m_root, 1)
            link(nc.vector.reciprocal(ss_v[:, 2], ss_v[:, 1]))
            for tb in range(TB):
                link(nc.vector.tensor_scalar(v2[:, tb], v2[:, tb], ss_v[:, 2, tb:tb + 1], None, ALU.mult))
            dve.sem_inc(m_vn, 1)
            unit += M_V + M_U
            for j in range(M_CX):
                u = j % 2
                dve.wait_ge(m_gc, j + 1)
                dve.wait_ge(tile_done, 2 * (unit + j) + 2)
                link(nc.vector.tensor_tensor(tpad[:, u, 1:S + 1], ps[:, 2 * u + 1], gc[:, u], ALU.mult))
                dve.sem_inc(banks_free[u], 2)
                dve.sem_inc(m_prod, 1)
                link(nc.vector.tensor_scalar(cv[:, j], tpad[:, u, 0:S], conv2_w[:, j, 0:1], None, ALU.mult))
                for tap in (1, 2):
                    link(nc.vector.scalar_tensor_tensor(out=cv[:, j], in0=tpad[:, u, tap:tap + S],
                                                        scalar=conv2_w[:, j, tap:tap + 1], in1=cv[:, j],
                                                        op0=ALU.mult, op1=ALU.add))
            unit += M_CX
            dve.wait_ge(sgu_in, 32)
            for h in range(KT):
                dve.wait_ge(sgu_mm, h + 1)
                tmp_free("sgu", h)
                link(nc.vector.scalar_tensor_tensor(
                    out=tmp[:, h % 2].rearrange("p (c q) -> p c q", c=TB),
                    in0=ps[:, 4 + h % 2].rearrange("p (c q) -> p c q", c=TB), scalar=sgu_g[:, h:h + 1],
                    in1=bs[:, h].unsqueeze(1).to_broadcast([P, TB, P]), op0=ALU.mult, op1=ALU.add))
                dve.sem_inc(sgu_free, 1)
                nc.vector.tensor_tensor(tmp[:, h % 2], tmp[:, h % 2], u2[:, h], ALU.mult).then_inc(tmp_ready, 1)
                if h:
                    low("sgu", h - 1, al[:, h - 1], ah[:, h - 1])
            low("sgu", KT - 1, al[:, KT - 1], ah[:, KT - 1])
            for m in range(KT):
                u, t = m // 2 % 2, m % 2
                dve.wait_ge(tile_done, 2 * (unit + m // 2) + t + 1)
                tmp_free("gb", m)
                nc.vector.tensor_tensor(tmp[:, m % 2], ps[:, 2 * u + t], cv[:, m], ALU.mult
                                        ).then_inc(tmp_ready, 1)
                dve.wait_ge(tmp_ready, SPLIT0["gb"] + m + 1)
                dve.sem_inc(banks_free[u], 1)
                low("gb", m, bl[:, m], bh[:, m])
            unit += M_GB
            for j in range(KT):
                dve.wait_ge(m_sig, 2 * j + 2)
                dve.wait_ge(tile_done, 2 * unit + 4 * j + 4)
                tmp_free("merge", j)
                for t in range(2):
                    link(nc.vector.tensor_tensor(gc[:, t], ps[:, 2 + t], gc[:, t], ALU.mult))
                dve.sem_inc(banks_free[1], 2)
                nc.vector.tensor_tensor(tmp[:, j % 2], gc[:, 0], gc[:, 1], ALU.add).then_inc(tmp_ready, 1)
                dve.wait_ge(tmp_ready, SPLIT0["merge"] + j + 1)
                dve.sem_inc(m_sig_used, 2)
                low("merge", j, ml[:, j], mh[:, j])
            unit += M_MERGE
            residual(4, unit, lambda m: 1.0, False)
            ffn("ffn2", 4, gains[:, 2])
            norm(5, gains[:, 3])


def _tiles(w):
    return w.reshape(-1, P, w.shape[-1]).transpose(1, 0, 2)


def _feature_chunks(a, b):
    n = a.shape[1] // P
    both = np.stack([_tiles(a).reshape(P, KT, n, P), _tiles(b).reshape(P, KT, n, P)])
    return both.transpose(3, 1, 0, 2, 4).reshape(n, P, CW)


def _pair_chunks(w):
    n = w.shape[1] // P
    t = _tiles(w).reshape(P, KT, n // 2, 2, P)
    return t.transpose(2, 0, 3, 1, 4).reshape(n // 2, P, CW)


def _token_chunks(w):
    n = w.shape[1] // 256
    return _tiles(w).reshape(P, KT, n, 256).transpose(2, 0, 1, 3).reshape(n, P, CW)


def _half_chunks(w):
    t = w.reshape(2, FH, P, KT, P)
    return t.transpose(3, 0, 2, 1, 4).reshape(2 * KT, P, FW)


def _columns(a):
    a = a.reshape(*a.shape[:-1], -1, P)
    return np.moveaxis(a, -1, 0)


def kernel(x, c, w_ada, b_ada, norm_g, w_in, conv_w, w_gk, b_gk, gla_norm_g, qn_g, kn_g, lam_q1, lam_k1,
           lam_q2, lam_k2, diff_norm_g, w_out, ffn1_norm_2, ffn1_w_in_2, ffn1_w_out_2, mix_norm_2, w_in_2,
           sgu_norm_2, sgu_w_2, sgu_b_2, conv_w_2, w_proj_a_2, w_proj_b_2, w_out_2, ffn2_norm_2,
           ffn2_w_in_2, ffn2_w_out_2, final_norm_2):
    import concourse.bacc as bacc
    from concourse.bass_utils import run_bass_kernel_spmd

    arrays = {
        "x_t": _tiles(x[0].T),
        "c_col": _columns(c[0]),
        "b_ada": _columns(b_ada),
        "norm_g": _columns(norm_g),
        "gains": _columns(np.stack([ffn1_norm_2[0], mix_norm_2[0], ffn2_norm_2[0], final_norm_2])),
        "conv_w": _columns(conv_w).transpose(0, 1, 3, 2),
        "conv2_w": _columns(conv_w_2[0]).transpose(0, 2, 1),
        "sgu_g": _columns(sgu_norm_2[0]),
        "qk_g": np.stack([np.concatenate([qn_g, qn_g], 1).T, np.concatenate([kn_g, kn_g], 1).T], 2),
        "lam": np.stack([lam_q1, lam_k1, lam_q2, lam_k2], 1).reshape(1, -1),
        "o_g": np.stack([gla_norm_g, diff_norm_g], 1).reshape(1, -1),
        "w_gk": w_gk.transpose(1, 0, 2),
        "b_gk": b_gk,
        "w_ada": w_ada.reshape(LAYERS, KT, P, 3 * D),
        "sgu_w_t": sgu_w_2[0].transpose(2, 0, 1),
        "sgu_b": sgu_b_2[0].reshape(1, -1),
    }
    at, cols = 0, {}
    for name, n in (("gq", 256), ("gk", 256), ("gv", 512), ("lr", RANK), ("gz", 512), ("dq", 512),
                    ("dk", 512), ("dv", 512), ("dz", 512)):
        cols[name] = slice(at, at + n)
        at += n
    arrays["w_lr"] = np.stack([_tiles(w_in[l][:, cols["lr"]]) for l in range(LAYERS)], 1)
    for l in range(LAYERS):
        w = w_in[l]
        arrays[f"layer{l}_stream"] = np.concatenate([
            _pair_chunks(w[:, 0:1024]), _pair_chunks(w[:, cols["dq"]]), _token_chunks(w[:, cols["dk"]]),
            _token_chunks(w[:, cols["dv"]]), _token_chunks(w[:, cols["gz"]]), _token_chunks(w[:, cols["dz"]]),
            _pair_chunks(w_out[l])])
    for name, win, wout in (("ffn1", ffn1_w_in_2[0], ffn1_w_out_2[0]), ("ffn2", ffn2_w_in_2[0], ffn2_w_out_2[0])):
        arrays[name + "_in_stream"] = _feature_chunks(win[:, :D_FF], win[:, D_FF:])
        arrays[name + "_out_stream"] = _half_chunks(wout)
    u, v, gate_b, gate_c, xb, g_a, g_b = np.split(w_in_2[0], 7, axis=1)
    gates, projections = _feature_chunks(g_a, g_b), _feature_chunks(w_proj_a_2[0], w_proj_b_2[0])
    arrays["mixer_stream"] = np.concatenate([
        _token_chunks(v), _pair_chunks(u), _feature_chunks(gate_c, xb), _pair_chunks(gate_b),
        np.stack([gates, projections], 1).reshape(2 * KT, P, CW), _pair_chunks(w_out_2[0])])

    nc = bacc.Bacc("TRN2", target_bir_lowering=False, num_devices=1, dynamic_dma_scratch_size=1024)
    arrays = {name: np.ascontiguousarray(a) for name, a in arrays.items()}
    ins = {name: nc.dram_tensor(name, a.shape, F32, kind="ExternalInput").ap() for name, a in arrays.items()}
    out = nc.dram_tensor("y_t", (P, KT, S), F32, kind="ExternalOutput").ap()
    build(nc, ins, out)
    r = run_bass_kernel_spmd(nc, [arrays], core_ids=[0])
    return r.results[0]["y_t"].transpose(2, 1, 0).reshape(1, S, D)
```

```python
import math
from contextlib import ExitStack

import numpy as np

import concourse.bass as bass
import concourse.mybir as mybir

F32 = mybir.dt.float32
F32R = mybir.dt.float32r
ALU = mybir.AluOpType
ACT = mybir.ActivationFunctionType
AX_X = mybir.AxisListType.X

P = 128
D = 1024
S = 512
KT = D // P
TB = S // P
EPS = 1e-6
LAYERS = 2
CHUNK = 64
NCH = S // CHUNK
HEADS = 4
DK = 64
RANK = 16
CONV_K = 4
GLA_QK = 256
WIDTH = 512
D_FF = 2816
FT = D_FF // P
FH = FT // 2
CW = 16 * P
FW = FH * P
NEG = -1.0e30

L_CONV, L_Q, L_K, L_V, L_Z, L_OUT = 4, 2, 2, 2, 4, 4
L_UNITS = L_Q + L_K + L_V + L_CONV + L_Z + L_OUT
M_V, M_U, M_CX, M_GB, M_MERGE, M_OUT = 4, 4, 8, 4, 16, 4
M_UNITS = M_V + M_U + M_CX + M_GB + M_MERGE + M_OUT
FFN_UNITS = FT + KT
FFN_CHUNKS = FT + 2 * KT
UNIT0 = {"layer0": 0, "layer1": L_UNITS, "ffn1": 2 * L_UNITS}
UNIT0["mixer"] = UNIT0["ffn1"] + FFN_UNITS
UNIT0["ffn2"] = UNIT0["mixer"] + M_UNITS
CHUNK0 = {"layer0": 0, "layer1": L_UNITS, "ffn1": 2 * L_UNITS}
CHUNK0["mixer"] = CHUNK0["ffn1"] + FFN_CHUNKS
CHUNK0["ffn2"] = CHUNK0["mixer"] + M_UNITS
STEPS = HEADS * TB


ADA_LATE_PIECES = [(0, k, 2 * D, 0) for k in range(KT)] + \
                  [(1, k, part * D, (1 + part) * D) for k in range(KT) for part in range(3)]
ADA_LATE = len(ADA_LATE_PIECES)
ADA_PE = 2


def layer_order():
    parts = [("part", stage, j, p) for stage, n in
             (("conv", L_CONV), ("q", L_Q), ("k", L_K), ("v", L_V), ("z", L_Z))
             for j in range(n) for p in range(4)]
    after = {}

    def put(n, *stage):
        after.setdefault(n, []).append(stage)

    put(3, "lr")
    put(6, "gate")
    put(10, "decay")
    for m in range(KT):
        put(2 * m + 2, "conv", m)
    put(14, "conv_act", range(0, 4))
    put(19, "conv_act", range(4, KT))
    put(21, "turn_k")
    for tb in range(TB):
        put(21 + tb, "turn_v", tb)
    for c in range(NCH):
        put(25 + c, "outer", c)
    for tb in range(TB):
        put(27 + 2 * tb, "read_out", tb)
        put(28 + 2 * tb, "gla_ss", tb)
    put(32, "q_squares")
    put(33, "k_sums")
    put(34, "q_sums")
    put(34, "qk_norm")
    put(36, "turn_keys")
    for s in range(STEPS + 2):
        put(38 + s, "attn", s)
        if s >= 5 and s % 4 == 1:
            put(min(39 + s, 55), "diff_ss", (s - 5) // 4)
        if s == 11:
            put(49, "z_act", 0)
        if 12 <= s < 12 + TB:
            put(38 + s, "gated", 0, s - 12)
    put(55, "mix_gla")
    put(55, "z_act", 1)
    for tb in range(TB):
        put(55, "gated", 1, tb)
    order = []
    for n, part in enumerate(parts):
        order.append(part)
        order += [("ada", piece) for piece in range(ADA_LATE)
                  if n == 4 + (piece if piece < 7 else 7 + (piece - 7) * 2 // 3)]
        order += after.get(n, [])
    return order


ORDER = layer_order()
PART0 = {"conv": 0, "q": L_CONV, "k": L_CONV + L_Q, "v": L_CONV + L_Q + L_K,
         "z": L_CONV + L_Q + L_K + L_V}


def emptied(unit, t):
    return 2 * (unit // 2) + 3 + t


def lam_init(l):
    return 0.8 - 0.6 * math.exp(-0.3 * l)


def build(nc, ins, out):
    ctx = ExitStack()
    with ctx:
        def sem(name):
            return ctx.enter_context(nc.semaphore(name))

        base = nc.sbuf_base
        top = nc.sbuf_usable_end
        base = (base + 63) // 64 * 64
        cursor = [base]

        def at(name, shape, dt, offset):
            n = 4 * int(np.prod(shape[1:]))
            assert offset + n <= top, (name, offset + n, top)
            return nc.alloc_sbuf_tensor_at(name, shape, dt, offset=offset, align_bytes=4)

        def sb(name, shape, dt=F32):
            n = (4 * int(np.prod(shape[1:])) + 31) // 32 * 32
            t = at(name, shape, dt, cursor[0])
            cursor[0] += n
            return t

        ps = ctx.enter_context(nc.psum_tensor("ps", [P, 8, 512], F32))

        x = sb("x", [P, KT, S])
        xh = sb("xh", [P, KT, S], F32R)
        xl = sb("xl", [P, KT, S], F32R)
        raw = [sb(f"raw{u}", [P, CW]) for u in range(2)]
        wh = [sb(f"wh{u}", [P, CW], F32R) for u in range(2)]
        wl = [sb(f"wl{u}", [P, CW], F32R) for u in range(2)]
        ones = sb("ones", [P, P])
        ident = sb("ident", [P, P])
        later = sb("later", [P, P])
        inchunk = sb("inchunk", [P, 2])
        inhalf = sb("inhalf", [P, 2])
        eps = sb("eps", [P, 3])
        sumsq = sb("sumsq", [P, S])
        sq = sb("sq", [P, 2, S])
        tmp = sb("tmp", [P, 2, S])
        diag = sq[:, 1].rearrange("p (b c) -> p b c", b=TB)
        norm_sd = sb("norm_sd", [P, TB])
        norm_r = sb("norm_r", [P, TB])
        mod = sb("mod", [P, LAYERS, 24])
        b_ada = sb("b_ada", [P, LAYERS, 24])
        norm_g = sb("norm_g", [P, LAYERS, KT])
        gains = sb("gains", [P, 4, KT])
        c_col = sb("c_col", [P, KT])
        c_act = sb("c_act", [P, KT])
        conv_w = sb("conv_w", [P, LAYERS, KT, CONV_K])
        conv2_w = sb("conv2_w", [P, KT, 3])
        sgu_g = sb("sgu_g", [P, KT])
        qk_g = sb("qk_g", [P, LAYERS, 2])
        qkg = sb("qkg", [P, LAYERS])
        lam_in = sb("lam_in", [P, LAYERS, 4, DK])
        lam_p = sb("lam_p", [P, LAYERS, 2, DK])
        lam_s = sb("lam_s", [P, LAYERS, 2])
        lam_e = sb("lam_e", [P, LAYERS, 2])
        neglam = sb("neglam", [P, LAYERS])
        o_g = sb("o_g", [P, LAYERS, 2, P])
        wgk = sb("wgk", [RANK + 1, LAYERS, GLA_QK])
        glr = sb("glr", [32, S])
        wr_raw = sb("wr_raw", [P, LAYERS, KT, RANK])
        arena = cursor[0]

        def place(name, shape, dt=F32):
            n = (4 * int(np.prod(shape[1:])) + 31) // 32 * 32
            t = at(name, shape, dt, cursor[0])
            cursor[0] += n
            return t

        acc = place("ada_acc", [P, 2 * D])
        ada_w = [place(f"ada_w{k}", [P, 2 * D]) for k in range(KT)]

        cursor[0] = arena
        u_in = place("u_in", [P, KT, S + CONV_K - 1])
        at_conv = cursor[0]
        conv = place("conv", [P, KT, S])
        q = place("q", [P, HEADS, S])
        k_tok = place("k_tok", [P, TB, WIDTH])
        at_kf = cursor[0]
        kf = place("kf", [P, HEADS, S])
        at_v = cursor[0]
        v = place("v", [P, TB, WIDTH])
        at_zg = cursor[0]
        zg = place("zg", [P, TB, 2 * WIDTH])
        at_p = cursor[0]
        prob = place("prob", [P, 2, 2, S])
        attn_t = place("attn_t", [P, 2, S])
        at_od = cursor[0]
        o_diff = place("o_diff", [P, TB, WIDTH])
        ss_qk = place("ss_qk", [P, 2, TB, 8])
        r_qk = place("r_qk", [P, 2, TB, 8])
        nrq = place("nrq", [P, TB, 8])
        smax = place("smax", [P, 2, 2])
        nbias = place("nbias", [P, 2, 2])
        zs = place("zs", [P, 2, 2])
        rz = place("rz", [P, 2, 2])
        ss_o = place("ss_o", [P, 2, TB, HEADS])
        sd_o = place("sd_o", [P, 2, TB, HEADS])
        r_o = place("r_o", [P, 2, TB, HEADS])
        aend = place("aend", [P, 2, NCH])
        k_sq = at("k_sq", [P, TB, WIDTH], F32, at_od)
        states = at("states", [P, NCH, 2, 256], F32, arena)
        log_a = at("log_a", [P, TB, 256], F32, at_kf)
        decay = at("decay", [P, TB, 256], F32, at_kf + 4096)
        gv = at("gv", [P, TB, WIDTH], F32, at_p)
        soft = at("soft", [P, TB, 256], F32, at_p + 8192)
        wr_h = at("wr_h", [P, KT, P], F32R, at_p)
        wr_l = at("wr_l", [P, KT, P], F32R, at_p + 4096)
        o_gla = at("o_gla", [P, TB, WIDTH], F32, at_conv + 4 * S * 4)
        o = (o_gla, o_diff)
        acc_late = at("acc_late", [P, 4 * D], F32, at_zg)
        ada_late = [at(f"ada_late{n}", [P, D], F32, (at_od, at_od + 4 * D, at_v, at_v + 4 * D)[n])
                    for n in range(4)]

        cursor[0] = arena
        fh = place("fh", [P, FT, S], F32R)
        fl = place("fl", [P, FT, S], F32R)
        gate = place("gate", [P, 2, S])

        cursor[0] = arena
        at_v2 = cursor[0]
        v2 = place("v2", [P, TB, D])
        u2 = place("u2", [P, KT, S])
        bh = at("bh", [P, KT, S], F32R, at_v2)
        bl = at("bl", [P, KT, S], F32R, at_v2 + KT * S * 4)
        ah = place("ah", [P, KT, S], F32R)
        al = place("al", [P, KT, S], F32R)
        at_m = cursor[0]
        cv = place("cv", [P, KT, S])
        mh = at("mh", [P, KT, S], F32R, at_m)
        at_ml = cursor[0]
        ml = place("ml", [P, KT, S], F32R)
        ws_t = at("ws_t", [P, KT, P], F32, at_ml)
        bs = at("bs", [P, KT, P], F32, at_ml + 4096)
        v2_sq = at("v2_sq", [P, D], F32, at_ml + 8192)
        ss_v = at("ss_v", [P, 3, TB], F32, at_ml + 12288)
        gc = place("gc", [P, 2, S])
        tpad = place("tpad", [P, 2, S + 2])

        y = at("y", [P, KT, S], F32, arena)

        raw_landed = [sem(f"raw_landed{u}") for u in range(2)]
        w_high = sem("w_high")
        w_ready = sem("w_ready")
        half_used = sem("half_used")
        tile_done = sem("tile_done")
        banks_free = [sem(f"banks_free{u}") for u in range(2)]
        small_in = sem("small_in")
        x_in = sem("x_in")
        c_in = sem("c_in")
        ada_landed = [sem(f"ada_landed{k}") for k in range(KT)]
        late_landed = [sem(f"late_landed{n}") for n in range(4)]
        late_used = sem("late_used")
        ada_used = sem("ada_used")
        consts = sem("consts")
        dve_step = sem("dve_step")
        act_step = sem("act_step")
        pool_step = sem("pool_step")
        c_ready = sem("c_ready")
        ada_sum = sem("ada_sum")
        ada_cols = sem("ada_cols")
        ada_read = sem("ada_read")
        lam_ready = sem("lam_ready")
        lam_exp = sem("lam_exp")
        x_ready = sem("x_ready")
        sq_ready = sem("sq_ready")
        sq_used = sem("sq_used")
        sumsq_ready = sem("sumsq_ready")
        norm_ss = sem("norm_ss")
        norm_root = sem("norm_root")
        diag_ready = sem("diag_ready")
        norm_bc = sem("norm_bc")
        tmp_ready = sem("tmp_ready")
        high_ready = sem("high_ready")
        low_ready = sem("low_ready")
        lr_w = sem("lr_w")
        glr_done = sem("glr_done")
        glr_copied = sem("glr_copied")
        conv_done = sem("conv_done")
        conv_act = sem("conv_act")
        q_sq = sem("q_sq")
        q_ss = sem("q_ss")
        qk_var = sem("qk_var")
        qk_root = sem("qk_root")
        k_normed = sem("k_normed")
        k_turned = sem("k_turned")
        kf_ready = sem("kf_ready")
        scores = sem("scores")
        bias_ready = sem("bias_ready")
        exp_done = sem("exp_done")
        attn_ready = sem("attn_ready")
        attn_turned = sem("attn_turned")
        at_copied = sem("at_copied")
        pv_done = sem("pv_done")
        o_copied = sem("o_copied")
        gate_mm = sem("gate_mm")
        gate_min = sem("gate_min")
        gate_soft = sem("gate_soft")
        loga_ready = sem("loga_ready")
        decay_mm = sem("decay_mm")
        decay_exp = sem("decay_exp")
        gk_turned = sem("gk_turned")
        gk_ready = sem("gk_ready")
        gv_turned = sem("gv_turned")
        gv_ready = sem("gv_ready")
        outer_done = sem("outer_done")
        state_ready = sem("state_ready")
        gla_o = sem("gla_o")
        gla_copied = sem("gla_copied")
        o_var = sem("o_var")
        o_root = sem("o_root")
        o_normed = sem("o_normed")
        o_turned = sem("o_turned")
        mix_high = sem("mix_high")
        mix_low = sem("mix_low")
        z_act = sem("z_act")
        ff_gate = sem("ff_gate")
        m_root_in = sem("m_root_in")
        m_root = sem("m_root")
        m_vn = sem("m_vn")
        m_gc = sem("m_gc")
        m_prod = sem("m_prod")
        sgu_in = sem("sgu_in")
        sgu_mm = sem("sgu_mm")
        sgu_free = sem("sgu_free")
        m_sig = sem("m_sig")
        m_sig_used = sem("m_sig_used")
        y_ready = sem("y_ready")
        y_out = sem("y_out")

        SPLIT0 = {}
        n = 0
        for name, count in (("norm0", 8), ("norm1", 8), ("norm2", 8), ("ffn1", FT), ("norm3", 8),
                            ("sgu", 8), ("gb", 8), ("merge", 8), ("norm4", 8), ("ffn2", FT)):
            SPLIT0[name] = n
            n += count

        block = ctx.enter_context(nc.Block())

        segments = []
        for l in range(LAYERS):
            segments += [(ins[f"layer{l}_stream"], L_UNITS, CW)]
        segments += [(ins["ffn1_in_stream"], FT, CW), (ins["ffn1_out_stream"], 2 * KT, FW),
                     (ins["mixer_stream"], M_UNITS, CW),
                     (ins["ffn2_in_stream"], FT, CW), (ins["ffn2_out_stream"], 2 * KT, FW)]
        CHUNKS = sum(count for _, count, _ in segments)

        small = [
            (b_ada, ins["b_ada"]), (norm_g, ins["norm_g"]), (gains, ins["gains"]),
            (conv_w, ins["conv_w"]), (conv2_w, ins["conv2_w"]), (sgu_g, ins["sgu_g"]), (qk_g, ins["qk_g"]),
            (wr_raw, ins["w_lr"]),
        ]
        N_SMALL = 16 * (len(small) + 3 + LAYERS)

        @block.sync
        def _(sp):
            sp.dma_start(x[:], ins["x_t"]).then_inc(x_in, 16)

            def load_pair(dram, size, i, chunk):
                for u in range(2):
                    if not (isinstance(i, int) and chunk == 0):
                        sp.wait_ge(w_ready, i * 2 + (chunk + u - 1))
                    sp.dma_start(raw[u][:, 0:size], dram[i * 2 + u]).then_inc(raw_landed[u], 16)

            chunk = 0
            for dram, count, size in segments:
                if chunk == 0:
                    sp.wait_ge(ada_landed[4], 16)
                    load_pair(dram, size, 0, 0)
                    with sp.Fori(0, count // 2 - 1) as i:
                        load_pair(dram[2:], size, i, 2)
                else:
                    with sp.Fori(0, count // 2) as i:
                        load_pair(dram, size, i, chunk)
                chunk += count
            for k in range(KT):
                sp.wait_ge(y_ready, k + 1)
                sp.dma_start(out[:, k], y[:, k]).then_inc(y_out, 16)
            sp.wait_ge(y_out, 16 * KT)

        @block.gpsimd
        def _(pool):
            nc.gpsimd.memset(ones[:], 1.0).then_inc(pool_step, 1)
            nc.gpsimd.memset(ident[:], 0.0).then_inc(pool_step, 1)
            nc.gpsimd.memset(later[:], 1.0 / 16).then_inc(pool_step, 1)
            nc.gpsimd.memset(glr[:], 1.0).then_inc(pool_step, 1)
            pool.wait_ge(pool_step, 4)
            nc.gpsimd.affine_select(out=ident[:], in_=ident[:], compare_op=ALU.not_equal, fill=1.0, base=0,
                                    pattern=[[-1, P]], channel_multiplier=1).then_inc(pool_step, 1)
            nc.gpsimd.affine_select(out=later[:], in_=later[:], compare_op=ALU.is_gt, fill=0.0, base=0,
                                    pattern=[[-1, P]], channel_multiplier=1).then_inc(pool_step, 1)
            def split(size, i, chunk, u):
                pool.wait_ge(w_high, i * 2 + (chunk + u + 1))
                nc.gpsimd.tensor_tensor(wl[u][:, 0:size], raw[u][:, 0:size], wh[u][:, 0:size].bitcast(F32),
                                        ALU.subtract).then_inc(w_ready, 1)

            chunk = 0
            for _, count, size in segments:
                with pool.Fori(0, count // 2) as i:
                    for u in range(2):
                        split(size, i, chunk, u)
                chunk += count

        N_CONST = 10

        @block.scalar
        def _(act):
            act.dma_start(c_col[:], ins["c_col"]).then_inc(c_in, 16)
            for k in range(KT):
                act.dma_start(ada_w[k][:], ins["w_ada"][0, k, :, 0:2 * D]).then_inc(ada_landed[k], 16)
            for dst, src in small:
                act.dma_start(dst[:], src).then_inc(small_in, 16)
            act.dma_start(lam_in[:], ins["lam"].to_broadcast([P, LAYERS * 4 * DK])
                          .rearrange("p (l a d) -> p l a d", l=LAYERS, a=4)).then_inc(small_in, 16)
            act.dma_start(o_g[:], ins["o_g"].to_broadcast([P, LAYERS * 2 * P])
                          .rearrange("p (l a d) -> p l a d", l=LAYERS, a=2)).then_inc(small_in, 16)
            act.dma_start(wgk[0:RANK], ins["w_gk"]).then_inc(small_in, 16)
            for l in range(LAYERS):
                act.dma_start(wgk[RANK:RANK + 1, l], ins["b_gk"][l:l + 1]).then_inc(small_in, 16)
            chain = [0]

            def link(ins_):
                chain[0] += 1
                ins_.then_inc(act_step, 1)
                act.wait_ge(act_step, chain[0])

            def take_high(chunk, i=0):
                if isinstance(i, int) and chunk >= CHUNKS:
                    return
                u = chunk % 2
                act.wait_ge(raw_landed[u], i * 16 + (16 * (chunk // 2) + 16))
                nc.scalar.activation(wh[u][:], raw[u][:], ACT.Copy).then_inc(w_high, 1)

            act.wait_ge(c_in, 16)
            nc.scalar.activation(c_act[:], c_col[:], ACT.Silu).then_inc(c_ready, 1)

            def late_load(n):
                if n >= ADA_LATE:
                    return
                la, k, col, _ = ADA_LATE_PIECES[n]
                if n >= 4:
                    act.wait_ge(late_used, n - 3)
                act.dma_start(ada_late[n % 4][:], ins["w_ada"][la, k, :, col:col + D]
                              ).then_inc(late_landed[n % 4], 16)

            def squares(n, ms=range(KT)):
                for m in ms:
                    at_ = n * KT + m
                    if n == 0:
                        act.wait_ge(x_in, 16)
                    else:
                        act.wait_ge(x_ready, at_ - KT + 1)
                    if at_ >= 2:
                        act.wait_ge(sq_used, at_ - 1)
                    nc.scalar.activation(sq[:, m % 2], x[:, m], ACT.Square).then_inc(sq_ready, 1)

            def output_squares(n, unit, chunk, count):
                for j in range(count):
                    squares(n, (2 * j,))
                    if j == count - 1:
                        squares(n, (2 * j + 1,))
                    act.wait_ge(tile_done, 2 * (unit + j + 1))
                    if j < count - 1:
                        take_high(chunk + j + 2)
                        squares(n, (2 * j + 1,))

            def norm(n, splits=True):
                act.wait_ge(norm_ss, n + 1)
                nc.scalar.activation(norm_sd[:], ps[:, 6, 0:TB], ACT.Sqrt, bias=eps[:, 0:1],
                                     scale=1.0 / D).then_inc(norm_root, 1)
                first = (0, CHUNK0["layer1"], CHUNK0["ffn1"], CHUNK0["mixer"], CHUNK0["ffn2"], CHUNKS)[n]
                if n == 0:
                    take_high(first)
                take_high(first + 1)
                if n == 0:
                    act.wait_ge(lam_ready, 1)
                    nc.scalar.activation(lam_e[:], lam_s[:], ACT.Exp).then_inc(lam_exp, 1)
                if splits:
                    for k in range(KT):
                        high(f"norm{n}", k, xh[:, k])

            def high(name, k, dst):
                at_ = SPLIT0[name] + k
                act.wait_ge(tmp_ready, at_ + 1)
                nc.scalar.activation(dst, tmp[:, k % 2], ACT.Copy).then_inc(high_ready, 1)

            act.wait_ge(consts, N_CONST)
            squares(0)
            for l in range(LAYERS):
                unit0 = UNIT0[f"layer{l}"]
                norm(l)

                def empty(stage, j, t):
                    unit = unit0 + PART0[stage] + j
                    u = unit % 2
                    act.wait_ge(tile_done, 2 * unit + t + 1)
                    if t:
                        take_high(unit + 2)
                    bank = ps[:, 2 * u + t]
                    if stage == "conv":
                        dst = u_in[:, 2 * j + t, CONV_K - 1:]
                    elif stage == "q":
                        dst = q[:, 2 * j + t]
                    else:
                        dst = {"k": k_tok, "v": v, "z": zg}[stage][:, 2 * t:2 * t + 2, 256 * j:256 * j + 256]
                        bank = bank.rearrange("p (b c) -> p b c", b=2)
                    nc.scalar.activation(dst, bank, ACT.Copy).then_inc(banks_free[u], 1)

                def mix_highs(j):
                    g, tb = j // TB, j % TB
                    act.wait_ge(o_turned, l * 8 + j + 1)
                    nc.scalar.activation(xh[:, 4 * g:4 * g + 4, tb * P:tb * P + P],
                                         ps[:, 4 + j % 4].rearrange("p (h c) -> p h c", h=4),
                                         ACT.Copy).then_inc(mix_high, 1)

                def exps(s):
                    qb, h = s // HEADS, s % HEADS
                    n = P * (qb + 1)
                    if s >= 2:
                        act.wait_ge(attn_turned, l * STEPS + s - 1)
                    act.wait_ge(bias_ready, l * STEPS + s + 1)
                    for m in range(2):
                        nc.scalar.activation(prob[:, s % 2, m, 0:n], ps[:, 4 + m, 0:n], ACT.Exp,
                                             bias=nbias[:, s % 2, m:m + 1],
                                             scale=r_qk[:, 1, qb, 2 * h + m:2 * h + m + 1],
                                             accum_out=zs[:, s % 2, m:m + 1]).then_inc(exp_done, 1)

                def copy_turned(s):
                    n = P * (s // HEADS + 1)
                    act.wait_ge(attn_turned, l * STEPS + s + 1)
                    if s >= 2:
                        act.wait_ge(pv_done, l * STEPS + s - 1)
                    nc.scalar.activation(attn_t[:, s % 2, 0:n], ps[:, 6, 0:n], ACT.Copy
                                         ).then_inc(at_copied, 1)

                def copy_o(s):
                    qb, h = s // HEADS, s % HEADS
                    act.wait_ge(pv_done, l * STEPS + s + 1)
                    nc.scalar.activation(o_diff[:, qb, h * P:h * P + P], ps[:, 7, 0:P],
                                         ACT.Copy).then_inc(o_copied, 1)

                for stage, *at_ in ORDER:
                    if stage == "part":
                        if at_[2] % 2:
                            empty(at_[0], at_[1], at_[2] // 2)
                    elif stage == "lr":
                        act.wait_ge(glr_done, l + 1)
                        nc.scalar.activation(glr[0:RANK], ps[0:RANK, 4], ACT.Copy).then_inc(glr_copied, 1)
                        if l == 0:
                            for n in range(3):
                                late_load(n)
                    elif stage == "ada":
                        if l == 0:
                            late_load(at_[0] + 3)
                    elif stage == "conv_act":
                        for m in at_[0]:
                            act.wait_ge(conv_done, l * KT + m + 1)
                            nc.scalar.activation(conv[:, m], conv[:, m], ACT.Silu).then_inc(conv_act, 1)
                    elif stage == "gate":
                        act.wait_ge(gate_min, l + 1)
                        link(nc.scalar.activation(soft[:], ps[:, 4:6].rearrange("p a (b c) -> p (a b) c", b=2),
                                                  ACT.Abs))
                        link(nc.scalar.activation(soft[:], soft[:], ACT.Exp, scale=-1.0))
                        nc.scalar.activation(soft[:], soft[:], ACT.Ln, bias=eps[:, 2:3]).then_inc(gate_soft, 1)
                    elif stage == "decay":
                        act.wait_ge(decay_mm, 2 * l + 1)
                        nc.scalar.activation(decay[:], ps[:, 6:8].rearrange("p a (b c) -> p (a b) c", b=2),
                                             ACT.Exp).then_inc(decay_exp, 1)
                        act.wait_ge(decay_mm, 2 * l + 2)
                        nc.scalar.activation(aend[:], ps[:, 4, 0:16].rearrange("p (a c) -> p a c", a=2),
                                             ACT.Exp).then_inc(decay_exp, 1)
                    elif stage == "turn_v":
                        tb = at_[0]
                        act.wait_ge(gv_turned, l * TB + tb + 1)
                        nc.scalar.activation(gv[:, tb], ps[:, 4 + tb % 2], ACT.Copy).then_inc(gv_ready, 1)
                    elif stage == "read_out":
                        tb = at_[0]
                        act.wait_ge(gla_o, l * TB + tb + 1)
                        nc.scalar.activation(o_gla[:, tb].rearrange("p (a b c) -> p a b c", a=2, b=2),
                                             ps[:, 6:8, 0:256].rearrange("p b (a c) -> p a b c", a=2),
                                             ACT.Copy).then_inc(gla_copied, 1)
                    elif stage == "qk_norm":
                        act.wait_ge(qk_var, l + 1)
                        nc.scalar.activation(r_qk[:], ss_qk[:], ACT.Sqrt, bias=eps[:, 0:1], scale=1.0 / DK
                                             ).then_inc(qk_root, 1)
                        act.wait_ge(o_var, 2 * l + 1)
                        nc.scalar.activation(sd_o[:, 0], ss_o[:, 0], ACT.Sqrt, bias=eps[:, 1:2],
                                             scale=1.0 / P).then_inc(o_root, 1)
                    elif stage == "turn_keys":
                        for h in range(HEADS):
                            act.wait_ge(k_turned, l * HEADS + h + 1)
                            nc.scalar.activation(kf[:, h], ps[:, 4 + h], ACT.Copy).then_inc(kf_ready, 1)
                    elif stage == "attn":
                        s = at_[0]
                        if 1 <= s <= STEPS:
                            copy_turned(s - 1)
                        if s < STEPS:
                            exps(s)
                        if s >= 2:
                            copy_o(s - 2)
                    elif stage == "mix_gla":
                        for j in range(TB):
                            mix_highs(j)
                    elif stage == "z_act":
                        g = at_[0]
                        for u in range(2):
                            act.wait_ge(banks_free[u], emptied(unit0 + PART0["z"] + 2 * g + u, 1))
                        part = zg[:, :, g * WIDTH:(g + 1) * WIDTH]
                        nc.scalar.activation(part, part, ACT.Silu).then_inc(z_act, 1)

                act.wait_ge(o_var, 2 * l + 2)
                nc.scalar.activation(sd_o[:, 1], ss_o[:, 1], ACT.Sqrt, bias=eps[:, 0:1],
                                     scale=1.0 / P).then_inc(o_root, 1)
                for j in range(TB, 2 * TB):
                    mix_highs(j)
                out_unit = unit0 + L_UNITS - L_OUT
                output_squares(l + 1, out_unit, out_unit, L_OUT)

            def ffn(name, n):
                norm(n)
                unit, chunk = UNIT0[name], CHUNK0[name]
                split = SPLIT0[name]
                with act.Fori(0, FT // 2) as i:
                    for u in range(2):
                        act.wait_ge(tile_done, i * 4 + (2 * unit + 2 * u + 1))
                        act.wait_ge(tmp_ready, i * 2 + (split + u - 1))
                        nc.scalar.activation(gate[:, u], ps[:, 2 * u], ACT.Silu).then_inc(ff_gate, 1)
                        act.wait_ge(tile_done, i * 4 + (2 * unit + 2 * u + 2))
                        take_high(chunk + 2 + u, i)
                        act.wait_ge(tmp_ready, i * 2 + (split + u + 1))
                        nc.scalar.activation(fh[:, bass.ds(i * 2 + u, 1)], tmp[:, u:u + 1], ACT.Copy
                                             ).then_inc(high_ready, 1)
                unit += FT
                chunk += FT
                for m in range(KT):
                    act.wait_ge(half_used, (0 if name == "ffn1" else KT) + m + 1)
                    take_high(chunk + 2 * m + 2)
                    if m == KT - 1:
                        squares(n + 1, (m,))
                    act.wait_ge(tile_done, 2 * (unit + m + 1))
                    if m < KT - 1:
                        take_high(chunk + 2 * m + 3)
                        squares(n + 1, (m,))

            ffn("ffn1", 2)

            norm(3)
            unit, chunk = UNIT0["mixer"], CHUNK0["mixer"]
            for j in range(M_V):
                for t in range(2):
                    act.wait_ge(tile_done, 2 * unit + 2 * j + t + 1)
                    if t:
                        take_high(chunk + j + 2)
                    nc.scalar.activation(v2[:, 2 * t:2 * t + 2, 256 * j:256 * j + 256],
                                         ps[:, 2 * (j % 2) + t].rearrange("p (b c) -> p b c", b=2),
                                         ACT.Gelu_apprx_tanh).then_inc(banks_free[j % 2], 1)
            act.dma_start(ws_t[:], ins["sgu_w_t"]).then_inc(sgu_in, 16)
            act.dma_start(bs[:].rearrange("p h q -> p (h q)"), ins["sgu_b"].to_broadcast([P, KT * P])
                          ).then_inc(sgu_in, 16)
            unit += M_V
            chunk += M_V
            with act.Fori(0, M_U // 2) as i:
                for u in range(2):
                    for t in range(2):
                        act.wait_ge(tile_done, i * 4 + (2 * unit + 2 * u + t + 1))
                        if t:
                            take_high(chunk + u + 2, i)
                        nc.scalar.activation(u2[:, bass.ds(i * 4 + (2 * u + t), 1)],
                                             ps[:, 2 * u + t:2 * u + t + 1],
                                             ACT.Gelu_apprx_tanh).then_inc(banks_free[u], 1)
            unit += M_U
            chunk += M_U
            act.wait_ge(m_root_in, 1)
            nc.scalar.activation(ss_v[:, 1], ss_v[:, 0], ACT.Sqrt, bias=eps[:, 0:1], scale=1.0 / D
                                 ).then_inc(m_root, 1)
            with act.Fori(0, M_CX // 2) as i:
                for u in range(2):
                    act.wait_ge(tile_done, i * 4 + (2 * unit + 2 * u + 1))
                    act.wait_ge(m_prod, i * 2 + (u + 1))
                    nc.scalar.activation(gc[:, u], ps[:, 2 * u], ACT.Copy).then_inc(m_gc, 1)
                    act.wait_ge(tile_done, i * 4 + (2 * unit + 2 * u + 2))
                    take_high(chunk + u + 2, i)
            unit += M_CX
            chunk += M_CX
            for h in range(KT):
                high("sgu", h, ah[:, h])
            for j in range(M_GB):
                high("gb", 2 * j, bh[:, 2 * j])
                act.wait_ge(tile_done, 2 * (unit + j + 1))
                take_high(chunk + j + 2)
                high("gb", 2 * j + 1, bh[:, 2 * j + 1])
            unit += M_GB
            chunk += M_GB
            for j in range(KT):
                for t in range(2):
                    act.wait_ge(tile_done, 2 * unit + 4 * j + t + 1)
                    if t:
                        take_high(chunk + 2 * j + 2)
                    if j:
                        act.wait_ge(m_sig_used, 2 * j)
                    nc.scalar.activation(gc[:, t], ps[:, t], ACT.Sigmoid).then_inc(m_sig, 1)
                act.wait_ge(m_sig, 2 * j + 2)
                act.sem_inc(banks_free[0], 2)
                act.wait_ge(tile_done, 2 * unit + 4 * j + 4)
                take_high(chunk + 2 * j + 3)
                high("merge", j, mh[:, j])
            unit += M_MERGE
            chunk += M_MERGE
            output_squares(4, unit, chunk, M_OUT)
            ffn("ffn2", 4)
            norm(5, splits=False)

        @block.tensor
        def _(pe):
            def products(bank_ap, wt, xk, first, last):
                (w0, w1), (x0, x1) = wt, xk
                nc.tensor.matmul(bank_ap, w0, x0, start=first, stop=False)
                nc.tensor.matmul(bank_ap, w0, x1, start=False, stop=False)
                return nc.tensor.matmul(bank_ap, w1, x0, start=False, stop=last)

            def claim(i, unit, u):
                pe.wait_ge(banks_free[u], i * 2 + (unit + 2))

            def chunk_ready(i, chunk, u):
                pe.wait_ge(w_ready, i * 2 + (chunk + u + 1))

            def feature_unit(i, unit, chunk, u, moving):
                claim(i, unit, u)
                chunk_ready(i, chunk, u)
                for t in range(2):
                    mh_, ml_ = moving[t]
                    for k in range(KT):
                        cols = slice((t * KT + k) * P, (t * KT + k + 1) * P)
                        last = products(ps[:, 2 * u + t], (wh[u][:, cols], wl[u][:, cols]),
                                        (mh_[:, k], ml_[:, k]), k == 0, k == KT - 1)
                    last.then_inc(tile_done, 1)

            def token_block(u, tb):
                cols = slice(tb * P, tb * P + P)
                dst = ps[:, 2 * u + tb // 2, (tb % 2) * 256:(tb % 2) * 256 + 256]
                for k in range(KT):
                    w = slice(k * 256, k * 256 + 256)
                    nc.tensor.matmul(dst, xh[:, k, cols], wh[u][:, w], start=(k == 0), stop=False)
                    nc.tensor.matmul(dst, xl[:, k, cols], wh[u][:, w], start=False, stop=False)
                    last = nc.tensor.matmul(dst, xh[:, k, cols], wl[u][:, w], start=False,
                                            stop=(k == KT - 1))
                return last

            def token_unit(i, unit, chunk, u):
                claim(i, unit, u)
                chunk_ready(i, chunk, u)
                for tb in range(TB):
                    last = token_block(u, tb)
                    if tb % 2:
                        last.then_inc(tile_done, 1)

            def first_feature_unit(unit, chunk, moving, low0):
                claim(0, unit, 0)
                chunk_ready(0, chunk, 0)
                for k in range(KT):
                    pe.wait_ge(low_ready, low0 + k + 1)
                    for t in range(2):
                        cols = slice((t * KT + k) * P, (t * KT + k + 1) * P)
                        last = products(ps[:, t], (wh[0][:, cols], wl[0][:, cols]),
                                        (moving[0][:, k], moving[1][:, k]), k == 0, k == KT - 1)
                        if k == KT - 1:
                            last.then_inc(tile_done, 1)

            def first_token_unit(unit, chunk, low0):
                claim(0, unit, 0)
                chunk_ready(0, chunk, 0)
                for k in range(KT):
                    pe.wait_ge(low_ready, low0 + k + 1)
                    w = slice(k * 256, k * 256 + 256)
                    for tb in range(TB):
                        cols = slice(tb * P, tb * P + P)
                        dst = ps[:, tb // 2, (tb % 2) * 256:(tb % 2) * 256 + 256]
                        nc.tensor.matmul(dst, xh[:, k, cols], wh[0][:, w],
                                         start=(k == 0 and tb % 2 == 0), stop=False)
                        nc.tensor.matmul(dst, xl[:, k, cols], wh[0][:, w], start=False, stop=False)
                        last = nc.tensor.matmul(dst, xh[:, k, cols], wl[0][:, w], start=False,
                                                stop=(k == KT - 1 and tb % 2 == 1))
                        if k == KT - 1 and tb % 2:
                            last.then_inc(tile_done, 1)

            def units(count, unit, chunk, body):
                with pe.Fori(0, count // 2) as i:
                    for u in range(2):
                        body(i, unit, chunk, u)

            both_x = [(xh, xl), (xh, xl)]

            def norm(n):
                pe.wait_ge(sumsq_ready, n + 1)
                for tb in range(TB):
                    nc.tensor.matmul(ps[:, 6, tb:tb + 1], sumsq[:, tb * P:tb * P + P], ones[:, 0:1],
                                     start=(tb == 0), stop=False)
                pe.wait_ge(sq_ready, (n + 1) * KT)
                for tb in range(TB):
                    last = nc.tensor.matmul(ps[:, 6, tb:tb + 1], sq[:, 1, tb * P:tb * P + P], ones[:, 0:1],
                                            start=False, stop=(tb == TB - 1))
                last.then_inc(norm_ss, 1)
                pe.wait_ge(diag_ready, n + 1)
                nc.tensor.matmul(ps[:, 7], ones[:], sq[:, 1], start=True,
                                 stop=True).then_inc(norm_bc, 1)

            pe.wait_ge(consts, N_CONST)
            for l in range(LAYERS):
                unit0 = UNIT0[f"layer{l}"]
                if l == 0:
                    pe.wait_ge(c_ready, 1)
                    for k in range(ADA_PE):
                        pe.wait_ge(ada_landed[k], 16)
                        for m in range(16):
                            nc.tensor.matmul(ps[:, 4, m:m + 1], ada_w[k][:, m * P:m * P + P], c_act[:, k:k + 1],
                                             start=(k == 0 and m == 0), stop=False)
                norm(l)
                if l == 0:
                    for half in range(2):
                        pe.wait_ge(ada_sum, half + 1)
                        for m in range(8 * half, 8 * half + 8):
                            last = nc.tensor.matmul(ps[:, 4, m:m + 1], acc[:, m * P:m * P + P], ones[:, 0:1],
                                                    start=False, stop=(m == 15))
                    last.then_inc(ada_cols, 1)

                def part(stage, j, p):
                    unit = unit0 + PART0[stage] + j
                    u, t, half = unit % 2, p // 2, p % 2
                    if (stage, j) == ("conv", 0):
                        if p == 0:
                            first_feature_unit(unit0, unit0, (xh, xl), SPLIT0[f"norm{l}"])
                        return
                    if p == 0:
                        pe.wait_ge(banks_free[u], emptied(unit, 1) - 2)
                        pe.wait_ge(w_ready, unit + 1)
                    if stage in ("conv", "q"):
                        for k in range(half * KT // 2, (half + 1) * KT // 2):
                            cols = slice((t * KT + k) * P, (t * KT + k + 1) * P)
                            last = products(ps[:, 2 * u + t], (wh[u][:, cols], wl[u][:, cols]),
                                            (xh[:, k], xl[:, k]), k == 0, k == KT - 1)
                    else:
                        last = token_block(u, p)
                    if half:
                        last.then_inc(tile_done, 1)

                out_unit = unit0 + L_UNITS - L_OUT

                def turn_output(j):
                    g, tb = j // TB, j % TB
                    pe.wait_ge(o_normed, l * 8 + j + 1)
                    for h in range(HEADS):
                        last = nc.tensor.transpose(ps[:, 4 + j % 4, h * P:h * P + P],
                                                   o[g][:, tb, h * P:h * P + P], ident[:])
                    last.then_inc(o_turned, 1)

                def first_out(ks):
                    for u in range(2):
                        for t in range(2):
                            for k in ks:
                                cols = slice((t * KT + k) * P, (t * KT + k + 1) * P)
                                last = products(ps[:, 2 * u + t], (wh[u][:, cols], wl[u][:, cols]),
                                                (xh[:, k], xl[:, k]), k == 0, k == KT - 1)
                            if ks[-1] == KT - 1:
                                last.then_inc(tile_done, 1)

                def score(s):
                    qb, h = s // HEADS, s % HEADS
                    if s:
                        pe.wait_ge(exp_done, 2 * (l * STEPS + s))
                    for m in range(2):
                        rows = slice(64 * m, 64 * m + 64)
                        nc.tensor.matmul(ps[:, 4 + m, 0:P * (qb + 1)], q[rows, h, qb * P:qb * P + P],
                                         kf[rows, h, 0:P * (qb + 1)], start=True, stop=True
                                         ).then_inc(scores, 1)

                def turn(s):
                    pe.wait_ge(attn_ready, l * STEPS + s + 1)
                    if s:
                        pe.wait_ge(at_copied, l * STEPS + s)
                    for kb in range(s // HEADS + 1):
                        last = nc.tensor.transpose(ps[:, 6, kb * P:kb * P + P],
                                                   prob[:, s % 2, 0, kb * P:kb * P + P], ident[:])
                    last.then_inc(attn_turned, 1)

                def pv(s):
                    qb, h = s // HEADS, s % HEADS
                    pe.wait_ge(at_copied, l * STEPS + s + 1)
                    if s:
                        pe.wait_ge(o_copied, l * STEPS + s)
                    for kb in range(qb + 1):
                        last = nc.tensor.matmul(ps[:, 7, 0:P], attn_t[:, s % 2, kb * P:kb * P + P],
                                                v[:, kb, h * P:h * P + P], start=(kb == 0), stop=(kb == qb))
                    last.then_inc(pv_done, 1)

                def outer(c):
                    if c >= 2:
                        pe.wait_ge(state_ready, l * NCH + c - 1)
                    rows = slice(64 * (c % 2), 64 * (c % 2) + 64)
                    for p in range(2):
                        last = nc.tensor.matmul(ps[:, 4 + c % 2, p * 256:p * 256 + 256],
                                                decay[rows, c // 2, p * P:p * P + P],
                                                gv[rows, c // 2, p * 256:p * 256 + 256],
                                                start=True, stop=True)
                    last.then_inc(outer_done, 1)

                def read_out(tb):
                    pe.wait_ge(state_ready, l * NCH + 2 * tb + 2)
                    if tb:
                        pe.wait_ge(gla_copied, l * TB + tb)
                    for half in range(2):
                        c = 2 * tb + half
                        for h in range(HEADS):
                            rows = slice(64 * (h % 2), 64 * (h % 2) + 64)
                            last = nc.tensor.matmul(
                                ps[64 * half:64 * half + 64, 6 + h % 2, (h // 2) * P:(h // 2) * P + P],
                                conv[rows, h // 2, c * CHUNK:(c + 1) * CHUNK],
                                states[rows, c, h // 2, (h % 2) * P:(h % 2) * P + P],
                                start=True, stop=True)
                    last.then_inc(gla_o, 1)

                for stage, *at_ in ORDER:
                    if stage == "part":
                        part(*at_)
                    elif stage == "lr":
                        pe.wait_ge(lr_w, l + 1)
                        for k in range(KT):
                            last = products(ps[:, 4], (wr_h[:, k], wr_l[:, k]), (xh[:, k], xl[:, k]),
                                            k == 0, k == KT - 1)
                        last.then_inc(glr_done, 1)
                    elif stage == "gate":
                        pe.wait_ge(glr_copied, l + 1)
                        for tb in range(TB):
                            last = nc.tensor.matmul(ps[:, 4 + tb // 2, (tb % 2) * 256:(tb % 2) * 256 + 256],
                                                    glr[0:RANK + 1, tb * P:tb * P + P], wgk[:, l],
                                                    start=True, stop=True)
                        last.then_inc(gate_mm, 1)
                    elif stage == "decay":
                        pe.wait_ge(loga_ready, l + 1)
                        for tb in range(TB):
                            last = nc.tensor.matmul(ps[:, 6 + tb // 2, (tb % 2) * 256:(tb % 2) * 256 + 256],
                                                    later[:], log_a[:, tb], start=True, stop=True)
                        last.then_inc(decay_mm, 1)
                        for tb in range(TB):
                            for p in range(2):
                                last = nc.tensor.matmul(ps[:, 4, p * NCH + 2 * tb:p * NCH + 2 * tb + 2],
                                                        log_a[:, tb, p * P:p * P + P], inchunk[:],
                                                        start=True, stop=True)
                        last.then_inc(decay_mm, 1)
                    elif stage == "turn_k":
                        pe.wait_ge(conv_act, l * KT + 4)
                        pe.wait_ge(decay_exp, 2 * l + 2)
                        for tb in range(TB):
                            for p in range(2):
                                c0 = (tb % 2) * 256 + p * P
                                last = nc.tensor.transpose(ps[:, 6 + tb // 2, c0:c0 + P],
                                                           conv[:, 2 + p, tb * P:tb * P + P], ident[:])
                        last.then_inc(gk_turned, 1)
                    elif stage == "turn_v":
                        tb = at_[0]
                        if tb == 0:
                            pe.wait_ge(conv_act, (l + 1) * KT)
                        if tb >= 2:
                            pe.wait_ge(gv_ready, l * TB + tb - 1)
                        for h in range(HEADS):
                            last = nc.tensor.transpose(ps[:, 4 + tb % 2, h * P:h * P + P],
                                                       conv[:, 4 + h, tb * P:tb * P + P], ident[:])
                        last.then_inc(gv_turned, 1)
                    elif stage == "outer":
                        if at_[0] == 0:
                            pe.wait_ge(gk_ready, l + 1)
                            pe.wait_ge(gv_ready, (l + 1) * TB)
                        outer(at_[0])
                    elif stage == "read_out":
                        read_out(at_[0])
                    elif stage == "q_sums":
                        pe.wait_ge(q_sq, (l + 1) * HEADS)
                        pe.wait_ge(state_ready, (l + 1) * NCH)
                        for h in range(HEADS):
                            for tb in range(TB):
                                last = nc.tensor.matmul(ps[:, 5, tb * 8 + 2 * h:tb * 8 + 2 * h + 2],
                                                        (sq, tmp)[h // 2][:, h % 2, tb * P:tb * P + P],
                                                        inhalf[:], start=True, stop=True)
                        if l == 0:
                            pe.wait_ge(ada_sum, 3)
                            for m in range(32):
                                last = nc.tensor.matmul(ps[:, 5, 64 + m:65 + m],
                                                        acc_late[:, m * P:m * P + P], ones[:, 0:1],
                                                        start=True, stop=True)
                        last.then_inc(q_ss, 1)
                    elif stage == "turn_keys":
                        pe.wait_ge(k_normed, l + 1)
                        pe.wait_ge(gla_copied, (l + 1) * TB)
                        for h in range(HEADS):
                            for tb in range(TB):
                                last = nc.tensor.transpose(ps[:, 4 + h, tb * P:tb * P + P],
                                                           k_tok[:, tb, h * P:h * P + P], ident[:])
                            last.then_inc(k_turned, 1)
                    elif stage == "attn":
                        s = at_[0]
                        if s == 0:
                            pe.wait_ge(kf_ready, (l + 1) * HEADS)
                        if s == 2:
                            for u in range(2):
                                pe.wait_ge(banks_free[u], emptied(unit0 + PART0["v"] + u, 1))
                        if s < STEPS:
                            score(s)
                        if 1 <= s <= STEPS:
                            turn(s - 1)
                        if s >= 2:
                            pv(s - 2)
                    elif stage == "mix_gla":
                        pe.wait_ge(o_copied, (l + 1) * STEPS)
                        for j in range(TB):
                            turn_output(j)
                        pe.wait_ge(mix_low, l * 8 + TB)
                        for u in range(2):
                            claim(0, out_unit, u)
                            chunk_ready(0, out_unit, u)
                        first_out(range(TB))

                for j in range(TB, 2 * TB):
                    turn_output(j)
                pe.wait_ge(mix_low, (l + 1) * 8)
                first_out(range(TB, KT))
                with pe.Fori(1, L_OUT // 2) as i:
                    for u in range(2):
                        feature_unit(i, out_unit, out_unit, u, both_x)

            def ffn(name, n):
                norm(n)
                unit, chunk = UNIT0[name], CHUNK0[name]
                first_feature_unit(unit, chunk, (xh, xl), SPLIT0[f"norm{n}"])
                feature_unit(0, unit, chunk, 1, both_x)
                with pe.Fori(1, FT // 2) as i:
                    for u in range(2):
                        feature_unit(i, unit, chunk, u, both_x)
                unit += FT
                chunk += FT

                def output_tile(i, m, low0=None):
                    claim(i, unit, m)
                    for half in range(2):
                        pe.wait_ge(w_ready, i * 4 + (chunk + 2 * m + half + 1))
                        for kk in range(FH):
                            k = half * FH + kk
                            if low0 is not None:
                                pe.wait_ge(low_ready, low0 + k + 1)
                            cols = slice(kk * P, kk * P + P)
                            last = products(ps[:, 2 * m], (wh[half][:, cols], wl[half][:, cols]),
                                            (fh[:, k], fl[:, k]), k == 0, k == FT - 1)
                        if half == 0:
                            last.then_inc(half_used, 1)
                    last.then_inc(tile_done, 2)

                output_tile(0, 0, low0=SPLIT0[name])
                output_tile(0, 1)
                with pe.Fori(1, KT // 2) as i:
                    for m in range(2):
                        output_tile(i, m)

            ffn("ffn1", 2)

            norm(3)
            unit, chunk = UNIT0["mixer"], CHUNK0["mixer"]
            first_token_unit(unit, chunk, SPLIT0["norm3"])
            token_unit(0, unit, chunk, 1)
            with pe.Fori(1, M_V // 2) as i:
                for u in range(2):
                    token_unit(i, unit, chunk, u)
            unit += M_V
            chunk += M_V
            units(M_U + M_CX, unit, chunk, lambda i, a, b, u: feature_unit(i, a, b, u, both_x))
            unit += M_U + M_CX
            chunk += M_U + M_CX
            pe.wait_ge(m_vn, 1)
            pe.wait_ge(sgu_in, 32)
            for h in range(KT):
                if h >= 2:
                    pe.wait_ge(sgu_free, h - 1)
                for c in range(TB):
                    last = nc.tensor.matmul(ps[:, 4 + h % 2, c * P:c * P + P], v2[:, c, h * P:h * P + P],
                                            ws_t[:, h], start=True, stop=True)
                last.then_inc(sgu_mm, 1)
            units(M_GB, unit, chunk, lambda i, a, b, u: feature_unit(i, a, b, u, both_x))
            unit += M_GB
            chunk += M_GB
            feature_unit(0, unit, chunk, 0, both_x)
            pe.wait_ge(low_ready, SPLIT0["gb"] + KT)
            feature_unit(0, unit, chunk, 1, [(ah, al), (bh, bl)])
            with pe.Fori(1, M_MERGE // 2) as i:
                feature_unit(i, unit, chunk, 0, both_x)
                feature_unit(i, unit, chunk, 1, [(ah, al), (bh, bl)])
            unit += M_MERGE
            chunk += M_MERGE
            merged = [(mh, ml), (mh, ml)]
            first_feature_unit(unit, chunk, (mh, ml), SPLIT0["merge"])
            feature_unit(0, unit, chunk, 1, merged)
            with pe.Fori(1, M_OUT // 2) as i:
                for u in range(2):
                    feature_unit(i, unit, chunk, u, merged)
            ffn("ffn2", 4)
            norm(5)

        @block.vector
        def _(dve):
            chain = [0]

            def link(ins_):
                chain[0] = chain[0] + 1
                ins_.then_inc(dve_step, 1)
                dve.wait_ge(dve_step, chain[0])

            def low(name, k, dst, hi):
                at_ = SPLIT0[name] + k
                dve.wait_ge(high_ready, at_ + 1)
                nc.vector.tensor_tensor(dst, tmp[:, k % 2], hi.bitcast(F32), ALU.subtract).then_inc(low_ready, 1)

            def tmp_free(name, k):
                at_ = SPLIT0[name] + k
                if at_ >= 2:
                    dve.wait_ge(low_ready, at_ - 1)

            def add_square(n, m):
                at_ = n * KT + m
                dve.wait_ge(sq_ready, at_ + 1)
                if m == 0:
                    ins_ = nc.vector.tensor_copy(sumsq[:], sq[:, 0])
                else:
                    dve.wait_ge(sq_used, at_)
                    ins_ = nc.vector.tensor_tensor(sumsq[:], sumsq[:], sq[:, m % 2], ALU.add)
                ins_.then_inc(sq_used, 1)
                if m == KT - 2:
                    dve.wait_ge(sq_used, at_ + 1)
                    dve.sem_inc(sumsq_ready, 1)

            def norm_head(n):
                dve.wait_ge(norm_root, n + 1)
                dve.sem_inc(sq_used, 1)
                link(nc.vector.reciprocal(norm_r[:], norm_sd[:]))
                nc.vector.tensor_tensor(diag, ident[:].unsqueeze(1).to_broadcast([P, TB, P]),
                                        norm_r[:].unsqueeze(2).to_broadcast([P, TB, P]), ALU.mult
                                        ).then_inc(diag_ready, 1)

            def norm(n, gain, shift=None):
                if n:
                    norm_head(n)
                dve.wait_ge(norm_bc, n + 1)
                for k in range(KT):
                    name = f"norm{n}"
                    if n == 5:
                        nc.vector.scalar_tensor_tensor(out=y[:, k], in0=x[:, k], scalar=gain[:, k:k + 1],
                                                       in1=ps[:, 7], op0=ALU.mult, op1=ALU.mult
                                                       ).then_inc(y_ready, 1)
                        continue
                    tmp_free(name, k)
                    if shift is None:
                        nc.vector.scalar_tensor_tensor(out=tmp[:, k % 2], in0=x[:, k],
                                                       scalar=gain[:, k:k + 1], in1=ps[:, 7],
                                                       op0=ALU.mult, op1=ALU.mult).then_inc(tmp_ready, 1)
                    else:
                        link(nc.vector.tensor_tensor(tmp[:, k % 2], x[:, k], ps[:, 7], ALU.mult))
                        nc.vector.tensor_scalar(tmp[:, k % 2], tmp[:, k % 2], gain[:, k:k + 1],
                                                shift[:, k:k + 1], ALU.mult, ALU.add).then_inc(tmp_ready, 1)
                    if k:
                        low(name, k - 1, xl[:, k - 1], xh[:, k - 1])
                if n < 5:
                    low(f"norm{n}", KT - 1, xl[:, KT - 1], xh[:, KT - 1])

            def residual(n, unit, scale_of, whole_unit):
                for m in range(KT):
                    j, t = (m, 0) if whole_unit else (m // 2, m % 2)
                    u = j % 2
                    if m:
                        add_square(n, m - 1)
                    dve.wait_ge(tile_done, 2 * (unit + j) + (2 if whole_unit else t + 1))
                    nc.vector.scalar_tensor_tensor(out=x[:, m], in0=ps[:, 2 * u + t], scalar=scale_of(m),
                                                   in1=x[:, m], op0=ALU.mult, op1=ALU.add
                                                   ).then_inc(x_ready, 1)
                    dve.wait_ge(x_ready, (n - 1) * KT + m + 1)
                    dve.sem_inc(banks_free[u], 2 if whole_unit else 1)

            for u in range(2):
                dve.sem_inc(banks_free[u], 2)
            nc.vector.memset(inchunk[:], 0.0).then_inc(consts, 1)
            nc.vector.memset(inhalf[:], 0.0).then_inc(consts, 1)
            dve.wait_ge(consts, 2)
            for h in range(2):
                rows = slice(h * 64, h * 64 + 64)
                nc.vector.memset(inchunk[rows, h:h + 1], 1.0 / 16).then_inc(consts, 1)
                nc.vector.memset(inhalf[rows, h:h + 1], 1.0).then_inc(consts, 1)
            for i, value in enumerate((EPS, 64 * EPS, 1.0)):
                nc.vector.memset(eps[:, i:i + 1], value).then_inc(consts, 1)
            dve.wait_ge(pool_step, 6)
            nc.vector.memset(later[64:128, 0:64], 0.0).then_inc(consts, 1)
            dve.wait_ge(consts, N_CONST)

            def ada_piece(dst, w, k, used, before):
                if before is None:
                    ins_ = nc.vector.tensor_scalar(dst, w, c_act[:, k:k + 1], None, ALU.mult)
                else:
                    dve.wait_ge(used, before)
                    ins_ = nc.vector.scalar_tensor_tensor(out=dst, in0=w, scalar=c_act[:, k:k + 1],
                                                          in1=dst, op0=ALU.mult, op1=ALU.add)
                ins_.then_inc(used, 1)

            def ada_first(ks):
                for k in ks:
                    dve.wait_ge(ada_landed[k], 16)
                    for half in range(2):
                        cols = slice(half * D, half * D + D)
                        done = 2 * (k - ADA_PE) + half
                        ada_piece(acc[:, cols], ada_w[k][:, cols], k, ada_used,
                                  None if k == ADA_PE else done - 1)
                        if k == KT - 1:
                            dve.wait_ge(ada_used, done + 1)
                            dve.sem_inc(ada_sum, 1)

            def modulation(l, mod_part, sums):
                link(nc.vector.tensor_tensor(mod[:, l, mod_part], sums, b_ada[:, l, mod_part], ALU.add))
                if mod_part.start == 0:
                    link(nc.vector.scalar_tensor_tensor(out=mod[:, l, 8:16], in0=mod[:, l, 8:16], scalar=1.0,
                                                        in1=norm_g[:, l], op0=ALU.add, op1=ALU.mult))

            def rank_zeros():
                link(nc.vector.memset(wr_h[:].bitcast(F32), 0.0))
                link(nc.vector.memset(wr_l[:].bitcast(F32), 0.0))

            def rank_weights(l):
                link(nc.vector.tensor_copy(wr_h[:, :, 0:RANK], wr_raw[:, l]))
                nc.vector.tensor_tensor(wr_l[:, :, 0:RANK], wr_raw[:, l], wr_h[:, :, 0:RANK].bitcast(F32),
                                        ALU.subtract).then_inc(lr_w, 1)

            def conv_zeros():
                link(nc.vector.memset(u_in[:, :, 0:CONV_K - 1], 0.0))

            rank_zeros()
            dve.wait_ge(c_ready, 1)
            ada_first(range(ADA_PE, 5))
            for m in range(KT - 1):
                add_square(0, m)
            ada_first(range(5, 6))
            norm_head(0)
            ada_first(range(6, KT))
            dve.wait_ge(small_in, N_SMALL)
            nc.vector.tensor_tensor(qkg[:], qk_g[:, :, 0], qk_g[:, :, 1], ALU.mult).then_inc(dve_step, 1)
            nc.vector.tensor_tensor(lam_p[:], lam_in[:, :, 0:4:2], lam_in[:, :, 1:4:2], ALU.mult
                                    ).then_inc(dve_step, 1)
            chain[0] += 2
            dve.wait_ge(dve_step, chain[0])
            link(nc.vector.tensor_scalar(qkg[:], qkg[:], DK ** -0.5, None, ALU.mult))
            nc.vector.tensor_reduce(lam_s[:], lam_p[:], AX_X, ALU.add).then_inc(lam_ready, 1)
            for l in range(LAYERS):
                link(nc.vector.tensor_scalar(o_g[:, l, 1], o_g[:, l, 1], 1.0 - lam_init(l), None, ALU.mult))
            rank_weights(0)
            dve.wait_ge(ada_cols, 1)
            modulation(0, slice(0, 16), ps[:, 4, 0:16])
            conv_zeros()
            for l in range(LAYERS):
                unit0 = UNIT0[f"layer{l}"]
                norm(l, mod[:, l, 8:16], mod[:, l, 0:8])
                if l == 0:
                    dve.wait_ge(lam_exp, 1)
                    for ll in range(LAYERS):
                        link(nc.vector.scalar_tensor_tensor(out=neglam[:, ll:ll + 1], in0=lam_e[:, ll, 1:2],
                                                            scalar=-lam_init(ll), in1=lam_e[:, ll, 0:1],
                                                            op0=ALU.add, op1=ALU.subtract))

                def copied(stage, j, t=1):
                    unit = unit0 + PART0[stage] + j
                    dve.wait_ge(banks_free[unit % 2], emptied(unit, t))

                def head_sums(g, tb):
                    o_sq = conv[:, 2 + tb % 2]
                    link(nc.vector.tensor_tensor(o_sq, o[g][:, tb], o[g][:, tb], ALU.mult))
                    link(nc.vector.tensor_reduce(ss_o[:, g, tb],
                                                 o_sq.rearrange("p (h d) -> p h d", d=P), AX_X, ALU.add))

                def gated(g, tb):
                    z_ = zg[:, tb, g * WIDTH:(g + 1) * WIDTH]
                    heads = z_.rearrange("p (h d) -> p h d", d=P)
                    dve.wait_ge(z_act, 2 * l + g + 1)
                    link(nc.vector.tensor_tensor(heads, heads, o_g[:, l, g].unsqueeze(1).to_broadcast([P, HEADS, P]),
                                                 ALU.mult))
                    link(nc.vector.tensor_tensor(z_, z_, o[g][:, tb], ALU.mult))
                    nc.vector.tensor_tensor(o[g][:, tb].rearrange("p (h d) -> p h d", d=P), heads,
                                            r_o[:, g, tb].unsqueeze(2).to_broadcast([P, HEADS, P]),
                                            ALU.mult).then_inc(o_normed, 1)

                def biases(s):
                    qb, h = s // HEADS, s % HEADS
                    n = P * (qb + 1)
                    dve.wait_ge(scores, 2 * (l * STEPS + s) + 2)
                    for m in range(2):
                        ins_ = nc.vector.memset(ps[0:64, 4 + m, n - 64:n], NEG)
                        ins_.then_inc(dve_step, 1)
                        chain[0] += 1
                    dve.wait_ge(dve_step, chain[0])
                    link(nc.vector.tensor_reduce(smax[:, s % 2], ps[:, 4:6, 0:n], AX_X, ALU.max))
                    nc.vector.tensor_tensor(nbias[:, s % 2], smax[:, s % 2], nrq[:, qb, 2 * h:2 * h + 2], ALU.mult
                                            ).then_inc(bias_ready, 1)

                def combine(s):
                    n = P * (s // HEADS + 1)
                    dve.wait_ge(exp_done, 2 * (l * STEPS + s) + 2)
                    link(nc.vector.reciprocal(rz[:, s % 2], zs[:, s % 2]))
                    link(nc.vector.tensor_scalar(prob[:, s % 2, 1, 0:n], prob[:, s % 2, 1, 0:n], rz[:, s % 2, 1:2],
                                                 neglam[:, l:l + 1], ALU.mult, ALU.mult))
                    nc.vector.scalar_tensor_tensor(out=prob[:, s % 2, 0, 0:n], in0=prob[:, s % 2, 0, 0:n],
                                                   scalar=rz[:, s % 2, 0:1], in1=prob[:, s % 2, 1, 0:n],
                                                   op0=ALU.mult, op1=ALU.add).then_inc(attn_ready, 1)

                def mix_lows(j):
                    g, tb = j // TB, j % TB
                    dve.wait_ge(mix_high, l * 8 + j + 1)
                    hi = xh[:, 4 * g:4 * g + 4, tb * P:tb * P + P]
                    nc.vector.tensor_tensor(xl[:, 4 * g:4 * g + 4, tb * P:tb * P + P],
                                            ps[:, 4 + j % 4].rearrange("p (h c) -> p h c", h=4),
                                            hi.bitcast(F32), ALU.subtract).then_inc(mix_low, 1)

                for stage, *at_ in ORDER:
                    if stage == "ada":
                        if l == 0:
                            n = at_[0]
                            la, k, _, place_ = ADA_LATE_PIECES[n]
                            dve.wait_ge(late_landed[n % 4], 16 * (n // 4 + 1))
                            ada_piece(acc_late[:, place_:place_ + D], ada_late[n % 4][:], k, late_used,
                                      None if k == 0 else n if la == 0 else n - 2)
                            if n == ADA_LATE - 1:
                                dve.wait_ge(late_used, ADA_LATE)
                                dve.sem_inc(ada_sum, 1)
                    elif stage == "conv":
                        m = at_[0]
                        copied("conv", m // 2, m % 2)
                        link(nc.vector.tensor_scalar(conv[:, m], u_in[:, m, 0:S], conv_w[:, l, m, 0:1], None,
                                                     ALU.mult))
                        for j in range(1, CONV_K):
                            ins_ = nc.vector.scalar_tensor_tensor(
                                out=conv[:, m], in0=u_in[:, m, j:j + S], scalar=conv_w[:, l, m, j:j + 1],
                                in1=conv[:, m], op0=ALU.mult, op1=ALU.add)
                            if j < CONV_K - 1:
                                link(ins_)
                        ins_.then_inc(conv_done, 1)
                    elif stage == "gate":
                        dve.wait_ge(gate_mm, l + 1)
                        nc.vector.tensor_scalar(log_a[:], ps[:, 4:6].rearrange("p a (b c) -> p (a b) c", b=2),
                                                0.0, None, ALU.min).then_inc(gate_min, 1)
                        dve.wait_ge(gate_soft, l + 1)
                        nc.vector.tensor_tensor(log_a[:], log_a[:], soft[:], ALU.subtract
                                                ).then_inc(loga_ready, 1)
                    elif stage == "turn_k":
                        dve.wait_ge(gk_turned, l + 1)
                        nc.vector.tensor_tensor(decay[:], ps[:, 6:8].rearrange("p a (b c) -> p (a b) c", b=2),
                                                decay[:], ALU.mult).then_inc(gk_ready, 1)
                    elif stage == "outer":
                        c = at_[0]
                        dve.wait_ge(outer_done, l * NCH + c + 1)
                        if c:
                            dve.wait_ge(state_ready, l * NCH + c)
                        for p in range(2):
                            if c == 0:
                                ins_ = nc.vector.tensor_copy(states[:, 0, p], ps[:, 4, p * 256:p * 256 + 256])
                            else:
                                ins_ = nc.vector.scalar_tensor_tensor(
                                    out=states[:, c, p], in0=states[:, c - 1, p], scalar=aend[:, p, c:c + 1],
                                    in1=ps[:, 4 + c % 2, p * 256:p * 256 + 256], op0=ALU.mult, op1=ALU.add)
                            if p == 0:
                                link(ins_)
                        ins_.then_inc(state_ready, 1)
                    elif stage == "gla_ss":
                        dve.wait_ge(gla_copied, l * TB + at_[0] + 1)
                        head_sums(0, at_[0])
                        if at_[0] == TB - 1:
                            dve.sem_inc(o_var, 1)
                    elif stage == "q_squares":
                        for h in range(HEADS):
                            copied("q", h // 2, h % 2)
                            nc.vector.tensor_tensor((sq, tmp)[h // 2][:, h % 2], q[:, h], q[:, h], ALU.mult
                                                    ).then_inc(q_sq, 1)
                        dve.wait_ge(q_sq, (l + 1) * HEADS)
                        link(nc.vector.tensor_scalar(q[:], q[:], qkg[:, l:l + 1], None, ALU.mult))
                    elif stage == "k_sums":
                        copied("k", 0)
                        copied("k", 1)
                        link(nc.vector.tensor_tensor(k_sq[:], k_tok[:], k_tok[:], ALU.mult))
                        link(nc.vector.tensor_reduce(ss_qk[:, 0].rearrange("p b g -> p (b g)"),
                                                     k_sq[:].rearrange("p b (g d) -> p (b g) d", d=DK),
                                                     AX_X, ALU.add))
                    elif stage == "qk_norm":
                        dve.wait_ge(q_ss, l + 1)
                        nc.vector.tensor_copy(ss_qk[:, 1].rearrange("p b g -> p (b g)"), ps[:, 5, 0:32]
                                              ).then_inc(qk_var, 1)
                        if l == 0:
                            modulation(0, slice(16, 24), ps[:, 5, 64:72])
                            modulation(1, slice(0, 24), ps[:, 5, 72:96])
                        dve.wait_ge(qk_root, l + 1)
                        link(nc.vector.reciprocal(r_qk[:], r_qk[:]))
                        link(nc.vector.tensor_scalar(nrq[:], r_qk[:, 1], -1.0, None, ALU.mult))
                        keys = k_tok[:].rearrange("p b (g d) -> p (b g) d", d=DK)
                        rk = r_qk[:, 0].rearrange("p b g -> p (b g)").unsqueeze(2)
                        nc.vector.tensor_tensor(keys, keys, rk.to_broadcast([P, TB * 8, DK]), ALU.mult
                                                ).then_inc(k_normed, 1)
                        dve.wait_ge(o_root, 2 * l + 1)
                        link(nc.vector.reciprocal(r_o[:, 0], sd_o[:, 0]))
                    elif stage == "attn":
                        s = at_[0]
                        if 1 <= s <= STEPS:
                            combine(s - 1)
                        if s < STEPS:
                            biases(s)
                    elif stage == "diff_ss":
                        qb = at_[0]
                        dve.wait_ge(o_copied, l * STEPS + HEADS * (qb + 1))
                        head_sums(1, qb)
                    elif stage == "gated":
                        g, tb = at_
                        if g == 1 and tb == 0:
                            dve.sem_inc(o_var, 1)
                            dve.wait_ge(o_root, 2 * l + 2)
                            link(nc.vector.reciprocal(r_o[:, 1], sd_o[:, 1]))
                        gated(g, tb)
                    elif stage == "mix_gla":
                        for j in range(TB):
                            mix_lows(j)
                for j in range(TB, 2 * TB):
                    mix_lows(j)
                if l + 1 < LAYERS:
                    rank_zeros()
                    rank_weights(l + 1)
                    conv_zeros()
                residual(l + 1, unit0 + L_UNITS - L_OUT, lambda m: mod[:, l, 16 + m:17 + m], False)

            def ffn(name, n, gain):
                norm(n, gain)
                unit, split = UNIT0[name], SPLIT0[name]
                gate0 = 0 if name == "ffn1" else FT
                with dve.Fori(0, FT // 2) as i:
                    for u in range(2):
                        dve.wait_ge(ff_gate, i * 2 + (gate0 + u + 1))
                        dve.wait_ge(tile_done, i * 4 + (2 * unit + 2 * u + 2))
                        dve.wait_ge(low_ready, i * 2 + (split + u - 1))
                        nc.vector.tensor_tensor(tmp[:, u], ps[:, 2 * u + 1], gate[:, u], ALU.mult
                                                ).then_inc(tmp_ready, 1)
                        dve.wait_ge(tmp_ready, i * 2 + (split + u + 1))
                        dve.sem_inc(banks_free[u], 2)
                        dve.wait_ge(high_ready, i * 2 + (split + u + 1))
                        nc.vector.tensor_tensor(fl[:, bass.ds(i * 2 + u, 1)], tmp[:, u:u + 1],
                                                fh[:, bass.ds(i * 2 + u, 1)].bitcast(F32), ALU.subtract
                                                ).then_inc(low_ready, 1)
                residual(n + 1, unit + FT, lambda m: 0.5, True)

            ffn("ffn1", 2, gains[:, 0])

            norm(3, gains[:, 1])
            unit = UNIT0["mixer"]
            nc.vector.memset(tpad[:], 0.0).then_inc(dve_step, 1)
            chain[0] += 1
            dve.wait_ge(dve_step, chain[0])
            dve.sem_inc(m_prod, 2)
            for u in range(2):
                dve.wait_ge(banks_free[u], emptied(unit + 3, 1))
            for tb in range(TB):
                link(nc.vector.tensor_tensor(v2_sq[:], v2[:, tb], v2[:, tb], ALU.mult))
                link(nc.vector.tensor_reduce(ss_v[:, 0, tb:tb + 1], v2_sq[:], AX_X, ALU.add))
            dve.sem_inc(m_root_in, 1)
            dve.wait_ge(m_root, 1)
            link(nc.vector.reciprocal(ss_v[:, 2], ss_v[:, 1]))
            for tb in range(TB):
                link(nc.vector.tensor_scalar(v2[:, tb], v2[:, tb], ss_v[:, 2, tb:tb + 1], None, ALU.mult))
            dve.sem_inc(m_vn, 1)
            unit += M_V + M_U
            for j in range(M_CX):
                u = j % 2
                dve.wait_ge(m_gc, j + 1)
                dve.wait_ge(tile_done, 2 * (unit + j) + 2)
                link(nc.vector.tensor_tensor(tpad[:, u, 1:S + 1], ps[:, 2 * u + 1], gc[:, u], ALU.mult))
                dve.sem_inc(banks_free[u], 2)
                dve.sem_inc(m_prod, 1)
                link(nc.vector.tensor_scalar(cv[:, j], tpad[:, u, 0:S], conv2_w[:, j, 0:1], None, ALU.mult))
                for tap in (1, 2):
                    link(nc.vector.scalar_tensor_tensor(out=cv[:, j], in0=tpad[:, u, tap:tap + S],
                                                        scalar=conv2_w[:, j, tap:tap + 1], in1=cv[:, j],
                                                        op0=ALU.mult, op1=ALU.add))
            unit += M_CX
            dve.wait_ge(sgu_in, 32)
            for h in range(KT):
                dve.wait_ge(sgu_mm, h + 1)
                tmp_free("sgu", h)
                link(nc.vector.scalar_tensor_tensor(
                    out=tmp[:, h % 2].rearrange("p (c q) -> p c q", c=TB),
                    in0=ps[:, 4 + h % 2].rearrange("p (c q) -> p c q", c=TB), scalar=sgu_g[:, h:h + 1],
                    in1=bs[:, h].unsqueeze(1).to_broadcast([P, TB, P]), op0=ALU.mult, op1=ALU.add))
                dve.sem_inc(sgu_free, 1)
                nc.vector.tensor_tensor(tmp[:, h % 2], tmp[:, h % 2], u2[:, h], ALU.mult).then_inc(tmp_ready, 1)
                if h:
                    low("sgu", h - 1, al[:, h - 1], ah[:, h - 1])
            low("sgu", KT - 1, al[:, KT - 1], ah[:, KT - 1])
            for m in range(KT):
                u, t = m // 2 % 2, m % 2
                dve.wait_ge(tile_done, 2 * (unit + m // 2) + t + 1)
                tmp_free("gb", m)
                nc.vector.tensor_tensor(tmp[:, m % 2], ps[:, 2 * u + t], cv[:, m], ALU.mult
                                        ).then_inc(tmp_ready, 1)
                dve.wait_ge(tmp_ready, SPLIT0["gb"] + m + 1)
                dve.sem_inc(banks_free[u], 1)
                low("gb", m, bl[:, m], bh[:, m])
            unit += M_GB
            for j in range(KT):
                dve.wait_ge(m_sig, 2 * j + 2)
                dve.wait_ge(tile_done, 2 * unit + 4 * j + 4)
                tmp_free("merge", j)
                for t in range(2):
                    link(nc.vector.tensor_tensor(gc[:, t], ps[:, 2 + t], gc[:, t], ALU.mult))
                dve.sem_inc(banks_free[1], 2)
                nc.vector.tensor_tensor(tmp[:, j % 2], gc[:, 0], gc[:, 1], ALU.add).then_inc(tmp_ready, 1)
                dve.wait_ge(tmp_ready, SPLIT0["merge"] + j + 1)
                dve.sem_inc(m_sig_used, 2)
                low("merge", j, ml[:, j], mh[:, j])
            unit += M_MERGE
            residual(4, unit, lambda m: 1.0, False)
            ffn("ffn2", 4, gains[:, 2])
            norm(5, gains[:, 3])


def _tiles(w):
    return w.reshape(-1, P, w.shape[-1]).transpose(1, 0, 2)


def _feature_chunks(a, b):
    n = a.shape[1] // P
    both = np.stack([_tiles(a).reshape(P, KT, n, P), _tiles(b).reshape(P, KT, n, P)])
    return both.transpose(3, 1, 0, 2, 4).reshape(n, P, CW)


def _pair_chunks(w):
    n = w.shape[1] // P
    t = _tiles(w).reshape(P, KT, n // 2, 2, P)
    return t.transpose(2, 0, 3, 1, 4).reshape(n // 2, P, CW)


def _token_chunks(w):
    n = w.shape[1] // 256
    return _tiles(w).reshape(P, KT, n, 256).transpose(2, 0, 1, 3).reshape(n, P, CW)


def _half_chunks(w):
    t = w.reshape(2, FH, P, KT, P)
    return t.transpose(3, 0, 2, 1, 4).reshape(2 * KT, P, FW)


def _columns(a):
    a = a.reshape(*a.shape[:-1], -1, P)
    return np.moveaxis(a, -1, 0)


def kernel(x, c, w_ada, b_ada, norm_g, w_in, conv_w, w_gk, b_gk, gla_norm_g, qn_g, kn_g, lam_q1, lam_k1,
           lam_q2, lam_k2, diff_norm_g, w_out, ffn1_norm_2, ffn1_w_in_2, ffn1_w_out_2, mix_norm_2, w_in_2,
           sgu_norm_2, sgu_w_2, sgu_b_2, conv_w_2, w_proj_a_2, w_proj_b_2, w_out_2, ffn2_norm_2,
           ffn2_w_in_2, ffn2_w_out_2, final_norm_2):
    import concourse.bacc as bacc
    from concourse.bass_utils import run_bass_kernel_spmd

    arrays = {
        "x_t": _tiles(x[0].T),
        "c_col": _columns(c[0]),
        "b_ada": _columns(b_ada),
        "norm_g": _columns(norm_g),
        "gains": _columns(np.stack([ffn1_norm_2[0], mix_norm_2[0], ffn2_norm_2[0], final_norm_2])),
        "conv_w": _columns(conv_w).transpose(0, 1, 3, 2),
        "conv2_w": _columns(conv_w_2[0]).transpose(0, 2, 1),
        "sgu_g": _columns(sgu_norm_2[0]),
        "qk_g": np.stack([np.concatenate([qn_g, qn_g], 1).T, np.concatenate([kn_g, kn_g], 1).T], 2),
        "lam": np.stack([lam_q1, lam_k1, lam_q2, lam_k2], 1).reshape(1, -1),
        "o_g": np.stack([gla_norm_g, diff_norm_g], 1).reshape(1, -1),
        "w_gk": w_gk.transpose(1, 0, 2),
        "b_gk": b_gk,
        "w_ada": w_ada.reshape(LAYERS, KT, P, 3 * D),
        "sgu_w_t": sgu_w_2[0].transpose(2, 0, 1),
        "sgu_b": sgu_b_2[0].reshape(1, -1),
    }
    at, cols = 0, {}
    for name, n in (("gq", 256), ("gk", 256), ("gv", 512), ("lr", RANK), ("gz", 512), ("dq", 512),
                    ("dk", 512), ("dv", 512), ("dz", 512)):
        cols[name] = slice(at, at + n)
        at += n
    arrays["w_lr"] = np.stack([_tiles(w_in[l][:, cols["lr"]]) for l in range(LAYERS)], 1)
    for l in range(LAYERS):
        w = w_in[l]
        arrays[f"layer{l}_stream"] = np.concatenate([
            _pair_chunks(w[:, 0:1024]), _pair_chunks(w[:, cols["dq"]]), _token_chunks(w[:, cols["dk"]]),
            _token_chunks(w[:, cols["dv"]]), _token_chunks(w[:, cols["gz"]]), _token_chunks(w[:, cols["dz"]]),
            _pair_chunks(w_out[l])])
    for name, win, wout in (("ffn1", ffn1_w_in_2[0], ffn1_w_out_2[0]), ("ffn2", ffn2_w_in_2[0], ffn2_w_out_2[0])):
        arrays[name + "_in_stream"] = _feature_chunks(win[:, :D_FF], win[:, D_FF:])
        arrays[name + "_out_stream"] = _half_chunks(wout)
    u, v, gate_b, gate_c, xb, g_a, g_b = np.split(w_in_2[0], 7, axis=1)
    gates, projections = _feature_chunks(g_a, g_b), _feature_chunks(w_proj_a_2[0], w_proj_b_2[0])
    arrays["mixer_stream"] = np.concatenate([
        _token_chunks(v), _pair_chunks(u), _feature_chunks(gate_c, xb), _pair_chunks(gate_b),
        np.stack([gates, projections], 1).reshape(2 * KT, P, CW), _pair_chunks(w_out_2[0])])

    nc = bacc.Bacc("TRN2", target_bir_lowering=False, num_devices=1, dynamic_dma_scratch_size=1024)
    arrays = {name: np.ascontiguousarray(a) for name, a in arrays.items()}
    ins = {name: nc.dram_tensor(name, a.shape, F32, kind="ExternalInput").ap() for name, a in arrays.items()}
    out = nc.dram_tensor("y_t", (P, KT, S), F32, kind="ExternalOutput").ap()
    build(nc, ins, out)
    r = run_bass_kernel_spmd(nc, [arrays], core_ids=[0])
    return r.results[0]["y_t"].transpose(2, 1, 0).reshape(1, S, D)
```
